# Optimizing a Trainium2 kernel written in Bass

```python
import math
import jax
import jax.numpy as jnp
from jax import lax
import numpy as np

'''One inference step of a hybrid decoder trunk (DEPTH layers) serving a prompt group and a sample group with shared weights.

Layer: h = RMSNorm(x); p = h @ w_in (one combined projection whose columns are partitioned into a gated-DeltaNet head group
(4 heads, q/k/v short causal conv, per-head decay, delta-rule state) and a differential-attention head group (4 heads, two
softmax maps per head, partial rotary on the first quarter of each q/k component)); the two group outputs are concatenated
and passed through one output projection w_out; residual add; then RMSNorm + hierarchical MoE (top-1 of 4 expert groups,
top-2 of 8 gated-MLP experts inside the group); residual add. A final RMSNorm follows the stack. 16 learned meta tokens are
prepended to every prompt sequence (positions 0..15) and dropped from y_prompt.

Inputs:
  x_prompt   (BATCH, SEQ, D_MODEL)
  x_sample   (DEC_BATCH, DEC_SEQ, D_MODEL)   positions PAST_LEN .. PAST_LEN+DEC_SEQ-1
  cache_k    (DEPTH, N_POOL, PAGE_SIZE, DA_HEADS, 2*DA_DQK)  paged rotated keys [k1 | k2] per head
  cache_v    (DEPTH, N_POOL, PAGE_SIZE, DA_HEADS, DA_DV)     paged values
  state_conv (DEPTH, DEC_BATCH, CONV_W-1, CONV_CH)           last pre-conv q/k/v rows of the DeltaNet group
  state_gdn  (DEPTH, DEC_BATCH, GDN_HEADS, GDN_DK, GDN_DV)   gated delta-rule state matrices
  page_table (DEC_BATCH, N_PAGES) int32, N_PAGES = PAST_LEN // PAGE_SIZE
Returns the tuple
  (y_prompt (BATCH, SEQ, D_MODEL),
   y_sample (DEC_BATCH, DEC_SEQ, D_MODEL),
   p_conv (DEPTH, BATCH, CONV_W-1, CONV_CH), p_gdn (DEPTH, BATCH, GDN_HEADS, GDN_DK, GDN_DV),
   p_k (DEPTH, BATCH, SEQ+N_META, DA_HEADS, 2*DA_DQK), p_v (DEPTH, BATCH, SEQ+N_META, DA_HEADS, DA_DV),
   s_conv (DEPTH, DEC_BATCH, CONV_W-1, CONV_CH), s_gdn (DEPTH, DEC_BATCH, GDN_HEADS, GDN_DK, GDN_DV),
   s_k (DEPTH, DEC_BATCH, DEC_SEQ, DA_HEADS, 2*DA_DQK), s_v (DEPTH, DEC_BATCH, DEC_SEQ, DA_HEADS, DA_DV))
'''

D_MODEL = 1024
BATCH = 1
SEQ = 1024
DEPTH = 1
DEC_BATCH = 8
DEC_SEQ = 1
PAST_LEN = 8192
PAGE_SIZE = 128

N_META = 16
EPS = 1e-6
GDN_HEADS = 4
GDN_DK = 128
GDN_DV = 128
GDN_CHUNK = 64
CONV_W = 4
GDN_QK_W = GDN_HEADS * GDN_DK
GDN_V_W = GDN_HEADS * GDN_DV
CONV_CH = 2 * GDN_QK_W + GDN_V_W
DA_HEADS = 4
DA_DQK = 64
DA_DV = 2 * DA_DQK
DA_QK_W = DA_HEADS * 2 * DA_DQK
DA_V_W = DA_HEADS * DA_DV
ROPE_DIM = DA_DQK // 4
ROPE_THETA = 500000.0
Q_BLOCK = 128
MIX_W = GDN_V_W + DA_V_W
PROJ_W = CONV_CH + GDN_V_W + 2 * GDN_HEADS + 2 * DA_QK_W + DA_V_W
N_GROUPS = 4
EXPERTS_PER_GROUP = 8
N_EXPERTS = N_GROUPS * EXPERTS_PER_GROUP
TOP_K = 2
D_EXPERT = 256

kernel_name = 'hymba_gdn_diffattn_hmoe_step'

def rmsnorm(x, w):
    xf = x.astype(jnp.float32)
    y = xf * lax.rsqrt(jnp.mean(xf * xf, axis=-1, keepdims=True) + EPS)
    return (y * w.astype(jnp.float32)).astype(x.dtype)

def l2norm(x):
    xf = x.astype(jnp.float32)
    return xf * lax.rsqrt(jnp.sum(xf * xf, axis=-1, keepdims=True) + EPS)

def partial_rope(x, pos):
    half = ROPE_DIM // 2
    inv_freq = ROPE_THETA ** (-jnp.arange(half, dtype=jnp.float32) * 2.0 / ROPE_DIM)
    ang = pos.astype(jnp.float32)[:, None] * inv_freq[None, :]
    cos = jnp.cos(ang)[None, :, None, None, :]
    sin = jnp.sin(ang)[None, :, None, None, :]
    xr = x[..., :ROPE_DIM].astype(jnp.float32)
    x1, x2 = xr[..., :half], xr[..., half:]
    rot = jnp.concatenate([x1 * cos - x2 * sin, x2 * cos + x1 * sin], axis=-1)
    return jnp.concatenate([rot.astype(x.dtype), x[..., ROPE_DIM:]], axis=-1)

def split_proj(p):
    sizes = [CONV_CH, GDN_V_W, GDN_HEADS, GDN_HEADS, DA_QK_W, DA_QK_W, DA_V_W]
    offs = np.cumsum(sizes)[:-1].tolist()
    return jnp.split(p, offs, axis=-1)

def gdn_chunked(q, k, v, g, beta, s0):
    bsz, t = q.shape[0], q.shape[1]
    n = t // GDN_CHUNK

    def to_chunks(a):
        return jnp.moveaxis(a.reshape((bsz, n, GDN_CHUNK) + a.shape[2:]), 1, 0)

    xs = tuple(to_chunks(a) for a in (q, k, v, g, beta))
    idx = jnp.arange(GDN_CHUNK)
    strict = idx[:, None] > idx[None, :]
    causal = idx[:, None] >= idx[None, :]
    eye = jnp.eye(GDN_CHUNK, dtype=jnp.float32)

    def step(S, inp):
        qi, ki, vi, gi, bi = inp
        G = jnp.cumsum(gi, axis=1)
        Gh = jnp.swapaxes(G, 1, 2)
        decay = jnp.exp(jnp.where(causal, Gh[..., :, None] - Gh[..., None, :], -jnp.inf))
        bh = jnp.swapaxes(bi, 1, 2)
        kk = jnp.einsum('bihd,bjhd->bhij', ki, ki)
        A = eye + jnp.where(strict, kk * decay * bh[..., :, None], 0.0)
        vb = jnp.swapaxes(vi * bi[..., None], 1, 2)
        kb = jnp.swapaxes(ki * (bi * jnp.exp(G))[..., None], 1, 2)
        sol = lax.linalg.triangular_solve(A, jnp.concatenate([vb, kb], axis=-1),
                                          left_side=True, lower=True, unit_diagonal=True)
        u = sol[..., :GDN_DV] - jnp.einsum('bhik,bhkv->bhiv', sol[..., GDN_DV:], S)
        qk = jnp.einsum('bihd,bjhd->bhij', qi, ki) * decay
        o = (jnp.einsum('bihd,bhdv->bhiv', qi * jnp.exp(G)[..., None], S)
             + jnp.einsum('bhij,bhjv->bhiv', qk, u))
        g_last = Gh[..., -1]
        kw = jnp.swapaxes(ki, 1, 2) * jnp.exp(g_last[..., None] - Gh)[..., None]
        S_new = S * jnp.exp(g_last)[..., None, None] + jnp.einsum('bhjd,bhjv->bhdv', kw, u)
        return S_new, jnp.swapaxes(o, 1, 2)

    S, o = lax.scan(step, s0, xs)
    o = jnp.moveaxis(o, 0, 1).reshape(bsz, t, GDN_HEADS, GDN_DV)
    return o, S

def gdn_branch(xc, z, a, b, conv_prev, s0, pad_front, pad_back, w_conv, a_log, dt_bias, w_gnorm):
    bsz, t = xc.shape[0], xc.shape[1]
    ext = jnp.concatenate([conv_prev.astype(xc.dtype), xc], axis=1)
    conv = jax.nn.silu(sum(ext[:, i:i + t] * w_conv[i] for i in range(CONV_W)))
    q, k, v = jnp.split(conv, [GDN_QK_W, 2 * GDN_QK_W], axis=-1)
    q = l2norm(q.reshape(bsz, t, GDN_HEADS, GDN_DK)) * (GDN_DK ** -0.5)
    k = l2norm(k.reshape(bsz, t, GDN_HEADS, GDN_DK))
    v = v.reshape(bsz, t, GDN_HEADS, GDN_DV).astype(jnp.float32)
    g = -jnp.exp(a_log.astype(jnp.float32)) * jax.nn.softplus(a.astype(jnp.float32) + dt_bias.astype(jnp.float32))
    beta = jax.nn.sigmoid(b.astype(jnp.float32))

    def pad(arr):
        return jnp.pad(arr, ((0, 0), (pad_front, pad_back)) + ((0, 0),) * (arr.ndim - 2))

    o, s_new = gdn_chunked(pad(q), pad(k), pad(v), pad(g), pad(beta), s0.astype(jnp.float32))
    o = o[:, pad_front:pad_front + t]
    o = rmsnorm(o, w_gnorm) * jax.nn.silu(z.reshape(bsz, t, GDN_HEADS, GDN_DV).astype(jnp.float32))
    return o.reshape(bsz, t, GDN_V_W).astype(xc.dtype), ext[:, -(CONV_W - 1):], s_new.astype(s0.dtype)

def diff_attn_prompt(q, k, v, lam):
    bsz, t = q.shape[0], q.shape[1]
    nb = -(-t // Q_BLOCK)
    tp = nb * Q_BLOCK
    qp = jnp.pad(q, ((0, 0), (0, tp - t), (0, 0), (0, 0), (0, 0)))
    qb = jnp.moveaxis(qp.reshape(bsz, nb, Q_BLOCK, DA_HEADS, 2, DA_DQK), 1, 0)
    kpos = jnp.arange(t)
    scale = DA_DQK ** -0.5

    def block(args):
        qi, start = args
        s = jnp.einsum('bqhcd,bkhcd->bhcqk', qi, k).astype(jnp.float32) * scale
        qpos = start + jnp.arange(Q_BLOCK)
        s = jnp.where(kpos[None, :] <= qpos[:, None], s, -jnp.inf)
        p = jax.nn.softmax(s, axis=-1)
        w = p[:, :, 0] - lam * p[:, :, 1]
        return jnp.einsum('bhqk,bkhv->bqhv', w.astype(v.dtype), v)

    o = lax.map(block, (qb, jnp.arange(nb) * Q_BLOCK))
    o = jnp.moveaxis(o, 0, 1).reshape(bsz, tp, DA_HEADS, DA_DV)
    return o[:, :t]

def diff_attn_sample(q, k_new, v_new, k_past, v_past, lam):
    s_len, p_len = q.shape[1], k_past.shape[1]
    scale = DA_DQK ** -0.5
    s_past = jnp.einsum('bqhcd,bkhcd->bhcqk', q, k_past).astype(jnp.float32) * scale
    s_new = jnp.einsum('bqhcd,bkhcd->bhcqk', q, k_new).astype(jnp.float32) * scale
    causal = jnp.arange(s_len)[None, :] <= jnp.arange(s_len)[:, None]
    s_new = jnp.where(causal, s_new, -jnp.inf)
    p = jax.nn.softmax(jnp.concatenate([s_past, s_new], axis=-1), axis=-1)
    w = (p[:, :, 0] - lam * p[:, :, 1]).astype(v_new.dtype)
    return (jnp.einsum('bhqk,bkhv->bqhv', w[..., :p_len], v_past)
            + jnp.einsum('bhqk,bkhv->bqhv', w[..., p_len:], v_new))

def hier_moe(x, w_group, w_expert, w_gate, w_up, w_down):
    shp = x.shape
    xf = x.reshape(-1, D_MODEL)
    n = xf.shape[0]
    g_logits = (xf @ w_group).astype(jnp.float32)
    g_prob = jax.nn.softmax(g_logits, axis=-1)
    g_sel = jnp.argmax(g_logits, axis=-1)
    g_w = jnp.max(g_prob, axis=-1)
    e_logits = (xf @ w_expert).astype(jnp.float32).reshape(n, N_GROUPS, EXPERTS_PER_GROUP)
    e_sel = e_logits[jnp.arange(n), g_sel]
    top_v, top_i = lax.top_k(e_sel, TOP_K)
    top_w = jax.nn.softmax(top_v, axis=-1) * g_w[:, None]
    eid = g_sel[:, None] * EXPERTS_PER_GROUP + top_i
    combine = jnp.sum(jax.nn.one_hot(eid, N_EXPERTS, dtype=jnp.float32) * top_w[..., None], axis=1)
    hg = jnp.einsum('nd,edf->nef', xf, w_gate)
    hu = jnp.einsum('nd,edf->nef', xf, w_up)
    hh = jax.nn.silu(hg) * hu * combine[:, :, None].astype(xf.dtype)
    return jnp.einsum('nef,efd->nd', hh, w_down).reshape(shp)

def setup_inputs(seed: int = 0) -> dict:
    key = jax.random.key(seed)
    ks = jax.random.split(key, 28)
    f32 = jnp.float32
    n_pages = PAST_LEN // PAGE_SIZE
    n_used = DEC_BATCH * n_pages
    n_pool = n_used + max(1, n_used // 4)

    def nrm(k, shape, scale):
        return jax.random.normal(k, shape, f32) * scale

    page_table = jax.random.permutation(ks[0], n_pool)[:n_used].reshape(DEC_BATCH, n_pages).astype(jnp.int32)
    dt = jnp.exp(jax.random.uniform(ks[1], (DEPTH, GDN_HEADS), f32, math.log(1e-3), math.log(1e-1)))
    return dict(
        x_prompt=nrm(ks[2], (BATCH, SEQ, D_MODEL), 1.0),
        x_sample=nrm(ks[3], (DEC_BATCH, DEC_SEQ, D_MODEL), 1.0),
        cache_k=nrm(ks[4], (DEPTH, n_pool, PAGE_SIZE, DA_HEADS, 2 * DA_DQK), 1.0),
        cache_v=nrm(ks[5], (DEPTH, n_pool, PAGE_SIZE, DA_HEADS, DA_DV), 1.0),
        state_conv=nrm(ks[6], (DEPTH, DEC_BATCH, CONV_W - 1, CONV_CH), 1.0),
        state_gdn=nrm(ks[7], (DEPTH, DEC_BATCH, GDN_HEADS, GDN_DK, GDN_DV), 0.1),
        page_table=page_table,
        meta_tokens=nrm(ks[8], (N_META, D_MODEL), 1.0),
        w_norm_mix=1.0 + nrm(ks[9], (DEPTH, D_MODEL), 0.02),
        w_in=nrm(ks[10], (DEPTH, D_MODEL, PROJ_W), D_MODEL ** -0.5),
        w_conv=nrm(ks[11], (DEPTH, CONV_W, CONV_CH), CONV_W ** -0.5),
        a_log=jnp.log(jax.random.uniform(ks[12], (DEPTH, GDN_HEADS), f32, 1.0, 16.0)),
        dt_bias=dt + jnp.log(-jnp.expm1(-dt)),
        w_gnorm=1.0 + nrm(ks[13], (DEPTH, GDN_DV), 0.02),
        lambda_q1=nrm(ks[14], (DEPTH, DA_DQK), 0.1),
        lambda_k1=nrm(ks[15], (DEPTH, DA_DQK), 0.1),
        lambda_q2=nrm(ks[16], (DEPTH, DA_DQK), 0.1),
        lambda_k2=nrm(ks[17], (DEPTH, DA_DQK), 0.1),
        w_subln=1.0 + nrm(ks[18], (DEPTH, DA_DV), 0.02),
        w_out=nrm(ks[19], (DEPTH, MIX_W, D_MODEL), MIX_W ** -0.5),
        w_norm_ffn=1.0 + nrm(ks[20], (DEPTH, D_MODEL), 0.02),
        w_group=nrm(ks[21], (DEPTH, D_MODEL, N_GROUPS), D_MODEL ** -0.5),
        w_expert=nrm(ks[22], (DEPTH, D_MODEL, N_EXPERTS), D_MODEL ** -0.5),
        w_gate=nrm(ks[23], (DEPTH, N_EXPERTS, D_MODEL, D_EXPERT), D_MODEL ** -0.5),
        w_up=nrm(ks[24], (DEPTH, N_EXPERTS, D_MODEL, D_EXPERT), D_MODEL ** -0.5),
        w_down=nrm(ks[25], (DEPTH, N_EXPERTS, D_EXPERT, D_MODEL), D_EXPERT ** -0.5),
        w_final=1.0 + nrm(ks[26], (D_MODEL,), 0.02),
    )

def reference(x_prompt, x_sample, cache_k, cache_v, state_conv, state_gdn, page_table, meta_tokens,
              w_norm_mix, w_in, w_conv, a_log, dt_bias, w_gnorm, lambda_q1, lambda_k1, lambda_q2, lambda_k2,
              w_subln, w_out, w_norm_ffn, w_group, w_expert, w_gate, w_up, w_down, w_final):
    bp, lp = x_prompt.shape[0], x_prompt.shape[1] + N_META
    bs, ls = x_sample.shape[0], x_sample.shape[1]
    past = page_table.shape[1] * cache_k.shape[2]
    meta = jnp.broadcast_to(meta_tokens[None].astype(x_prompt.dtype), (bp, N_META, D_MODEL))
    xp = jnp.concatenate([meta, x_prompt], axis=1)
    xs = x_sample
    pos_p = jnp.arange(lp)
    pos_s = past + jnp.arange(ls)
    pad_front = (-N_META) % GDN_CHUNK
    pad_back = (-ls) % GDN_CHUNK
    p_conv, p_gdn, p_k, p_v = [], [], [], []
    s_conv, s_gdn, s_k, s_v = [], [], [], []
    for l in range(DEPTH):
        lam_init = 0.8 - 0.6 * math.exp(-0.3 * l)
        lam = (jnp.exp(jnp.sum(lambda_q1[l].astype(jnp.float32) * lambda_k1[l].astype(jnp.float32)))
               - jnp.exp(jnp.sum(lambda_q2[l].astype(jnp.float32) * lambda_k2[l].astype(jnp.float32)))
               + lam_init)
        c, z, a, b, dq, dk, dv = split_proj(rmsnorm(xp, w_norm_mix[l]) @ w_in[l])
        g_out, conv_new, gdn_new = gdn_branch(
            c, z, a, b, jnp.zeros((bp, CONV_W - 1, CONV_CH), xp.dtype),
            jnp.zeros((bp, GDN_HEADS, GDN_DK, GDN_DV), state_gdn.dtype), pad_front, 0,
            w_conv[l], a_log[l], dt_bias[l], w_gnorm[l])
        q = partial_rope(dq.reshape(bp, lp, DA_HEADS, 2, DA_DQK), pos_p)
        k = partial_rope(dk.reshape(bp, lp, DA_HEADS, 2, DA_DQK), pos_p)
        v = dv.reshape(bp, lp, DA_HEADS, DA_DV)
        a_out = diff_attn_prompt(q, k, v, lam)
        a_out = (rmsnorm(a_out, w_subln[l]) * (1.0 - lam_init)).reshape(bp, lp, DA_V_W)
        xp = xp + jnp.concatenate([g_out, a_out], axis=-1) @ w_out[l]
        xp = xp + hier_moe(rmsnorm(xp, w_norm_ffn[l]), w_group[l], w_expert[l], w_gate[l], w_up[l], w_down[l])
        p_conv.append(conv_new)
        p_gdn.append(gdn_new)
        p_k.append(k.reshape(bp, lp, DA_HEADS, 2 * DA_DQK))
        p_v.append(v)
        c, z, a, b, dq, dk, dv = split_proj(rmsnorm(xs, w_norm_mix[l]) @ w_in[l])
        g_out, conv_new, gdn_new = gdn_branch(
            c, z, a, b, state_conv[l], state_gdn[l], 0, pad_back,
            w_conv[l], a_log[l], dt_bias[l], w_gnorm[l])
        q = partial_rope(dq.reshape(bs, ls, DA_HEADS, 2, DA_DQK), pos_s)
        k = partial_rope(dk.reshape(bs, ls, DA_HEADS, 2, DA_DQK), pos_s)
        v = dv.reshape(bs, ls, DA_HEADS, DA_DV)
        k_past = cache_k[l, page_table].reshape(bs, past, DA_HEADS, 2, DA_DQK)
        v_past = cache_v[l, page_table].reshape(bs, past, DA_HEADS, DA_DV)
        a_out = diff_attn_sample(q, k, v, k_past.astype(q.dtype), v_past.astype(v.dtype), lam)
        a_out = (rmsnorm(a_out, w_subln[l]) * (1.0 - lam_init)).reshape(bs, ls, DA_V_W)
        xs = xs + jnp.concatenate([g_out, a_out], axis=-1) @ w_out[l]
        xs = xs + hier_moe(rmsnorm(xs, w_norm_ffn[l]), w_group[l], w_expert[l], w_gate[l], w_up[l], w_down[l])
        s_conv.append(conv_new)
        s_gdn.append(gdn_new)
        s_k.append(k.reshape(bs, ls, DA_HEADS, 2 * DA_DQK))
        s_v.append(v)
    y_prompt = rmsnorm(xp, w_final)[:, N_META:]
    y_sample = rmsnorm(xs, w_final)
    return (y_prompt, y_sample, jnp.stack(p_conv), jnp.stack(p_gdn), jnp.stack(p_k), jnp.stack(p_v),
            jnp.stack(s_conv), jnp.stack(s_gdn), jnp.stack(s_k), jnp.stack(s_v))


_drawn_inputs = setup_inputs


def setup_inputs(seed=0):
    import zlib

    import numpy as np

    out = dict(_drawn_inputs(seed))
    spreads = {}
    factors = {'w_gnorm': 15.22,
     'lambda_q1': 12.111,
     'w_subln': 11.403,
     'w_final': 7.812,
     'w_norm_ffn': 5.091}
    for name, (base, spread) in spreads.items():
        noise = np.random.default_rng([zlib.crc32(name.encode()), seed]).standard_normal(out[name].shape)
        drawn = base * np.exp(spread * noise) if base else spread * noise
        out[name] = jnp.asarray(drawn.astype(out[name].dtype))
    for name, factor in factors.items():
        out[name] = (out[name] * factor).astype(out[name].dtype)
    return out
```

```python
import math
from contextlib import ExitStack, contextmanager

import numpy as np

import concourse.bass as bass
from concourse import mybir

F32 = mybir.dt.float32
I32 = mybir.dt.int32
U32 = mybir.dt.uint32
ALU = mybir.AluOpType
ACT = mybir.ActivationFunctionType
AX_X = mybir.AxisListType.X

P = 128
D = 1024
KD = D // P
SEQ, N_META = 1024, 16
LP = SEQ + N_META
BS = 8
ROWS = LP + BS
TILES = -(-ROWS // P)
RPAD = TILES * P
EPS = 1e-6
H = 4
DK = DV = 128
DQ = 64
CONV_W = 4
CONV_CH = 3 * H * DK
C_Z = CONV_CH
C_A = C_Z + H * DV
C_B = C_A + H
C_DQ = C_B + H
C_DK = C_DQ + H * 2 * DQ
C_DV = C_DK + H * 2 * DQ
PROJ_W = C_DV + H * DV
HALF = DQ // 4 // 2
ROPE_THETA = 500000.0
PAST, PAGE = 8192, 128
N_PAGES = PAST // PAGE
LAM_INIT = 0.8 - 0.6 * math.exp(-0.3 * 0)
G, EPG, NE, FE = 4, 8, 32, 256
SLOT_TILES = (2 * ROWS) // P + NE
SLOTS = SLOT_TILES * P
BIG = 1e30


@contextmanager
def own_semaphores(nc):
    held = []

    def own(name):
        held.append(nc.alloc_semaphore(name))
        return held[-1]

    yield own
    nc.clear_and_free_semaphores(held)
    nc.all_engine_barrier()


def tiles(eng, n=TILES):
    yield 0, 0, 0
    with eng.Fori(0, (n - 1) // 2) as u:
        yield 2 * u + 1, 1, u
        yield 2 * u + 2, 0, u + 1


class Chain:

    def __init__(self, eng, sem, per):
        self.eng, self.sem, self.per, self.base, self.n = eng, sem, per, 0, 0

    def begin(self, t):
        self.base, self.n = t * self.per, 0

    def done(self, ins):
        self.n += 1
        ins.then_inc(self.sem, 1)

    def sync(self):
        self.eng.wait_ge(self.sem, self.base + self.n)

    def link(self, ins):
        self.done(ins)
        self.sync()

    def end(self):
        assert self.n == self.per, f"{self.sem}: {self.n} steps, {self.per} declared"


RSQRT_STEPS = 12


def rsqrt(nc, ch, y, x, tmp, scale, bias, times=1.0):
    v = nc.vector
    ch.link(v.tensor_scalar(x, x, scale, bias, ALU.mult, ALU.add))
    ch.link(v.tensor_scalar(tmp.bitcast(I32), x.bitcast(I32), 1, None, ALU.logical_shift_right))
    ch.link(v.tensor_scalar(y.bitcast(I32), tmp.bitcast(I32), -1, 0x5F3759DF, ALU.mult, ALU.add))
    for step in range(3):
        last = times if step == 2 else 1.0
        ch.link(v.tensor_tensor(tmp, y, y, ALU.mult))
        ch.link(v.scalar_tensor_tensor(tmp, tmp, -0.5 * last, x, ALU.mult, ALU.mult))
        ch.link(v.scalar_tensor_tensor(y, tmp, 1.5 * last, y, ALU.add, ALU.mult))


def bc(ap, *shape):
    return ap.to_broadcast(list(shape))


def phase_project(nc, ps, A, keep):
    with ExitStack() as ctx, own_semaphores(nc) as own:
        def sb(n, s, d=F32):
            return ctx.enter_context(nc.sbuf_tensor("pj_" + n, s, d))

        def sem(n):
            return own("pj_" + n)

        def kept(n):
            return keep.enter_context(nc.semaphore("pj_" + n))

        w_in = sb("w_in", [P, KD, PROJ_W])
        w_norm = sb("w_norm", [P, D])
        ident = sb("ident", [P, P])
        x = sb("x", [P, 2, D])
        xn = sb("xn", [P, D])
        xT = sb("xT", [P, 2, D])
        proj = sb("proj", [P, 2, PROJ_W])
        sq = sb("sq", [P, 1])
        rs = sb("rs", [P, 2])
        squares = sb("squares", [P, D])
        zero = sb("zero", [4, (CONV_W - 1) * PROJ_W // 4])

        w_loaded = [sem(f"w_loaded{i}") for i in range(KD)]
        c_loaded = sem("c_loaded")
        x_loaded = [sem("x_loaded0"), sem("x_loaded1")]
        cleared, zeroed = sem("cleared"), kept("zeroed")
        sq_ready = sem("sq_ready")
        steps = sem("dve_steps")
        xn_ready = sem("xn_ready")
        xnT_ready = sem("xnT_ready")
        xT_ready = sem("xT_ready")
        mm_done = sem("mm_done")
        act_evac = sem("act_evac")
        dve_evac = sem("dve_evac")
        stored, proj_free = kept("stored"), sem("proj_free")
        NCH = 8
        cols = [(n * 512, min(512, PROJ_W - n * 512)) for n in range(NCH)]

        with nc.Block() as block:
            @block.sync
            def _(sp):
                def load(t, par):
                    sp.dma_start(x[:, par, :], A["x"][bass.ds(t * P, P), :]).then_inc(x_loaded[par], 16)

                load(0, 0)
                sp.dma_start(ident[:], A["ident"]).then_inc(c_loaded, 16)
                sp.dma_start(w_norm[:], A["w_norm_mix"].partition_broadcast(P)).then_inc(c_loaded, 16)
                for c in range(KD):
                    sp.dma_start(w_in[:, c, :], A["w_in"][c * P:(c + 1) * P, :]).then_inc(w_loaded[c], 16)
                for t, par, k in tiles(sp):
                    if not isinstance(t, int):
                        sp.wait_ge(xn_ready, t)
                    load(t + 1, 1 - par)

            @block.gpsimd
            def _(pool):
                pool.sem_inc(proj_free, 2)
                pool.memset(zero[:], 0.0).then_inc(cleared, 1)
                pool.wait_ge(cleared, 1)
                pool.dma_start(A["proj"][0:CONV_W - 1, :].rearrange("i n -> (i n)").rearrange("(p n) -> p n", p=4), zero[:]).then_inc(zeroed, 16)
                pool.wait_ge(zeroed, 16)
                for t, par, k in tiles(pool):
                    pool.wait_ge(act_evac, 4 * t + 4)
                    pool.wait_ge(dve_evac, 4 * t + 4)
                    if not isinstance(t, int):
                        pool.wait_ge(stored, 16 * t)
                        pool.sem_inc(proj_free, 1)
                    pool.dma_start(A["proj"][bass.ds(t * P + CONV_W - 1, P), :],
                                   proj[:, par, :]).then_inc(stored, 16)
                pool.wait_ge(stored, 16 * TILES)

            @block.scalar
            def _(act):
                def square(t, par, k):
                    act.wait_ge(x_loaded[par], 16 * (k + 1))
                    act.activation(squares[:], x[:, par, :], ACT.Square, accum_out=sq[:]).then_inc(sq_ready, 1)

                square(0, 0, 0)
                for t, par, k in tiles(act):
                    act.wait_ge(xnT_ready, t + 1)
                    act.activation(xT[:, par, :].rearrange("p (a b) -> p a b", a=2), ps[:, 0:2, :], ACT.Copy).then_inc(xT_ready, 1)
                    act.wait_ge(proj_free, t + 1)
                    for n in range(0, NCH, 2):
                        o, w = cols[n]
                        act.wait_ge(mm_done, 8 * t + n + 1)
                        act.activation(proj[:, par, o:o + w], ps[:, 2 + n % 4, 0:w], ACT.Copy).then_inc(act_evac, 1)
                        if n == 0:
                            act.wait_ge(xn_ready, t + 1)
                            square(t + 1, 1 - par, k + par)

            @block.vector
            def _(dve):
                ch = Chain(dve, steps, 12)

                def norm(t, par):
                    ch.begin(t)
                    dve.wait_ge(sq_ready, t + 1)
                    rsqrt(nc, ch, rs[:, 0:1], sq[:], rs[:, 1:2], 1.0 / D, EPS)
                    ch.end()
                    if not isinstance(t, int) or t > 0:
                        dve.wait_ge(xnT_ready, t)
                    nc.vector.scalar_tensor_tensor(xn[:], x[:, par, :], rs[:, 0:1], w_norm[:],
                                                   ALU.mult, ALU.mult).then_inc(xn_ready, 1)

                dve.wait_ge(c_loaded, 32)
                norm(0, 0)
                for t, par, k in tiles(dve):
                    dve.wait_ge(proj_free, t + 1)
                    for n in range(1, NCH, 2):
                        o, w = cols[n]
                        dve.wait_ge(mm_done, 8 * t + n + 1)
                        nc.vector.tensor_copy(proj[:, par, o:o + w], ps[:, 2 + n % 4, 0:w]).then_inc(dve_evac, 1)
                        if n == 1:
                            norm(t + 1, 1 - par)

            @block.tensor
            def _(pe):
                pe.wait_ge(c_loaded, 32)
                for t, par, k in tiles(pe):
                    pe.wait_ge(xn_ready, t + 1)
                    if not isinstance(t, int):
                        pe.wait_ge(xT_ready, t)
                    for c in range(KD):
                        last = pe.transpose(ps[:, c // 4, (c % 4) * P:(c % 4 + 1) * P], xn[:, c * P:(c + 1) * P], ident[:])
                    last.then_inc(xnT_ready, 1)
                    pe.wait_ge(xT_ready, t + 1)
                    for n in range(NCH):
                        o, w = cols[n]
                        if not (isinstance(t, int) and n < 4):
                            pe.wait_ge(dve_evac if n % 2 else act_evac, 4 * t + n // 2 - 1)
                        for c in range(KD):
                            if isinstance(t, int) and n == 0:
                                pe.wait_ge(w_loaded[c], 16)
                            last = pe.matmul(ps[:, 2 + n % 4, 0:w], xT[:, par, c * P:(c + 1) * P],
                                             w_in[:, c, o:o + w], start=(c == 0), stop=(c == KD - 1))
                        last.then_inc(mm_done, 1)


CHUNK = 4
CHUNKS = N_PAGES // CHUNK
RING = 4


def phase_recurrence_and_decode(nc, ps, A, keep):
    with ExitStack() as ctx, own_semaphores(nc) as own:
        def sb(n, s, d=F32):
            return ctx.enter_context(nc.sbuf_tensor("gd_" + n, s, d))

        def sem(n):
            return own("gd_" + n)

        def kept(n):
            return keep.enter_context(nc.semaphore("gd_" + n))

        HP = [P, H, P]
        HW = H * P
        ident, upper, ones = sb("ident", [P, P]), sb("upper", [P, P]), sb("ones", [P, P])
        levels = sb("levels", [P, 7, P])
        w_conv = sb("w_conv", [P, CONV_W, CONV_CH])
        w_gn = sb("w_gn", [P, DV])
        rowmask = sb("rowmask", [P, TILES])
        a_log, dt_bias = sb("a_log", [P, H]), sb("dt_bias", [P, H])
        ab = sb("ab", [P, TILES, 2 * H])
        ga, gb, gc = sb("ga", [P, TILES, H]), sb("gb", [P, TILES, H]), sb("gc", [P, TILES, H])
        gate, beta = sb("gate", [P, TILES, H]), sb("beta", [P, TILES, H])
        gu, bu = sb("gu", [P, TILES, H]), sb("bu", [P, TILES, H])
        cs = sb("cs", [P, CONV_W, CONV_CH])
        z = sb("z", [P, HW])
        th = sb("th", [P, CONV_CH])
        qkv = sb("qkv", [P, 3, HW])
        ss, rn, rt = sb("ss", [P, 8]), sb("rn", [P, 8]), sb("rt", [P, 8])
        gcol, glg, eg, beg, egl = (sb(n, [P, H]) for n in ("gcol", "glg", "eg", "beg", "egl"))
        egrow = sb("egrow", HP)
        dt = sb("dt", HP)
        kT, qT, qgT = sb("kT", HP), sb("qT", HP), sb("qgT", HP)
        vb, kbg, kw = sb("vb", HP), sb("kbg", HP), sb("kw", HP)
        ug, ib = kbg, kw
        LT, qkT = sb("LT", HP), sb("qkT", HP)
        TT = sb("TT", [P, 2, H, P])
        prod = sb("prod", HP)
        nwT, u, S = sb("nwT", HP), sb("u", HP), sb("S", HP)
        osq, on, zt, zs = prod, sb("on", HP), sb("zt", [P, HW]), sb("zs", [P, HW])

        C = 2 * H
        NP1 = N_PAGES + 1
        table = sb("table", [1, BS * N_PAGES], I32)
        keys, vals = sb("keys", [P, RING, CHUNK, HW]), sb("vals", [P, RING, CHUNK, HW])
        q, kn, vn = sb("q", [P, BS, HW]), sb("kn", [P, HW]), sb("vn", [P, HW])
        first, coef = sb("first", [P, 1]), sb("coef", [P, 2])
        s, e = sb("s", [P, NP1, C]), sb("e", [P, NP1, C])
        w = sb("w", [P, NP1, H])
        m, mx, l, lt, r = (sb(n, [P, C]) for n in ("m", "mx", "l", "lt", "r"))
        o = sb("o", [H, HW])
        od, dsq, w_sub = sb("od", [BS * H, DV]), sb("dsq", [BS * H, DV]), sb("w_sub", [BS * H, DV])
        s1, r1, r2 = sb("s1", [BS * H, 1]), sb("r1", [BS * H, 1]), sb("r2", [BS * H, 1])
        qk_s = vals[0:BS, 0, 0:2, :].rearrange("p a c -> p (a c)")
        rot = vals[0:BS, 1, 0, :].rearrange("p (a c j) -> p a c j", a=4, j=HALF)
        cos, sin = vals[0:BS, 1, 1, 0:HALF], vals[0:BS, 1, 1, HALF:2 * HALF]
        lams = vals[:, 2, 0, 0:4 * DQ].rearrange("p (i j) -> p i j", i=4)
        lprod = vals[:, 2, 1, 0:2 * DQ].rearrange("p (i j) -> p i j", i=2)
        lsum, lexp = vals[:, 2, 2, 0:2], vals[:, 2, 2, 2:4]
        pre_loaded, rot_ready, pre_stored, q_loaded, lam_ready = (sem(n) for n in ("pre_loaded", "rot_ready", "pre_stored", "q_loaded", "lam_ready"))
        new_loaded, vn_loaded = sem("new_loaded"), sem("vn_loaded")
        k_loaded, v_loaded = [sem(f"k_loaded{i}") for i in range(RING)], [sem(f"v_loaded{i}") for i in range(RING)]
        k_mult, k_mult_pool, k_used, v_used = sem("k_mult"), sem("k_mult_pool"), sem("k_used"), sem("v_used")
        dsteps, waited = sem("dsteps"), sem("waited")
        m_ready, mx_ready, s_ready, e_ready, l_ready, lt_ready = (sem(n) for n in ("m_ready", "mx_ready", "s_ready", "e_ready", "l_ready", "lt_ready"))
        w_ready, pv_done, od_ready, od_stored = sem("w_ready"), sem("pv_done"), sem("od_ready"), sem("od_stored")
        od_loaded, dn_ready, od_clear = sem("od_loaded"), sem("dn_ready"), sem("od_clear")

        c_loaded = sem("c_loaded")
        in_loaded = sem("in_loaded")
        cs_used, z_used = sem("cs_used"), sem("z_used")
        steps, psteps, asteps = sem("dve_steps"), sem("pool_steps"), sem("act_steps")
        gate_a, gate_b, gate_c = sem("gate_exp"), sem("gate_log"), sem("gates_ready")
        conv23 = sem("conv23_ready")
        conv_ready, th_ready = sem("conv_ready"), sem("tanh_ready")
        ug_ready, g_ps = sem("ug_ready"), sem("g_ps")
        qk_ready, qkT_ps, kqT_ready = sem("qk_ready"), sem("qkT_ps"), sem("kqT_ready")
        d_in, d_ready, eg_ready = sem("d_in"), sem("d_ready"), sem("eg_ready")
        operands = sem("operands_ready")
        kk_ps = sem("kk_ps")
        t_ready, p_ps, p_ready, dT_ps = sem("t_ready"), sem("p_ps"), sem("p_ready"), sem("dT_ps")
        w_ps, nw_ready, u_ps, u_ready = sem("w_ps"), sem("nw_ready"), sem("u_ps"), sem("u_ready")
        o_ps, osq_ready, zs_ready, zt_ready = sem("o_ps"), sem("osq_ready"), sem("zs_ready"), sem("zt_ready")
        on_free = sem("on_free")
        on_ready, on_stored, out_done = sem("on_ready"), kept("on_stored"), sem("out_done")

        def bank(b):
            return ps[:, b, :].rearrange("p (h j) -> p h j", h=H)

        def turns(eng):
            yield 0, True, False
            with eng.Fori(1, BS) as t:
                yield t, True, True
            yield BS, False, True

        with nc.Block() as block:
            @block.sync
            def _(sp):
                for dst, src in ((ident[:], A["ident"]), (upper[:], A["upper"]), (ones[:], A["ones"]),
                                 (levels[:], A["levels"]), (rowmask[:], A["rowmask"]),
                                 (w_conv[:].rearrange("p i c -> p (i c)"), A["w_conv"].rearrange("i c -> (i c)").partition_broadcast(P)),
                                 (w_gn[:], A["w_gnorm"].partition_broadcast(P)),
                                 (a_log[:], A["a_log"].partition_broadcast(P)),
                                 (dt_bias[:], A["dt_bias"].partition_broadcast(P)),
                                 (ab[:], A["proj"][CONV_W - 1:CONV_W - 1 + RPAD, C_A:C_A + 2 * H].rearrange("(t p) c -> p t c", p=P))):
                    sp.dma_start(dst, src).then_inc(c_loaded, 16)
                def load(t):
                    sp.wait_ge(cs_used, t + 1)
                    for i in range(CONV_W):
                        sp.dma_start(cs[:, i, :], A["proj"][bass.ds(t * P + i, P), 0:CONV_CH]).then_inc(in_loaded, 16)
                    sp.wait_ge(z_used, t + 1)
                    sp.dma_start(z[:], A["proj"][bass.ds(t * P + CONV_W - 1, P), C_Z:C_Z + HW]).then_inc(in_loaded, 16)

                load(0)
                row0 = CONV_W - 1 + LP
                for dst, src in [(qk_s, A["proj"][row0:row0 + BS, C_DQ:C_DQ + 2 * HW]), (cos, A["cos_s"]), (sin, A["sin_s"]),
                                 (table[:], A["page_table"]), (first[:], A["first"]), (w_sub[:], A["w_subln"].partition_broadcast(BS * H)),
                                 (A["s_v"], A["proj"][row0:row0 + BS, C_DV:C_DV + HW])] + \
                                [(lams[:, i, :], A[n].partition_broadcast(P)) for i, n in enumerate(("lambda_q1", "lambda_q2", "lambda_k1", "lambda_k2"))]:
                    sp.dma_start(dst, src).then_inc(pre_loaded, 16)
                sp.wait_ge(rot_ready, 1)
                sp.wait_ge(lam_ready, 3)
                for dst, src in [(A["q_s"], qk_s[:, 0:HW]), (A["s_k"], qk_s[:, HW:2 * HW]), (A["coef"], coef[:])]:
                    sp.dma_start(dst, src).then_inc(pre_stored, 16)
                sp.wait_ge(pre_stored, 48)
                sp.wait_ge(pre_loaded, 16 * 11)
                sp.dma_start(q[:].rearrange("p b c -> p (b c)"), A["q_s"].rearrange("b c -> (b c)").partition_broadcast(P)).then_inc(q_loaded, 16)

                def pages(cache, buf, done, used, b, cc):
                    for i in range(RING):
                        step = CHUNKS * b + RING * cc + i
                        sp.wait_ge(used, step + 1)
                        for j in range(CHUNK):
                            page = sp.value_load(table[0:1, bass.ds(CHUNK * step + j, 1)], min_val=0, max_val=A["cache_k"].shape[0] - 1)
                            sp.dma_start(buf[:, i, j, :], A[cache][bass.ds(page, 1), :, :].rearrange("g p c -> (g p) c")).then_inc(done[i], 16)

                def stream(t, with_k, with_v, c0, c1):
                    with sp.Fori(c0, c1) as cc:
                        if with_k:
                            pages("cache_k", keys, k_loaded, k_used, t, cc)
                        if with_v:
                            pages("cache_v", vals, v_loaded, v_used, t - 1, cc)

                for t, with_k, with_v in turns(sp):
                    half = CHUNKS // RING // 2
                    stream(t, with_k, with_v, 0, half)
                    if with_k:
                        load(t + 1)
                        if with_v:
                            sp.wait_ge(w_ready, t)
                        sp.dma_start(kn[:], A["s_k"][bass.ds(t, 1), :].rearrange("b c -> (b c)").partition_broadcast(P)).then_inc(new_loaded, 16)
                    if with_v:
                        sp.wait_ge(pv_done, t)
                        sp.dma_start(vn[:], A["s_v"][bass.ds(t - 1, 1), :].rearrange("b c -> (b c)").partition_broadcast(P)).then_inc(vn_loaded, 16)
                    stream(t, with_k, with_v, half, 2 * half)
                sp.wait_ge(od_stored, 16 * H * BS)
                sp.dma_start(od[:], A["o_s"]).then_inc(od_loaded, 16)
                sp.wait_ge(dn_ready, 1)
                for b in range(BS):
                    sp.dma_start(A["mix"][LP + b, HW:2 * HW].rearrange("(h j) -> h j", h=H), od[b * H:(b + 1) * H, :]).then_inc(out_done, 16)
                sp.wait_ge(on_stored, 16 * TILES)
                sp.dma_start(A["p_gdn"].rearrange("h k v -> k h v"), S[:]).then_inc(out_done, 16)
                last = TILES - 1
                r0 = LP - last * P
                sp.dma_start(A["gates_s"][0], gu[r0:r0 + BS, last, :]).then_inc(out_done, 16)
                sp.dma_start(A["gates_s"][1], bu[r0:r0 + BS, last, :]).then_inc(out_done, 16)
                sp.wait_ge(out_done, 48 + 16 * BS)

            @block.gpsimd
            def _(pool):
                ch = Chain(pool, psteps, 8)
                pool.sem_inc(cs_used, 1)
                pool.sem_inc(z_used, 1)
                pool.sem_inc(k_used, RING)
                pool.sem_inc(v_used, RING)

                def multiply(t, i):
                    pool.wait_ge(k_loaded[i % RING], 16 * CHUNK * (CHUNKS // RING * t + i // RING + 1))
                    pool.sem_inc(waited, 1)
                    pool.tensor_tensor(keys[:, i % RING], keys[:, i % RING], bc(q[:, bass.ds(t, 1), :], P, CHUNK, HW), ALU.mult).then_inc(k_mult_pool, 1)

                pool.sem_inc(on_free, 1)
                pool.wait_ge(c_loaded, 160)
                pool.wait_ge(gate_c, 1)
                pool.wait_ge(q_loaded, 16)
                for t, with_k, with_v in turns(pool):
                    ch.begin(t)
                    if with_v:
                        pool.wait_ge(on_stored, 16 * t)
                        pool.sem_inc(on_free, 1)
                    pool.wait_ge(in_loaded, 80 * (t + 1))
                    ch.done(pool.tensor_tensor(cs[:, 2, :], cs[:, 2, :], w_conv[:, 2, :], ALU.mult))
                    ch.link(pool.tensor_tensor(cs[:, 3, :], cs[:, 3, :], w_conv[:, 3, :], ALU.mult))
                    pool.tensor_tensor(cs[:, 2, :], cs[:, 2, :], cs[:, 3, :], ALU.add).then_inc(conv23, 1)
                    if with_k:
                        multiply(t, 1)
                    pool.wait_ge(eg_ready, t + 1)
                    pool.wait_ge(qk_ready, t + 1)
                    ch.done(pool.tensor_tensor(beg[:], beta[:, bass.ds(t, 1), :].rearrange("p t h -> p (t h)"), eg[:], ALU.mult))
                    ch.done(pool.tensor_tensor(vb[:], qkv[:, 2, :].rearrange("p (h j) -> p h j", h=H),
                                               bc(beta[:, bass.ds(t, 1), :].rearrange("p t (h o) -> p (t h) o", o=1), *HP), ALU.mult))
                    pool.wait_ge(d_ready, t + 1)
                    ch.link(pool.tensor_tensor(kw[:], qkv[:, 1, :].rearrange("p (h j) -> p h j", h=H),
                                               bc(egl[:].rearrange("p (h o) -> p h o", o=1), *HP), ALU.mult))
                    ch.link(pool.tensor_tensor(kbg[:], qkv[:, 1, :].rearrange("p (h j) -> p h j", h=H),
                                               bc(beg[:].rearrange("p (h o) -> p h o", o=1), *HP), ALU.mult))
                    pool.wait_ge(kqT_ready, t + 1)
                    pool.tensor_tensor(qgT[:], qT[:], egrow[:], ALU.mult).then_inc(operands, 1)
                    pool.wait_ge(zt_ready, t + 1)
                    ch.link(pool.tensor_tensor(zs[:], zt[:], z[:], ALU.mult))
                    ch.link(pool.tensor_tensor(zs[:], zs[:], z[:], ALU.add))
                    ch.end()
                    pool.sem_inc(z_used, 1)
                    if with_k:
                        for i in range(3, CHUNKS, 2):
                            multiply(t, i)
                        pool.wait_ge(m_ready, t + 1)
                        pool.sem_inc(waited, 1)
                        pool.partition_all_reduce(mx[:], m[:], P, bass.bass_isa.ReduceOp.max).then_inc(mx_ready, 1)
                        pool.wait_ge(l_ready, t + 1)
                        pool.sem_inc(waited, 1)
                        pool.partition_all_reduce(lt[:], l[:], P, bass.bass_isa.ReduceOp.add).then_inc(lt_ready, 1)
                    pool.wait_ge(on_ready, t + 1)
                    pool.dma_start(A["mix"][bass.ds(t * P, P), 0:HW], on[:].rearrange("p h j -> p (h j)")).then_inc(on_stored, 16)

            @block.scalar
            def _(act):
                act.wait_ge(c_loaded, 160)
                act.wait_ge(gate_a, 1)
                act.activation(ga[:], gc[:], ACT.Abs).then_inc(gate_a, 1)
                act.wait_ge(gate_a, 2)
                act.activation(gb[:], ga[:], ACT.Exp, scale=-1.0).then_inc(gate_a, 1)
                act.activation(a_log[:], a_log[:], ACT.Exp).then_inc(gate_a, 1)
                act.activation(bu[:], ab[:, :, H:2 * H], ACT.Exp, scale=-1.0).then_inc(gate_a, 1)
                act.wait_ge(gate_b, 1)
                act.activation(gb[:], gb[:], ACT.Ln).then_inc(gate_b, 1)
                act.sem_inc(od_clear, 1)
                act.wait_ge(lam_ready, 1)
                act.activation(lexp, lsum, ACT.Exp).then_inc(lam_ready, 1)
                for t, with_k, with_v in turns(act):
                    act.wait_ge(conv_ready, t + 1)
                    act.activation(th[:], cs[:, 0, :], ACT.Tanh).then_inc(th_ready, 1)
                    act.wait_ge(zs_ready, t + 1)
                    act.activation(zt[:], z[:], ACT.Tanh, scale=0.5).then_inc(zt_ready, 1)
                    act.wait_ge(g_ps, t + 1)
                    act.activation(eg[:], ps[:, 5, 0:H], ACT.Exp).then_inc(asteps, 1)
                    act.activation(gcol[:], ps[:, 5, 0:H], ACT.Copy).then_inc(asteps, 1)
                    act.activation(egrow[:], bank(1), ACT.Exp).then_inc(eg_ready, 1)
                    act.wait_ge(d_in, t + 1)
                    act.activation(egl[:], glg[:], ACT.Exp).then_inc(asteps, 1)
                    act.activation(dt[:], dt[:], ACT.Exp).then_inc(d_ready, 1)
                    act.wait_ge(qkT_ps, t + 1)
                    act.activation(kT[:], bank(3), ACT.Copy).then_inc(asteps, 1)
                    act.activation(qT[:], bank(4), ACT.Copy).then_inc(kqT_ready, 1)
                    act.wait_ge(w_ps, t + 1)
                    act.activation(nwT[:], bank(6), ACT.Copy, scale=-1.0).then_inc(nw_ready, 1)
                    act.wait_ge(u_ps, t + 1)
                    act.activation(u[:], bank(5), ACT.Copy).then_inc(u_ready, 1)
                    act.wait_ge(o_ps, t + 1)
                    act.activation(osq[:], bank(7), ACT.Square).then_inc(osq_ready, 1)
                    if with_k:
                        act.wait_ge(s_ready, t + 1)
                        act.activation(e[:], s[:], ACT.Exp, scale=DQ ** -0.5).then_inc(e_ready, 1)
                    if with_v:
                        act.wait_ge(pv_done, t + 1)
                        act.wait_ge(od_clear, t)
                        act.activation(o[:], ps[0:H, 0, :], ACT.Copy).then_inc(od_ready, 1)
                        act.wait_ge(od_ready, t + 1)
                        for h in range(H):
                            act.dma_start(A["o_s"][bass.ds((t - 1) * H + h, 1), :], o[h:h + 1, h * DV:(h + 1) * DV]).then_inc(od_stored, 16)
                        act.wait_ge(od_stored, 16 * H * t)
                        act.sem_inc(od_clear, 1)

            @block.vector
            def _(dve):
                v = nc.vector
                ch = Chain(dve, steps, DVE_GDN_STEPS)
                pre = Chain(dve, own("gd_gate_steps"), 0)
                dve.wait_ge(c_loaded, 160)
                v.tensor_tensor(gc[:], ab[:, :, 0:H], bc(dt_bias[:].rearrange("p (o h) -> p o h", o=1), P, TILES, H), ALU.add).then_inc(gate_a, 1)
                dve.wait_ge(gate_a, 5)
                pre.link(v.tensor_scalar(gc[:], gc[:], 0.0, None, ALU.max))
                v.tensor_scalar(gb[:], gb[:], 1.0, None, ALU.add).then_inc(gate_b, 1)
                pre.link(v.tensor_scalar(bu[:], bu[:], 1.0, None, ALU.add))
                pre.link(v.reciprocal(bu[:], bu[:]))
                pre.link(v.tensor_tensor(beta[:], bu[:], bc(rowmask[:].rearrange("p (t o) -> p t o", o=1), P, TILES, H), ALU.mult))
                dve.wait_ge(gate_b, 2)
                pre.link(v.tensor_tensor(gc[:], gc[:], gb[:], ALU.add))
                pre.link(v.scalar_tensor_tensor(gu[:], gc[:], -1.0, bc(a_log[:].rearrange("p (o h) -> p o h", o=1), P, TILES, H), ALU.mult, ALU.mult))
                pre.link(v.tensor_tensor(gate[:], gu[:], bc(rowmask[:].rearrange("p (t o) -> p t o", o=1), P, TILES, H), ALU.mult))
                pre.link(v.tensor_scalar(w_conv[:], w_conv[:], 0.5, None, ALU.mult))
                pre.link(v.tensor_scalar(w_gn[:], w_gn[:], 0.5, None, ALU.mult))
                v.memset(S[:], 0.0).then_inc(gate_c, 1)
                dve.wait_ge(pre_loaded, 16 * 11)
                pre.link(v.tensor_tensor(lprod, lams[:, 0:2, :], lams[:, 2:4, :], ALU.mult))
                v.tensor_reduce(lsum, lprod, AX_X, ALU.add).then_inc(lam_ready, 1)
                x = qk_s.rearrange("p (c j) -> p c j", j=DQ)
                x1, x2 = x[:, :, 0:HALF], x[:, :, HALF:2 * HALF]
                cb, sb_ = (bc(a.rearrange("p (o j) -> p o j", o=1), BS, 16, HALF) for a in (cos, sin))
                pre.done(v.tensor_tensor(rot[:, 0], x1, cb, ALU.mult))
                pre.done(v.tensor_tensor(rot[:, 1], x2, sb_, ALU.mult))
                pre.done(v.tensor_tensor(rot[:, 2], x2, cb, ALU.mult))
                pre.link(v.tensor_tensor(rot[:, 3], x1, sb_, ALU.mult))
                pre.done(v.tensor_tensor(x1, rot[:, 0], rot[:, 1], ALU.subtract))
                v.tensor_tensor(x2, rot[:, 2], rot[:, 3], ALU.add).then_inc(rot_ready, 1)
                dve.wait_ge(lam_ready, 2)
                pre.done(v.memset(coef[:, 0:1], 1.0))
                pre.link(v.tensor_tensor(coef[:, 1:2], lexp[:, 1:2], lexp[:, 0:1], ALU.subtract))
                v.tensor_scalar(coef[:, 1:2], coef[:, 1:2], -LAM_INIT, None, ALU.add).then_inc(lam_ready, 1)
                dve.wait_ge(lam_ready, 3)
                dve.wait_ge(gate_c, 1)
                dve.wait_ge(q_loaded, 16)
                dve.sem_inc(zs_ready, 1)

                def keys_times_query(t, i):
                    dve.wait_ge(k_loaded[i % RING], 16 * CHUNK * (CHUNKS // RING * t + i // RING + 1))
                    v.tensor_tensor(keys[:, i % RING], keys[:, i % RING], bc(q[:, bass.ds(t, 1), :], P, CHUNK, HW), ALU.mult).then_inc(k_mult, 1)

                def score(t, i):
                    dve.wait_ge(k_mult_pool if i % 2 else k_mult, CHUNKS // 2 * t + i // 2 + 1)
                    v.tensor_reduce(s[:, CHUNK * i:CHUNK * (i + 1), :], keys[:, i % RING].rearrange("p a (c j) -> p a c j", j=DQ), AX_X, ALU.add).then_inc(k_used, 1)

                for t, with_k, with_v in turns(dve):
                    base = D_STEPS * t
                    ch.begin(t)
                    dve.wait_ge(in_loaded, 80 * (t + 1))
                    ch.done(v.tensor_tensor(cs[:, 0, :], cs[:, 0, :], w_conv[:, 0, :], ALU.mult))
                    ch.link(v.tensor_tensor(cs[:, 1, :], cs[:, 1, :], w_conv[:, 1, :], ALU.mult))
                    ch.link(v.tensor_tensor(cs[:, 0, :], cs[:, 0, :], cs[:, 1, :], ALU.add))
                    dve.wait_ge(conv23, t + 1)
                    v.tensor_tensor(cs[:, 0, :], cs[:, 0, :], cs[:, 2, :], ALU.add).then_inc(conv_ready, 1)
                    if with_k:
                        keys_times_query(t, 0)
                    gt = gate[:, bass.ds(t, 1), :].rearrange("p t (h o) -> p (t h) o", o=1)
                    bt = beta[:, bass.ds(t, 1), :].rearrange("p t (h o) -> p (t h) o", o=1)
                    ch.done(v.tensor_tensor(ug[:], bc(upper[:].rearrange("p (o j) -> p o j", o=1), *HP), bc(gt, *HP), ALU.mult))
                    v.tensor_tensor(ib[:], bc(ident[:].rearrange("p (o j) -> p o j", o=1), *HP), bc(bt, *HP), ALU.mult).then_inc(ug_ready, 1)
                    dve.wait_ge(th_ready, t + 1)
                    qk = qkv[:, 0:2, :].rearrange("p a (h j) -> p (a h) j", h=H)
                    sq = th[:, 0:2 * HW].rearrange("p (h j) -> p h j", j=P)
                    ch.link(v.scalar_tensor_tensor(qkv[:].rearrange("p a j -> p (a j)"), th[:], 1.0, cs[:, 0, :], ALU.add, ALU.mult))
                    dve.sem_inc(cs_used, 1)
                    ch.link(v.tensor_tensor(sq, qk, qk, ALU.mult))
                    ch.link(v.tensor_reduce(ss[:], sq, AX_X, ALU.add))
                    rsqrt(nc, ch, rn[:], ss[:], rt[:], 1.0, EPS)
                    ch.link(v.tensor_scalar(rn[:, 0:H], rn[:, 0:H], DK ** -0.5, None, ALU.mult))
                    v.tensor_tensor(qk, qk, bc(rn[:].rearrange("p (h o) -> p h o", o=1), P, 2 * H, P), ALU.mult).then_inc(qk_ready, 1)
                    dve.wait_ge(eg_ready, t + 1)
                    gcb = bc(gcol[:].rearrange("p (h o) -> p h o", o=1), *HP)
                    ch.done(v.tensor_tensor(glg[:].rearrange("p (h o) -> p h o", o=1), bank(1)[:, :, P - 1:P], gcol[:].rearrange("p (h o) -> p h o", o=1), ALU.subtract))
                    ch.link(v.tensor_tensor(dt[:], bank(1), gcb, ALU.subtract))
                    v.tensor_scalar(dt[:], dt[:], 0.0, None, ALU.min).then_inc(d_in, 1)
                    if with_k:
                        score(t, 0)
                        score(t, 1)
                    dve.wait_ge(d_ready, t + 1)
                    ch.link(v.tensor_tensor(dt[:], dt[:], bc(upper[:].rearrange("p (o j) -> p o j", o=1), *HP), ALU.mult))
                    idb = ident[:].rearrange("p (o j) -> p o j", o=1)
                    ch.done(v.tensor_copy(TT[:].rearrange("p a h j -> p (a h) j"), bc(idb, P, 2 * H, P)))
                    if with_k:
                        keys_times_query(t, 2)
                        score(t, 2)
                    dve.wait_ge(kk_ps, t + 1)
                    ch.done(v.tensor_tensor(qkT[:], bank(6), dt[:], ALU.mult))
                    ch.link(v.tensor_tensor(LT[:], bank(5), dt[:], ALU.mult))
                    v.tensor_tensor(LT[:], LT[:], bank(2), ALU.mult).then_inc(t_ready, 1)
                    for lev in range(7):
                        dve.wait_ge(p_ps, 7 * t + lev + 1)
                        v.tensor_tensor(prod[:], bank(7), bc(levels[:, lev:lev + 1, :], *HP), ALU.mult).then_inc(p_ready, 1)
                        if with_k:
                            score(t, lev + 3)
                        dve.wait_ge(dT_ps, 7 * t + lev + 1)
                        v.tensor_tensor(TT[:].rearrange("p a h j -> p a (h j)"), TT[:].rearrange("p a h j -> p a (h j)"), ps[:, 3:5, :], ALU.subtract).then_inc(t_ready, 1)
                        if with_k and lev % 2 == 0:
                            keys_times_query(t, lev + 4)
                    if with_k:
                        for i in range(10, CHUNKS):
                            if i % 2 == 0 and i > 10:
                                keys_times_query(t, i)
                            score(t, i)
                        dve.wait_ge(new_loaded, 16 * (t + 1))
                        v.tensor_tensor(kn[:], kn[:], q[:, bass.ds(t, 1), :].rearrange("p b c -> p (b c)"), ALU.mult).then_inc(dsteps, 1)
                        dve.wait_ge(dsteps, base + 1)
                        v.tensor_reduce(s[:, N_PAGES, :], kn[:].rearrange("p (c j) -> p c j", j=DQ), AX_X, ALU.add).then_inc(dsteps, 1)
                        dve.wait_ge(dsteps, base + 2)
                        v.tensor_scalar(s[:, N_PAGES, :], s[:, N_PAGES, :], first[:], None, ALU.add).then_inc(dsteps, 1)
                        dve.wait_ge(dsteps, base + 3)
                        dve.wait_ge(k_used, CHUNKS * (t + 1) + RING)
                        v.tensor_reduce(m[:], s[:].rearrange("p g c -> p c g"), AX_X, ALU.max).then_inc(m_ready, 1)
                    dve.wait_ge(o_ps, t + 1)
                    for h in range(H):
                        ch.done(v.scalar_tensor_tensor(S[:, h, :], S[:, h, :], egrow[:, h, P - 1:P], bank(3)[:, h, :], ALU.mult, ALU.add))
                    dve.wait_ge(osq_ready, t + 1)
                    ch.link(v.tensor_reduce(ss[:, 0:H], osq[:], AX_X, ALU.add))
                    rsqrt(nc, ch, rn[:, 0:H], ss[:, 0:H], rt[:, 0:H], 1.0 / DV, EPS)
                    if with_k:
                        dve.wait_ge(mx_ready, t + 1)
                        v.tensor_tensor(s[:], s[:], bc(mx[:].rearrange("p (o c) -> p o c", o=1), P, NP1, C), ALU.subtract).then_inc(s_ready, 1)
                    dve.wait_ge(on_free, t + 1)
                    ch.link(v.tensor_tensor(on[:], bank(7), bc(rn[:, 0:H].rearrange("p (h o) -> p h o", o=1), *HP), ALU.mult))
                    ch.link(v.tensor_tensor(on[:], on[:], bc(w_gn[:].rearrange("p (o j) -> p o j", o=1), *HP), ALU.mult))
                    dve.wait_ge(psteps, 8 * t + 8)
                    v.tensor_tensor(on[:].rearrange("p h j -> p (h j)"), on[:].rearrange("p h j -> p (h j)"), zs[:], ALU.mult).then_inc(on_ready, 1)
                    ch.end()
                    dve.sem_inc(zs_ready, 1)
                    if not with_k:
                        continue
                    dve.wait_ge(e_ready, t + 1)
                    v.tensor_reduce(l[:], e[:].rearrange("p g c -> p c g"), AX_X, ALU.add).then_inc(l_ready, 1)
                    dve.wait_ge(lt_ready, t + 1)
                    v.reciprocal(r[:], lt[:]).then_inc(dsteps, 1)
                    dve.wait_ge(dsteps, base + 4)
                    v.tensor_tensor(r[:].rearrange("p (h c) -> p h c", c=2), r[:].rearrange("p (h c) -> p h c", c=2), bc(coef[:].rearrange("p (o c) -> p o c", o=1), P, H, 2), ALU.mult).then_inc(dsteps, 1)
                    dve.wait_ge(dsteps, base + 5)
                    v.tensor_tensor(e[:], e[:], bc(r[:].rearrange("p (o c) -> p o c", o=1), P, NP1, C), ALU.mult).then_inc(dsteps, 1)
                    dve.wait_ge(dsteps, base + 6)
                    dve.wait_ge(pv_done, t + 1)
                    e2 = e[:].rearrange("p g (h c) -> p g h c", c=2)
                    v.tensor_tensor(w[:], e2[:, :, :, 0], e2[:, :, :, 1], ALU.add).then_inc(w_ready, 1)
                fin = Chain(dve, own("de_final"), 0)
                dve.wait_ge(od_loaded, 16)
                fin.link(v.tensor_tensor(dsq[:], od[:], od[:], ALU.mult))
                fin.link(v.tensor_reduce(s1[:], dsq[:], AX_X, ALU.add))
                rsqrt(nc, fin, r1[:], s1[:], r2[:], 1.0 / DV, EPS, times=1.0 - LAM_INIT)
                v.scalar_tensor_tensor(od[:], od[:], r1[:], w_sub[:], ALU.mult, ALU.mult).then_inc(dn_ready, 1)

            @block.tensor
            def _(pe):
                pe.wait_ge(c_loaded, 160)
                pe.sem_inc(pv_done, 1)
                pe.sem_inc(od_ready, 1)
                pe.wait_ge(pre_stored, 48)

                def weigh(t, c0, c1):
                    if c0 == 0:
                        pe.wait_ge(w_ready, t)
                        pe.wait_ge(od_ready, t)
                    for c in range(c0, c1):
                        pe.wait_ge(v_loaded[c % RING], 16 * CHUNK * (CHUNKS // RING * (t - 1) + c // RING + 1))
                        for j in range(CHUNK):
                            last = pe.matmul(ps[0:H, 0, :], w[:, c * CHUNK + j, :], vals[:, c % RING, j, :], start=(c == 0 and j == 0), stop=False)
                        last.then_inc(v_used, 1)
                    if c1 == CHUNKS:
                        pe.wait_ge(vn_loaded, 16 * t)
                        pe.matmul(ps[0:H, 0, :], w[:, N_PAGES, :], vn[:], start=False, stop=True).then_inc(pv_done, 1)

                for t, with_k, with_v in turns(pe):
                    pe.wait_ge(ug_ready, t + 1)
                    pe.wait_ge(gate_c, 1)
                    pe.matmul(ps[:, 5, 0:H], upper[:], gate[:, bass.ds(t, 1), :].rearrange("p t h -> p (t h)"), start=True, stop=True)
                    pe.matmul(ps[:, 1, :], ones[:], ug[:].rearrange("p h j -> p (h j)"), start=True, stop=True)
                    pe.matmul(ps[:, 2, :], ones[:], ib[:].rearrange("p h j -> p (h j)"), start=True, stop=True).then_inc(g_ps, 1)
                    if with_v:
                        weigh(t, 0, 2)
                    pe.wait_ge(qk_ready, t + 1)
                    for h in range(H):
                        pe.transpose(bank(3)[:, h, :], qkv[:, 1, h * P:(h + 1) * P], ident[:])
                    for h in range(H):
                        last = pe.transpose(bank(4)[:, h, :], qkv[:, 0, h * P:(h + 1) * P], ident[:])
                    last.then_inc(qkT_ps, 1)
                    if with_v:
                        weigh(t, 2, 3)
                    pe.wait_ge(kqT_ready, t + 1)
                    for h in range(H):
                        pe.matmul(bank(5)[:, h, :], kT[:, h, :], kT[:, h, :], start=True, stop=True)
                    for h in range(H):
                        last = pe.matmul(bank(6)[:, h, :], kT[:, h, :], qT[:, h, :], start=True, stop=True)
                    last.then_inc(kk_ps, 1)
                    if with_v:
                        weigh(t, 3, 4)
                    for lev in range(7):
                        pe.wait_ge(t_ready, 8 * t + lev + 1)
                        for h in range(H):
                            last = pe.matmul(bank(7)[:, h, :], LT[:, h, :], TT[:, 0, h, :], start=True, stop=True)
                        last.then_inc(p_ps, 1)
                        pe.wait_ge(p_ready, 7 * t + lev + 1)
                        for h in range(H):
                            pe.matmul(bank(3)[:, h, :], TT[:, 1, h, :], prod[:, h, :], start=True, stop=True)
                            last = pe.matmul(bank(4)[:, h, :], prod[:, h, :], TT[:, 1, h, :], start=True, stop=True)
                        last.then_inc(dT_ps, 1)
                        if with_v:
                            weigh(t, 4 + lev, 5 + lev)
                    pe.wait_ge(t_ready, 8 * t + 8)
                    pe.wait_ge(operands, t + 1)
                    for h in range(H):
                        last = pe.matmul(bank(6)[:, h, :], kbg[:, h, :], TT[:, 1, h, :], start=True, stop=True)
                    last.then_inc(w_ps, 1)
                    if with_v:
                        weigh(t, 11, 12)
                    pe.wait_ge(nw_ready, t + 1)
                    for h in range(H):
                        pe.matmul(bank(5)[:, h, :], TT[:, 1, h, :], vb[:, h, :], start=True, stop=False)
                        last = pe.matmul(bank(5)[:, h, :], nwT[:, h, :], S[:, h, :], start=False, stop=True)
                    last.then_inc(u_ps, 1)
                    for h in range(H):
                        pe.matmul(bank(7)[:, h, :], qgT[:, h, :], S[:, h, :], start=True, stop=False)
                        if h == 0:
                            pe.wait_ge(u_ready, t + 1)
                        pe.matmul(bank(7)[:, h, :], qkT[:, h, :], u[:, h, :], start=False, stop=True)
                    for h in range(H):
                        last = pe.matmul(bank(3)[:, h, :], kw[:, h, :], u[:, h, :], start=True, stop=True)
                    last.then_inc(o_ps, 1)
                    if with_v:
                        weigh(t, 12, CHUNKS)


DVE_GDN_STEPS = 45
D_STEPS = 6


def phase_sample_gdn(nc, ps, A, keep):
    N = BS * H
    with ExitStack() as ctx, own_semaphores(nc) as own:
        def sb(n, s, d=F32):
            return ctx.enter_context(nc.sbuf_tensor("sg_" + n, s, d))

        def sem(n):
            return own("sg_" + n)

        ident, ones = sb("ident", [P, P]), sb("ones", [P, P])
        state = sb("state", [P, N, DV])
        taps, w_conv = sb("taps", [BS, CONV_W, CONV_CH]), sb("w_conv", [BS, CONV_W, CONV_CH])
        th, qkv, sq = sb("th", [BS, CONV_CH]), sb("qkv", [BS, 3, H * DK]), sb("sq", [BS, 8, DK])
        ss, rn, rt = sb("ss", [BS, 8]), sb("rn", [BS, 8]), sb("rt", [BS, 8])
        z, zt, w_gn = sb("z", [N, DV]), sb("zt", [N, DV]), sb("w_gn", [N, DV])
        gate, beta, eg = sb("gate", [N, 1]), sb("beta", [N, 1]), sb("eg", [N, 1])
        rows = sb("rows", [N, 3, DK])
        kT, qT = sb("kT", [P, N]), sb("qT", [P, N])
        diag, eb = sb("diag", [N, N]), sb("eb", [P, N])
        colT, u, spread = sb("colT", [P, N]), sb("u", [N, DV]), sb("spread", [N, N, DV])
        o, osq = sb("o", [N, DV]), sb("osq", [N, DV])
        s1, r1, r2 = sb("s1", [N, 1]), sb("r1", [N, 1]), sb("r2", [N, 1])
        loaded, rows_out, rows_in = sem("loaded"), sem("rows_out"), sem("rows_in")
        steps, conv_ready, th_ready, qkv_ready = sem("steps"), sem("conv_ready"), sem("th_ready"), sem("qkv_ready")
        eg_ready, zt_ready, diag_ready = sem("eg_ready"), sem("zt_ready"), sem("diag_ready")
        turned, turned_sb, ks_ps, ks_sb, ks_row = sem("turned"), sem("turned_sb"), sem("ks_ps"), sem("ks_sb"), sem("ks_row")
        u_ready, outer, state_ready = sem("u_ready"), sem("outer"), sem("state_ready")
        qs_ps, qs_sb, qs_row, o_ready, stored = sem("qs_ps"), sem("qs_sb"), sem("qs_row"), sem("o_ready"), sem("stored")
        row0 = CONV_W - 1 + LP

        with nc.Block() as block:
            @block.sync
            def _(sp):
                n = 0
                for dst, src in [(taps[:, 0:CONV_W - 1, :], A["state_conv"]),
                                 (taps[:, CONV_W - 1, :], A["proj"][row0:row0 + BS, 0:CONV_CH]),
                                 (w_conv[:].rearrange("p i c -> p (i c)"), A["w_conv"].rearrange("i c -> (i c)").partition_broadcast(BS)),
                                 (gate[:], A["gates_s"][0].rearrange("b (h o) -> (b h) o", o=1)),
                                 (beta[:], A["gates_s"][1].rearrange("b (h o) -> (b h) o", o=1)),
                                 (w_gn[:], A["w_gnorm"].partition_broadcast(N)),
                                 (ident[:], A["ident"]), (ones[:], A["ones"])]:
                    sp.dma_start(dst, src).then_inc(loaded, 16)
                for b in range(BS):
                    sp.dma_start(z[b * H:(b + 1) * H, :], A["proj"][row0 + b, C_Z:C_Z + H * DV].rearrange("(h j) -> h j", h=H)).then_inc(loaded, 16)
                sp.dma_start(state[:], A["state_gdn"].rearrange("i k v -> k i v")).then_inc(loaded, 16)
                sp.dma_start(A["s_conv"][:, 0:CONV_W - 2, :], A["state_conv"][:, 1:CONV_W - 1, :]).then_inc(stored, 16)
                sp.dma_start(A["s_conv"][:, CONV_W - 2, :], A["proj"][row0:row0 + BS, 0:CONV_CH]).then_inc(stored, 16)
                sp.dma_start(A["p_conv"], A["proj"][row0 - (CONV_W - 1):row0, 0:CONV_CH]).then_inc(stored, 16)
                sp.wait_ge(qkv_ready, 2)
                sp.dma_start(A["rows_s"].rearrange("a b c -> b a c"), qkv[:]).then_inc(rows_out, 16)
                sp.wait_ge(rows_out, 16)
                sp.dma_start(rows[:], A["rows_s"].rearrange("a b (h j) -> (b h) a j", h=H)).then_inc(rows_in, 16)
                sp.wait_ge(state_ready, 1)
                sp.dma_start(A["s_gdn"].rearrange("i k v -> k i v"), state[:]).then_inc(stored, 16)
                sp.wait_ge(o_ready, 1)
                for b in range(BS):
                    sp.dma_start(A["mix"][LP + b, 0:H * DV].rearrange("(h j) -> h j", h=H), o[b * H:(b + 1) * H, :]).then_inc(stored, 16)
                sp.wait_ge(stored, 16 * (4 + BS))

            @block.scalar
            def _(act):
                act.wait_ge(loaded, 16 * (9 + BS))
                act.activation(eg[:], gate[:], ACT.Exp).then_inc(eg_ready, 1)
                act.activation(zt[:], z[:], ACT.Tanh, scale=0.5).then_inc(zt_ready, 1)
                act.wait_ge(conv_ready, 1)
                act.activation(th[:], taps[:, 0, :], ACT.Tanh).then_inc(th_ready, 1)
                act.wait_ge(turned, 1)
                act.activation(kT[:], ps[:, 0, 0:N], ACT.Copy).then_inc(turned_sb, 1)
                act.activation(qT[:], ps[:, 1, 0:N], ACT.Copy).then_inc(turned_sb, 1)
                act.wait_ge(diag_ready, 2)
                act.activation(eb[:], ps[:, 2, 0:N], ACT.Copy).then_inc(turned_sb, 1)
                act.wait_ge(ks_ps, 1)
                act.activation(colT[:], ps[:, 3, 0:N], ACT.Copy).then_inc(ks_sb, 1)
                act.wait_ge(qs_ps, 1)
                act.activation(colT[:], ps[:, 0, 0:N], ACT.Copy).then_inc(qs_sb, 1)

            @block.vector
            def _(dve):
                v = nc.vector
                ch = Chain(dve, steps, 0)
                dve.wait_ge(loaded, 16 * (9 + BS))
                ch.link(v.tensor_scalar(w_conv[:], w_conv[:], 0.5, None, ALU.mult))
                ch.link(v.tensor_tensor(taps[:], taps[:], w_conv[:], ALU.mult))
                ch.link(v.tensor_tensor(taps[:, 0:2, :], taps[:, 0:2, :], taps[:, 2:4, :], ALU.add))
                v.tensor_tensor(taps[:, 0, :], taps[:, 0, :], taps[:, 1, :], ALU.add).then_inc(conv_ready, 1)
                dve.wait_ge(th_ready, 1)
                v.scalar_tensor_tensor(qkv[:].rearrange("p a j -> p (a j)"), th[:], 1.0, taps[:, 0, :], ALU.add, ALU.mult).then_inc(qkv_ready, 1)
                dve.wait_ge(qkv_ready, 1)
                qk = qkv[:, 0:2, :].rearrange("p a (h j) -> p (a h) j", h=H)
                ch.link(v.tensor_tensor(sq[:], qk, qk, ALU.mult))
                ch.link(v.tensor_reduce(ss[:], sq[:], AX_X, ALU.add))
                rsqrt(nc, ch, rn[:], ss[:], rt[:], 1.0, EPS)
                ch.link(v.tensor_scalar(rn[:, 0:H], rn[:, 0:H], DK ** -0.5, None, ALU.mult))
                v.tensor_tensor(qk, qk, bc(rn[:].rearrange("p (h o) -> p h o", o=1), BS, 2 * H, DK), ALU.mult).then_inc(qkv_ready, 1)
                dve.wait_ge(eg_ready, 1)
                v.tensor_scalar(diag[:], ident[0:N, 0:N], eg[:], None, ALU.mult).then_inc(diag_ready, 1)
                dve.wait_ge(ks_row, 1)
                ch.link(v.tensor_scalar(u[:], ps[0:N, 4, 0:DV], eg[:], None, ALU.mult))
                ch.link(v.tensor_tensor(u[:], rows[:, 2, :], u[:], ALU.subtract))
                ch.link(v.tensor_scalar(u[:], u[:], beta[:], None, ALU.mult))
                v.tensor_tensor(spread[:], bc(ident[0:N, 0:N].rearrange("p (i o) -> p i o", o=1), N, N, DV),
                                bc(u[:].rearrange("p (o j) -> p o j", o=1), N, N, DV), ALU.mult).then_inc(u_ready, 1)
                dve.wait_ge(turned_sb, 3)
                ch.link(v.tensor_tensor(state[:], state[:], bc(eb[:].rearrange("p (i o) -> p i o", o=1), P, N, DV), ALU.mult))
                dve.wait_ge(outer, 1)
                v.tensor_tensor(state[:].rearrange("p (c i) j -> p c (i j)", c=8), state[:].rearrange("p (c i) j -> p c (i j)", c=8), ps[:, :, :], ALU.add).then_inc(state_ready, 1)
                ch.link(v.tensor_scalar(zt[:], zt[:], 1.0, None, ALU.add))
                ch.link(v.tensor_tensor(zt[:], zt[:], z[:], ALU.mult))
                ch.link(v.tensor_tensor(zt[:], zt[:], w_gn[:], ALU.mult))
                dve.wait_ge(qs_row, 1)
                ch.link(v.tensor_copy(o[:], ps[0:N, 1, 0:DV]))
                ch.link(v.tensor_tensor(osq[:], o[:], o[:], ALU.mult))
                ch.link(v.tensor_reduce(s1[:], osq[:], AX_X, ALU.add))
                rsqrt(nc, ch, r1[:], s1[:], r2[:], 1.0 / DV, EPS, times=0.5)
                v.scalar_tensor_tensor(o[:], o[:], r1[:], zt[:], ALU.mult, ALU.mult).then_inc(o_ready, 1)

            @block.tensor
            def _(pe):
                pe.wait_ge(loaded, 16 * (9 + BS))
                pe.wait_ge(rows_in, 16)
                pe.transpose(ps[:, 0, 0:N], rows[:, 1, :], ident[0:N, 0:N])
                pe.transpose(ps[:, 1, 0:N], rows[:, 0, :], ident[0:N, 0:N]).then_inc(turned, 1)
                pe.wait_ge(diag_ready, 1)
                pe.matmul(ps[:, 2, 0:N], ones[0:N, :], diag[:], start=True, stop=True).then_inc(diag_ready, 1)
                pe.wait_ge(turned_sb, 1)
                for i in range(N):
                    last = pe.matmul(ps[:, 3, i:i + 1], state[:, i, :], kT[:, i:i + 1], start=True, stop=True)
                last.then_inc(ks_ps, 1)
                pe.wait_ge(ks_sb, 1)
                pe.transpose(ps[0:N, 4, 0:P], colT[:], ident[:]).then_inc(ks_row, 1)
                pe.wait_ge(u_ready, 1)
                pe.wait_ge(turned_sb, 3)
                for c in range(8):
                    last = pe.matmul(ps[:, c, :], rows[:, 1, :], spread[:, 4 * c:4 * c + 4, :].rearrange("p i j -> p (i j)"), start=True, stop=True)
                last.then_inc(outer, 1)
                pe.wait_ge(state_ready, 1)
                for i in range(N):
                    last = pe.matmul(ps[:, 0, i:i + 1], state[:, i, :], qT[:, i:i + 1], start=True, stop=True)
                last.then_inc(qs_ps, 1)
                pe.wait_ge(qs_sb, 1)
                pe.transpose(ps[0:N, 1, 0:P], colT[:], ident[:]).then_inc(qs_row, 1)


ATT_STEPS = 15


def phase_attention(nc, ps, A, keep):
    with ExitStack() as ctx, own_semaphores(nc) as own:
        def sb(n, s, d=F32):
            return ctx.enter_context(nc.sbuf_tensor("at_" + n, s, d))

        def sem(n):
            return own("at_" + n)

        HW = H * DV
        ident, causal = sb("ident", [P, P]), sb("causal", [P, P])
        qk = sb("qk", [P, TILES, 2 * HW])
        vals = sb("vals", [P, TILES, HW])
        cos, sin = sb("cos", [P, TILES, HALF]), sb("sin", [P, TILES, HALF])
        rot = sb("rot", [P, 4, TILES, 16, HALF])
        coef = sb("coef", [P, 2])
        w_sub = sb("w_sub", [P, DV])
        KT, qT = sb("KT", [P, H, RPAD]), sb("qT", [P, 2, H, P])
        prob, w = sb("prob", [P, 2, RPAD]), sb("w", [P, 2, RPAD])
        wT = sb("wT", [P, 2, 4 * P])
        nmax, sums, rcp = sb("nmax", [P, 2]), sb("sums", [P, 2]), sb("rcp", [P, 2])
        osq, ao = sb("osq", [P, H, DV]), sb("ao", [P, 2, H, DV])
        ss, rn, rt = sb("ss", [P, H]), sb("rn", [P, H]), sb("rt", [P, H])
        loaded, steps, rot_ready = sem("loaded"), sem("steps"), sem("rot_ready")
        kq_ps, kT_ready, qT_ready = sem("kq_ps"), sem("kT_ready"), sem("qT_ready")
        s_ps, max_ready, e_ready, w_ready = sem("s_ps"), sem("max_ready"), sem("e_ready"), sem("w_ready")
        wT_ps, wT_ready, av_ps, osq_ready = sem("wT_ps"), sem("wT_ready"), sem("av_ps"), sem("osq_ready")
        ao_ready, ao_stored, stored = sem("ao_ready"), [sem("ao_stored0"), sem("ao_stored1")], sem("stored")
        flat = ps[:].rearrange("p b j -> p (b j)")
        units = [(t, h) for t in range(TILES) for h in range(H)]
        groups = [(n, t, h, j0, min(j0 + 4, t + 1)) for n, (t, h) in enumerate(units) for j0 in range(0, t + 1, 4)]
        last_tile = TILES - 1
        tail = LP - last_tile * P

        with nc.Block() as block:
            @block.sync
            def _(sp):
                rows = A["proj"][CONV_W - 1:CONV_W - 1 + RPAD, :].rearrange("(t p) c -> p t c", p=P)
                for dst, src in [(qk[:], rows[:, :, C_DQ:C_DQ + 2 * HW]), (vals[:], rows[:, :, C_DV:C_DV + HW]),
                                 (ident[:], A["ident"]), (causal[:], A["causal"]), (cos[:], A["cos"]), (sin[:], A["sin"]),
                                 (w_sub[:], A["w_subln"].partition_broadcast(P)), (coef[:], A["coef"])]:
                    sp.dma_start(dst, src).then_inc(loaded, 16)
                sp.wait_ge(loaded, 16 * 8)
                sp.wait_ge(rot_ready, 1)
                for dst, src in [(A["p_k"][0:last_tile * P, :].rearrange("(t p) c -> p t c", p=P), qk[:, 0:last_tile, HW:2 * HW]),
                                 (A["p_v"][0:last_tile * P, :].rearrange("(t p) c -> p t c", p=P), vals[:, 0:last_tile, :]),
                                 (A["p_k"][last_tile * P:LP, :], qk[0:tail, last_tile, HW:2 * HW]),
                                 (A["p_v"][last_tile * P:LP, :], vals[0:tail, last_tile, :])]:
                    sp.dma_start(dst, src).then_inc(stored, 16)
                for t in range(TILES):
                    sp.wait_ge(ao_ready, t + 1)
                    for r0, r1 in ((0, P),) if t < last_tile else ((0, tail), (tail + BS, P)):
                        sp.dma_start(A["mix"][t * P + r0:t * P + r1, HW:2 * HW], ao[r0:r1, t % 2, :, :].rearrange("p h j -> p (h j)")).then_inc(ao_stored[t % 2], 16)
                sp.wait_ge(ao_stored[0], 16 * ((TILES + 1) // 2 + 1))
                sp.wait_ge(ao_stored[1], 16 * (TILES // 2))
                sp.wait_ge(stored, 16 * 4)

            @block.scalar
            def _(act):
                act.wait_ge(loaded, 16 * 8)

                def keys(t):
                    act.wait_ge(kq_ps, t + 1)
                    act.activation(KT[:, :, t * P:(t + 1) * P], ps[:, 6, :].rearrange("p (h j) -> p h j", h=H), ACT.Copy).then_inc(kT_ready, 1)

                def exps(n):
                    t, h = units[n]
                    wd = (t + 1) * P
                    act.wait_ge(max_ready, n + 1)
                    if n:
                        act.wait_ge(w_ready, n)
                    for c in range(2):
                        act.activation(prob[:, c, 0:wd], flat[:, c * 1536:c * 1536 + wd], ACT.Exp, bias=nmax[:, c:c + 1],
                                       accum_out=sums[:, c:c + 1]).then_inc(e_ready, 1)

                keys(0)
                exps(0)
                for g, (n, t, h, j0, j1) in enumerate(groups):
                    if j0 == 0 and n + 1 < len(units) and h < H - 1:
                        exps(n + 1)
                    act.wait_ge(wT_ps, g + 1)
                    act.activation(wT[:, g % 2, 0:(j1 - j0) * P], ps[:, 6, 0:(j1 - j0) * P], ACT.Copy).then_inc(wT_ready, 1)
                    if j1 == t + 1 and h == H - 1:
                        act.wait_ge(av_ps, n + 1)
                        act.activation(osq[:], ps[:, 7, :].rearrange("p (h j) -> p h j", h=H), ACT.Square).then_inc(osq_ready, 1)
                        if t < last_tile:
                            keys(t + 1)
                            exps(n + 1)

            @block.vector
            def _(dve):
                v = nc.vector
                ch = Chain(dve, steps, 0)
                dve.wait_ge(loaded, 16 * 8)
                x = qk[:].rearrange("p t (c j) -> p t c j", j=DQ)
                x1, x2 = x[:, :, :, 0:HALF], x[:, :, :, HALF:2 * HALF]
                sh = (P, TILES, 16, HALF)
                cb, sb_ = (bc(a[:].rearrange("p t (o j) -> p t o j", o=1), *sh) for a in (cos, sin))
                ch.done(v.tensor_tensor(rot[:, 0], x1, cb, ALU.mult))
                ch.done(v.tensor_tensor(rot[:, 1], x2, sb_, ALU.mult))
                ch.done(v.tensor_tensor(rot[:, 2], x2, cb, ALU.mult))
                ch.link(v.tensor_tensor(rot[:, 3], x1, sb_, ALU.mult))
                ch.done(v.tensor_tensor(x1, rot[:, 0], rot[:, 1], ALU.subtract))
                v.tensor_tensor(x2, rot[:, 2], rot[:, 3], ALU.add).then_inc(rot_ready, 1)

                def queries(t):
                    dve.wait_ge(kT_ready, t + 1)
                    dve.wait_ge(s_ps, 4 * t) if t else None
                    v.tensor_scalar(qT[:, t % 2, :, :], ps[:, 7, :].rearrange("p (h j) -> p h j", h=H), DQ ** -0.5, None, ALU.mult).then_inc(qT_ready, 1)

                def maxima(n):
                    t, h = units[n]
                    wd = (t + 1) * P
                    dve.wait_ge(s_ps, n + 1)
                    if n:
                        dve.wait_ge(e_ready, 2 * n)
                    ch.link(v.tensor_reduce(nmax[:, 0:1], flat[:, 0:wd], AX_X, ALU.max, negate=True))
                    v.tensor_reduce(nmax[:, 1:2], flat[:, 1536:1536 + wd], AX_X, ALU.max, negate=True).then_inc(max_ready, 1)

                queries(0)
                maxima(0)
                for n, (t, h) in enumerate(units):
                    wd = (t + 1) * P
                    dve.wait_ge(e_ready, 2 * n + 2)
                    ch.link(v.reciprocal(rcp[:], sums[:]))
                    ch.link(v.tensor_tensor(rcp[:], rcp[:], coef[:], ALU.mult))
                    ch.link(v.tensor_scalar(w[:, n % 2, 0:wd], prob[:, 1, 0:wd], rcp[:, 1:2], None, ALU.mult))
                    v.scalar_tensor_tensor(w[:, n % 2, 0:wd], prob[:, 0, 0:wd], rcp[:, 0:1], w[:, n % 2, 0:wd], ALU.mult, ALU.add).then_inc(w_ready, 1)
                    if h < H - 1:
                        maxima(n + 1)
                        continue
                    dve.wait_ge(osq_ready, t + 1)
                    ch.link(v.tensor_reduce(ss[:], osq[:], AX_X, ALU.add))
                    rsqrt(nc, ch, rn[:], ss[:], rt[:], 1.0 / DV, EPS, times=1.0 - LAM_INIT)
                    if t >= 2:
                        dve.wait_ge(ao_stored[t % 2], 16 * (t // 2))
                    ch.link(v.tensor_tensor(ao[:, t % 2], ps[:, 7, :].rearrange("p (h j) -> p h j", h=H), bc(rn[:].rearrange("p (h o) -> p h o", o=1), P, H, DV), ALU.mult))
                    v.tensor_tensor(ao[:, t % 2], ao[:, t % 2], bc(w_sub[:].rearrange("p (o j) -> p o j", o=1), P, H, DV), ALU.mult).then_inc(ao_ready, 1)
                    if t < last_tile:
                        queries(t + 1)
                        maxima(n + 1)

            @block.tensor
            def _(pe):
                pe.wait_ge(loaded, 16 * 8)
                pe.wait_ge(rot_ready, 1)

                def turn(t):
                    if t:
                        pe.wait_ge(ao_ready, t)
                    for b, o in ((6, HW), (7, 0)):
                        for h in range(H):
                            last = pe.transpose(ps[:, b, h * P:(h + 1) * P], qk[:, t, o + h * P:o + (h + 1) * P], ident[:])
                    last.then_inc(kq_ps, 1)

                def scores(n):
                    t, h = units[n]
                    wd = (t + 1) * P
                    if h == 0:
                        pe.wait_ge(kT_ready, t + 1)
                        pe.wait_ge(qT_ready, t + 1)
                    if n:
                        pe.wait_ge(e_ready, 2 * n)
                    for c in range(2):
                        q = qT[DQ * c:DQ * (c + 1), t % 2, h, :]
                        for k0 in range(0, wd, 512):
                            k1 = min(k0 + 512, wd)
                            diag = k1 == wd
                            pe.matmul(flat[:, c * 1536 + k0:c * 1536 + k1], q, KT[DQ * c:DQ * (c + 1), h, k0:k1], start=True, stop=not diag, skip_group_check=True)
                        last = pe.matmul(flat[:, c * 1536 + wd - P:c * 1536 + wd], ident[:], causal[:], start=False, stop=True, skip_group_check=True)
                    last.then_inc(s_ps, 1)

                turn(0)
                scores(0)
                for g, (n, t, h, j0, j1) in enumerate(groups):
                    if j0 == 0:
                        if h < H - 1:
                            scores(n + 1)
                        pe.wait_ge(w_ready, n + 1)
                    if g:
                        pe.wait_ge(wT_ready, g)
                    for j in range(j0, j1):
                        last = pe.transpose(ps[:, 6, (j - j0) * P:(j - j0 + 1) * P], w[:, n % 2, j * P:(j + 1) * P], ident[:])
                    last.then_inc(wT_ps, 1)
                    pe.wait_ge(wT_ready, g + 1)
                    if h == 0 and j0 == 0:
                        pe.wait_ge(qT_ready, t + 1)
                    for j in range(j0, j1):
                        last = pe.matmul(ps[:, 7, h * P:(h + 1) * P], wT[:, g % 2, (j - j0) * P:(j - j0 + 1) * P], vals[:, j, h * DV:(h + 1) * DV],
                                         start=(j == 0), stop=(j == t))
                    if j1 == t + 1:
                        last.then_inc(av_ps, 1)
                        if h == H - 1 and t < last_tile:
                            turn(t + 1)
                            scores(n + 1)


def phase_mix(nc, ps, A, keep):
    with ExitStack() as ctx, own_semaphores(nc) as own:
        def sb(n, s, d=F32):
            return ctx.enter_context(nc.sbuf_tensor("mx_" + n, s, d))

        def sem(n):
            return own("mx_" + n)

        def kept(n):
            return keep.enter_context(nc.semaphore("mx_" + n))

        NL = G + NE
        ident, ones, strict = sb("ident", [P, P]), sb("ones", [P, P]), sb("strict", [P, P])
        w_out, w_r, w_norm = sb("w_out", [P, KD, D]), sb("w_r", [P, KD, NL]), sb("w_norm", [P, D])
        x, mix = sb("x", [P, 2, D]), sb("mix", [P, 2, D])
        mixT, hnT = sb("mixT", [P, D]), sb("hnT", [P, D])
        x2, hn, squares = sb("x2", [P, 2, D]), sb("hn", [P, 2, D]), sb("squares", [P, D])
        sq, rs = sb("sq", [P, 1]), sb("rs", [P, 2])
        valid, dump, tok = sb("valid", [P, TILES]), sb("dump", [P, TILES, 2]), sb("tok", [P, TILES], I32)
        e_no, e_group = sb("e_no", [P, NE]), sb("e_group", [P, NE])
        lg, le, geq = sb("lg", [P, 8]), sb("le", [P, NE]), sb("geq", [P, NE])
        g8, gi8, e8, ei8 = sb("g8", [P, 8]), sb("gi8", [P, 8], U32), sb("e8", [P, 8]), sb("ei8", [P, 8], U32)
        gi, ei, ngm, gx, gs, gw = sb("gi", [P, 1]), sb("ei", [P, 2]), sb("ngm", [P, 1]), sb("gx", [P, G]), sb("gs", [P, 1]), sb("gw", [P, 1])
        dd, ex, pp = sb("dd", [P, 1]), sb("ex", [P, 1]), sb("pp", [P, 2])
        oh, wt = sb("oh", [P, TILES, 2, NE]), sb("wt", [P, TILES, 2])
        both, pre, rank = sb("both", [P, TILES, NE]), sb("pre", [P, TILES + 1, NE]), sb("rank", [P, TILES, NE])
        cnt, cnt_i, ntile, inc, inc2 = sb("cnt", [P, NE]), sb("cnt_i", [P, NE], I32), sb("ntile", [P, NE]), sb("inc", [P, NE]), sb("inc2", [P, NE])
        pick, slot, slot_i = sb("pick", [P, TILES, 2, NE]), sb("slot", [P, TILES, 2]), sb("slot_i", [P, TILES, 2], I32)
        slot_c = sb("slot_c", [P, TILES, 2], I32)
        tile_no, le_cmp, ownr, own_i = sb("tile_no", [1, SLOT_TILES]), sb("le_cmp", [1, SLOT_TILES, NE]), sb("own", [1, SLOT_TILES]), sb("own_i", [1, SLOT_TILES], I32)

        loaded = sem("loaded")
        in_loaded = [sem("in_loaded0"), sem("in_loaded1")]
        steps, waited = sem("steps"), sem("waited")
        mixT_ps, mixT_ready, x2_ps, x2_ready = sem("mixT_ps"), sem("mixT_ready"), sem("x2_ps"), sem("x2_ready")
        sq_ready, hn_ready, hnT_ps, hnT_ready, lg_ps = sem("sq_ready"), sem("hn_ready"), sem("hnT_ps"), sem("hnT_ready"), sem("lg_ps")
        g_in, g_out, tile_done = sem("g_in"), sem("g_out"), sem("tile_done")
        x2_stored, out_free = kept("x2_stored"), sem("out_free")
        pre_ready, rank_ps, slots_ready, scattered = sem("pre_ready"), sem("rank_ps"), sem("slots_ready"), kept("scattered")
        own_ready, stored = sem("own_ready"), sem("stored")
        NC = 14

        with nc.Block() as block:
            @block.sync
            def _(sp):
                consts = [(ident[:], A["ident"]), (ones[:], A["ones"]), (strict[:], A["strict"]),
                          (w_out[:], A["w_out"].rearrange("(c p) n -> p c n", p=P)),
                          (w_r[:, :, 0:G], A["w_group"].rearrange("(c p) n -> p c n", p=P)),
                          (w_r[:, :, G:NL], A["w_expert"].rearrange("(c p) n -> p c n", p=P)),
                          (w_norm[:], A["w_norm_ffn"].partition_broadcast(P)), (valid[:], A["valid"]), (dump[:], A["dump"]),
                          (tok[:], A["tok"]), (e_no[:], A["e_no"]), (e_group[:], A["e_group"]), (tile_no[:], A["tile_no"]),
                          (A["slot_tok"], A["slot_fill"])]
                assert len(consts) == NC
                for dst, src in consts:
                    sp.dma_start(dst, src).then_inc(loaded, 16)
                for t, par, k in tiles(sp):
                    if not isinstance(t, int):
                        sp.wait_ge(x2_ready, t)
                    sp.dma_start(x[:, par, :], A["x"][bass.ds(t * P, P), :]).then_inc(in_loaded[par], 16)
                    sp.dma_start(mix[:, par, :], A["mix"][bass.ds(t * P, P), :]).then_inc(in_loaded[par], 16)
                sp.wait_ge(slots_ready, 2)
                sp.dma_start(A["slots"], slot_c[:].rearrange("p t c -> p (t c)")).then_inc(stored, 16)
                sp.dma_start(A["weights"], wt[:].rearrange("p t c -> p (t c)")).then_inc(stored, 16)
                sp.wait_ge(own_ready, 1)
                sp.dma_start(A["owner"], own_i[:]).then_inc(stored, 16)
                sp.wait_ge(stored, 48)

            @block.gpsimd
            def _(pool):
                pool.sem_inc(out_free, 2)
                for t, par, k in tiles(pool):
                    if not isinstance(t, int):
                        pool.wait_ge(x2_stored, 32 * t)
                        pool.sem_inc(out_free, 1)
                    pool.wait_ge(hn_ready, t + 1)
                    pool.dma_start(A["x2"][bass.ds(t * P, P), :], x2[:, par, :]).then_inc(x2_stored, 16)
                    pool.dma_start(A["hn"][bass.ds(t * P, P), :], hn[:, par, :]).then_inc(x2_stored, 16)
                pool.wait_ge(x2_stored, 32 * TILES)
                pool.wait_ge(slots_ready, 2)
                for t in range(TILES):
                    for c in range(2):
                        pool.indirect_dma_start(out=A["slot_tok"], out_offset=bass.IndirectOffsetOnAxis(ap=slot_i[:, t, c:c + 1], axis=0),
                                                in_=tok[:, t:t + 1], in_offset=None).then_inc(scattered, 16)
                pool.wait_ge(scattered, 32 * TILES)

            @block.scalar
            def _(act):
                for t, par, k in tiles(act):
                    act.wait_ge(mixT_ps, t + 1)
                    act.activation(mixT[:].rearrange("p (a b) -> p a b", a=2), ps[:, 0:2, :], ACT.Copy).then_inc(mixT_ready, 1)
                    act.wait_ge(x2_ready, t + 1)
                    act.activation(squares[:], x2[:, par, :], ACT.Square, accum_out=sq[:]).then_inc(sq_ready, 1)
                    act.wait_ge(hnT_ps, t + 1)
                    act.activation(hnT[:].rearrange("p (a b) -> p a b", a=2), ps[:, 4:6, :], ACT.Copy).then_inc(hnT_ready, 1)
                    act.wait_ge(g_in, 2 * t + 1)
                    act.activation(gx[:], lg[:, 0:G], ACT.Exp, bias=ngm[:], accum_out=gs[:]).then_inc(g_out, 1)
                    act.wait_ge(g_in, 2 * t + 2)
                    act.activation(ex[:], dd[:], ACT.Exp).then_inc(g_out, 1)

            @block.vector
            def _(dve):
                v = nc.vector
                ch = Chain(dve, steps, MIX_STEPS)
                pre_ch = Chain(dve, own("mx_pre_steps"), 0)
                dve.wait_ge(loaded, 16 * NC)
                pre_ch.link(v.memset(lg[:], -BIG))
                for t, par, k in tiles(dve):
                    ch.begin(t)
                    dve.wait_ge(in_loaded[par], 32 * (k + 1))
                    dve.wait_ge(x2_ps, t + 1)
                    dve.wait_ge(out_free, t + 1)
                    v.tensor_tensor(x2[:, par, :].rearrange("p (a b) -> p a b", a=2), x[:, par, :].rearrange("p (a b) -> p a b", a=2), ps[:, 2:4, :], ALU.add).then_inc(x2_ready, 1)
                    dve.wait_ge(sq_ready, t + 1)
                    rsqrt(nc, ch, rs[:, 0:1], sq[:], rs[:, 1:2], 1.0 / D, EPS)
                    v.scalar_tensor_tensor(hn[:, par, :], x2[:, par, :], rs[:, 0:1], w_norm[:], ALU.mult, ALU.mult).then_inc(hn_ready, 1)
                    dve.wait_ge(lg_ps, t + 1)
                    ch.link(v.tensor_copy(lg[:, 0:G], ps[:, 6, 0:G]))
                    dve.sem_inc(waited, 1)
                    ch.link(v.max(g8[:], lg[:]))
                    v.tensor_scalar(ngm[:], g8[:, 0:1], -1.0, None, ALU.mult).then_inc(g_in, 1)
                    ch.link(v.max_index(gi8[:], g8[:], lg[:]))
                    ch.link(v.tensor_copy(gi[:], gi8[:, 0:1]))
                    ch.link(v.tensor_scalar(geq[:], e_group[:], gi[:], None, ALU.is_equal))
                    ch.link(v.tensor_scalar(geq[:], geq[:], -1.0, BIG, ALU.add, ALU.mult))
                    ch.link(v.tensor_tensor(le[:], ps[:, 6, G:NL], geq[:], ALU.add))
                    dve.sem_inc(waited, 1)
                    ch.link(v.max(e8[:], le[:]))
                    v.tensor_tensor(dd[:], e8[:, 1:2], e8[:, 0:1], ALU.subtract).then_inc(g_in, 1)
                    ch.link(v.max_index(ei8[:], e8[:], le[:]))
                    ch.link(v.tensor_copy(ei[:], ei8[:, 0:2]))
                    for c in range(2):
                        ch.done(v.tensor_scalar(oh[:, bass.ds(t, 1), c, :].rearrange("p t e -> p (t e)"), e_no[:], ei[:, c:c + 1], None, ALU.is_equal))
                    dve.wait_ge(g_out, 2 * t + 2)
                    ch.done(v.reciprocal(gw[:], gs[:]))
                    ch.link(v.tensor_scalar(pp[:, 0:1], ex[:], 1.0, None, ALU.add))
                    ch.link(v.reciprocal(pp[:, 0:1], pp[:, 0:1]))
                    ch.link(v.tensor_tensor(pp[:, 0:1], pp[:, 0:1], gw[:], ALU.mult))
                    ch.link(v.tensor_tensor(pp[:, 1:2], pp[:, 0:1], ex[:], ALU.mult))
                    ch.link(v.tensor_copy(wt[:, bass.ds(t, 1), :].rearrange("p t c -> p (t c)"), pp[:]))
                    ch.end()
                vb = bc(valid[:].rearrange("p (t c e) -> p t c e", c=1, e=1), P, TILES, 2, NE)
                pc = pre_ch
                pc.link(v.tensor_tensor(oh[:], oh[:], vb, ALU.mult))
                pc.link(v.tensor_tensor(both[:], oh[:, :, 0, :], oh[:, :, 1, :], ALU.add))
                pc.link(v.memset(pre[:, 0, :], 0.0))
                for t in range(TILES):
                    ins = v.tensor_tensor(pre[:, t + 1, :], pre[:, t, :], both[:, t, :], ALU.add)
                    pc.link(ins)
                dve.sem_inc(pre_ready, 1)
                dve.wait_ge(rank_ps, 1)
                pc.link(v.tensor_copy(cnt[:], ps[:, 1, 0:NE]))
                pc.link(v.tensor_scalar(cnt_i[:], cnt[:], float(P - 1), None, ALU.add))
                pc.link(v.tensor_scalar(cnt_i[:], cnt_i[:], 7, None, ALU.logical_shift_right))
                pc.link(v.tensor_copy(ntile[:], cnt_i[:]))
                pc.link(v.tensor_copy(inc[:], ntile[:]))
                a, b = inc, inc2
                for s in (1, 2, 4, 8, 16):
                    pc.done(v.tensor_copy(b[:, 0:s], a[:, 0:s]))
                    pc.link(v.tensor_tensor(b[:, s:NE], a[:, s:NE], a[:, 0:NE - s], ALU.add))
                    a, b = b, a
                pc.link(v.tensor_tensor(b[:], a[:], ntile[:], ALU.subtract))
                pc.link(v.tensor_scalar(b[:], b[:], float(P), None, ALU.mult))
                pc.link(v.tensor_tensor(rank[:], ps[:, 0, 0:TILES * NE].rearrange("p (t e) -> p t e", t=TILES), bc(b[:].rearrange("p (o e) -> p o e", o=1), P, TILES, NE), ALU.add))
                for c in range(2):
                    pc.link(v.tensor_tensor(pick[:, :, c, :], oh[:, :, c, :], rank[:], ALU.mult))
                pc.link(v.tensor_reduce(slot[:], pick[:], AX_X, ALU.add))
                pc.link(v.tensor_tensor(slot[:], slot[:], dump[:], ALU.add))
                pc.link(v.tensor_copy(slot_i[:], slot[:]))
                v.tensor_scalar(slot_c[:], slot[:], float(SLOTS - 1), None, ALU.min).then_inc(slots_ready, 1)
                v.tensor_tensor(wt[:], wt[:], bc(valid[:].rearrange("p (t c) -> p t c", c=1), P, TILES, 2), ALU.mult).then_inc(slots_ready, 1)
                pc.link(v.tensor_tensor(le_cmp[:], bc(a[0:1, :].rearrange("p (o e) -> p o e", o=1), 1, SLOT_TILES, NE),
                                        bc(tile_no[:].rearrange("p (j o) -> p j o", o=1), 1, SLOT_TILES, NE), ALU.is_le))
                pc.link(v.tensor_reduce(ownr[:], le_cmp[:], AX_X, ALU.add))
                v.tensor_scalar(own_i[:], ownr[:], float(NE - 1), None, ALU.min).then_inc(own_ready, 1)

            @block.tensor
            def _(pe):
                pe.wait_ge(loaded, 16 * NC)
                for t, par, k in tiles(pe):
                    pe.wait_ge(in_loaded[par], 32 * (k + 1))
                    for c in range(KD):
                        last = pe.transpose(ps[:, c // 4, (c % 4) * P:(c % 4 + 1) * P], mix[:, par, c * P:(c + 1) * P], ident[:])
                    last.then_inc(mixT_ps, 1)
                    pe.wait_ge(mixT_ready, t + 1)
                    for n in range(2):
                        for c in range(KD):
                            last = pe.matmul(ps[:, 2 + n, :], mixT[:, c * P:(c + 1) * P], w_out[:, c, n * 512:(n + 1) * 512], start=(c == 0), stop=(c == KD - 1))
                    last.then_inc(x2_ps, 1)
                    pe.wait_ge(hn_ready, t + 1)
                    for c in range(KD):
                        last = pe.transpose(ps[:, 4 + c // 4, (c % 4) * P:(c % 4 + 1) * P], hn[:, par, c * P:(c + 1) * P], ident[:])
                    last.then_inc(hnT_ps, 1)
                    pe.wait_ge(hnT_ready, t + 1)
                    for c in range(KD):
                        last = pe.matmul(ps[:, 6, 0:NL], hnT[:, c * P:(c + 1) * P], w_r[:, c, :], start=(c == 0), stop=(c == KD - 1))
                    last.then_inc(lg_ps, 1)
                pe.wait_ge(pre_ready, 1)
                flat = both[:].rearrange("p t e -> p (t e)")
                pe.matmul(ps[:, 0, 0:TILES * NE], strict[:], flat, start=True, stop=False)
                pe.matmul(ps[:, 0, 0:TILES * NE], ones[:], pre[:, 0:TILES, :].rearrange("p t e -> p (t e)"), start=False, stop=True)
                pe.matmul(ps[:, 1, 0:NE], ones[:], pre[:, TILES, :], start=True, stop=True).then_inc(rank_ps, 1)


MIX_STEPS = 30


def phase_experts(nc, ps, A, keep):
    with ExitStack() as ctx, own_semaphores(nc) as own:
        def sb(n, s, d=F32):
            return ctx.enter_context(nc.sbuf_tensor("ex_" + n, s, d))

        def sem(n):
            return own("ex_" + n)

        def kept(n):
            return keep.enter_context(nc.semaphore("ex_" + n))

        NF = FE // P
        ident = sb("ident", [P, P])
        owner = sb("owner", [1, SLOT_TILES], I32)
        rows_of = sb("rows_of", [P, SLOT_TILES + 2], I32)
        idx = [sb(f"idx{i}", [P, 1], I32) for i in range(2)]
        w_gu, w_d = sb("w_gu", [P, 2, KD, 2 * FE]), sb("w_d", [P, 2, NF, D])
        xg, xT = sb("xg", [P, 2, D]), sb("xT", [P, 2, D])
        th, act_g, hh, hhT = sb("th", [P, FE]), sb("act_g", [P, FE]), sb("hh", [P, FE]), sb("hhT", [P, FE])
        y = sb("y", [P, 2, D])
        loaded, waited = sem("loaded"), sem("waited")
        gu_loaded, d_loaded = [sem("gu_loaded0"), sem("gu_loaded1")], [sem("d_loaded0"), sem("d_loaded1")]
        idx_ready, x_loaded, x_used = sem("idx_ready"), [kept("x_loaded0"), kept("x_loaded1")], sem("x_used")
        xT_ready, gu_ps, th_ready, ag_ready, hh_ready = sem("xT_ready"), sem("gu_ps"), sem("th_ready"), sem("ag_ready"), sem("hh_ready")
        hhT_ps, hhT_ready, y_ps, y0_ready, y1_ready = sem("hhT_ps"), sem("hhT_ready"), sem("y_ps"), sem("y0_ready"), sem("y1_ready")
        y_stored, y_free = kept("y_stored"), sem("y_free")

        with nc.Block() as block:
            @block.sync
            def _(sp):
                sp.dma_start(ident[:], A["ident"]).then_inc(loaded, 16)
                sp.dma_start(owner[:], A["owner"]).then_inc(loaded, 16)
                with nc.allow_non_contiguous_dma(reason="slot lists are 4 bytes per slot"):
                    sp.dma_start(rows_of[:], A["slot_tok"].rearrange("(j p) o -> p (j o)", p=P)).then_inc(loaded, 16)
                sp.wait_ge(loaded, 48)
                with sp.Fori(0, SLOT_TILES // 2) as u:
                    for par in range(2):
                        j = 2 * u + par
                        e = sp.value_load(owner[0:1, bass.ds(j, 1)], min_val=0, max_val=NE - 1)
                        sp.wait_ge(gu_ps, j + 1)
                        sp.dma_start(w_gu[:, par, :, 0:FE], A["w_gate"][bass.ds(e, 1)].rearrange("e (p c) f -> (e p) c f", c=KD)).then_inc(gu_loaded[par], 16)
                        sp.dma_start(w_gu[:, par, :, FE:2 * FE], A["w_up"][bass.ds(e, 1)].rearrange("e (p c) f -> (e p) c f", c=KD)).then_inc(gu_loaded[par], 16)
                        sp.wait_ge(y_ps, j + 1)
                        sp.dma_start(w_d[:, par, :, :], A["w_down"][bass.ds(e, 1)].rearrange("e (p c) n -> (e p) c n", c=NF)).then_inc(d_loaded[par], 16)

            @block.gpsimd
            def _(pool):
                pool.wait_ge(loaded, 48)
                pool.sem_inc(y_free, 2)

                def gather(j, par):
                    pool.wait_ge(x_used, j + 1)
                    pool.tensor_copy(idx[par][:], rows_of[:, bass.ds(j, 1)]).then_inc(idx_ready, 1)
                    pool.wait_ge(idx_ready, j + 1)
                    pool.sem_inc(waited, 1)
                    pool.indirect_dma_start(out=xg[:, par, :], out_offset=None, in_=A["hn"],
                                            in_offset=bass.IndirectOffsetOnAxis(ap=idx[par][:], axis=0)).then_inc(x_loaded[par], 16)

                def store(j, par, first_one):
                    pool.wait_ge(y0_ready, j + 2)
                    pool.wait_ge(y1_ready, j + 2)
                    if not first_one:
                        pool.wait_ge(y_stored, 16 * j)
                        pool.sem_inc(y_free, 1)
                    pool.dma_start(A["ys"][bass.ds(j * P, P), :], y[:, par, :]).then_inc(y_stored, 16)

                gather(0, 0)
                gather(1, 1)
                gather(2, 0)
                store(0, 0, True)
                gather(3, 1)
                store(1, 1, False)
                with pool.Fori(1, SLOT_TILES // 2) as u:
                    for par in range(2):
                        if par == 0:
                            gather(2 * u + 2, 0)
                        store(2 * u + par, par, False)
                        if par == 0:
                            gather(2 * u + 3, 1)
                pool.wait_ge(y_stored, 16 * SLOT_TILES)
                pool.wait_ge(x_loaded[0], 16 * (SLOT_TILES // 2 + 1))
                pool.wait_ge(x_loaded[1], 16 * (SLOT_TILES // 2 + 1))

            @block.scalar
            def _(act):
                def turned(j, par):
                    act.wait_ge(x_used, j + 3)
                    act.activation(xT[:, par, :].rearrange("p (a b) -> p a b", a=2), ps[:, 0:2, :], ACT.Copy).then_inc(xT_ready, 1)

                turned(0, 0)
                with act.Fori(0, SLOT_TILES // 2) as u:
                    for par in range(2):
                        j = 2 * u + par
                        act.wait_ge(gu_ps, j + 3)
                        act.activation(th[:], ps[:, 2, 0:FE], ACT.Tanh, scale=0.5).then_inc(th_ready, 1)
                        turned(j + 1, 1 - par)
                        act.wait_ge(y_ps, j + 3)
                        act.wait_ge(y_free, j + 1)
                        act.activation(y[:, par, 0:512], ps[:, 4, :], ACT.Copy).then_inc(y0_ready, 1)

            @block.vector
            def _(dve):
                v = nc.vector
                with dve.Fori(0, SLOT_TILES // 2) as u:
                    for par in range(2):
                        j = 2 * u + par
                        dve.wait_ge(th_ready, j + 1)
                        v.scalar_tensor_tensor(act_g[:], th[:], 1.0, ps[:, 2, 0:FE], ALU.add, ALU.mult).then_inc(ag_ready, 1)
                        dve.wait_ge(ag_ready, j + 1)
                        v.scalar_tensor_tensor(hh[:], act_g[:], 0.5, ps[:, 2, FE:2 * FE], ALU.mult, ALU.mult).then_inc(hh_ready, 1)
                        dve.wait_ge(hhT_ps, j + 1)
                        v.tensor_copy(hhT[:], ps[:, 3, 0:FE]).then_inc(hhT_ready, 1)
                        dve.wait_ge(y_ps, j + 3)
                        dve.wait_ge(y_free, j + 1)
                        v.tensor_copy(y[:, par, 512:1024], ps[:, 5, :]).then_inc(y1_ready, 1)

            @block.tensor
            def _(pe):
                pe.wait_ge(loaded, 48)
                pe.sem_inc(gu_ps, 2)
                pe.sem_inc(y_ps, 2)
                pe.sem_inc(x_used, 2)
                pe.sem_inc(y0_ready, 1)
                pe.sem_inc(y1_ready, 1)

                def turn(j, par, k):
                    pe.wait_ge(x_loaded[par], 16 * (k + 1))
                    xv = xg[:, par, :].rearrange("p (i c) -> p c i", c=KD)
                    for c in range(KD):
                        last = pe.transpose(ps[:, c // 4, (c % 4) * P:(c % 4 + 1) * P], xv[:, c, :], ident[:])
                    last.then_inc(x_used, 1)

                turn(0, 0, 0)
                with pe.Fori(0, SLOT_TILES // 2) as u:
                    for par in range(2):
                        j = 2 * u + par
                        pe.wait_ge(gu_loaded[par], 32 * (u + 1))
                        pe.wait_ge(xT_ready, j + 1)
                        for c in range(KD):
                            last = pe.matmul(ps[:, 2, :], xT[:, par, c * P:(c + 1) * P], w_gu[:, par, c, :], start=(c == 0), stop=(c == KD - 1))
                        last.then_inc(gu_ps, 1)
                        turn(j + 1, 1 - par, u + par)
                        pe.wait_ge(hh_ready, j + 1)
                        hv = hh[:].rearrange("p (i c) -> p c i", c=NF)
                        for c in range(NF):
                            last = pe.transpose(ps[:, 3, c * P:(c + 1) * P], hv[:, c, :], ident[:])
                        last.then_inc(hhT_ps, 1)
                        pe.wait_ge(hhT_ready, j + 1)
                        pe.wait_ge(d_loaded[par], 16 * (u + 1))
                        pe.wait_ge(y0_ready, j + 1)
                        pe.wait_ge(y1_ready, j + 1)
                        for n in range(2):
                            for c in range(NF):
                                last = pe.matmul(ps[:, 4 + n, :], hhT[:, c * P:(c + 1) * P], w_d[:, par, c, n * 512:(n + 1) * 512], start=(c == 0), stop=(c == NF - 1))
                        last.then_inc(y_ps, 1)


def phase_combine(nc, ps, A, keep):
    with ExitStack() as ctx, own_semaphores(nc) as own:
        def sb(n, s, d=F32):
            return ctx.enter_context(nc.sbuf_tensor("co_" + n, s, d))

        def sem(n):
            return own("co_" + n)

        def kept(n):
            return keep.enter_context(nc.semaphore("co_" + n))

        w_fin = sb("w_fin", [P, D])
        slots, wt = sb("slots", [P, TILES, 2], I32), sb("wt", [P, TILES, 2])
        idx = sb("idx", [P, 2, 2], I32)
        x2, ya, yb, out = sb("x2", [P, 2, D]), sb("ya", [P, 2, D]), sb("yb", [P, 2, D]), sb("out", [P, 2, D])
        wts = sb("wts", [P, 2])
        squares, sq, rs = sb("squares", [P, D]), sb("sq", [P, 1]), sb("rs", [P, 2])
        loaded, steps = sem("loaded"), sem("steps")
        x_loaded, y_loaded = [sem("x_loaded0"), sem("x_loaded1")], [kept("y_loaded0"), kept("y_loaded1")]
        idx_ready, used, sum_ready, sq_ready, out_ready = sem("idx_ready"), sem("used"), sem("sum_ready"), sem("sq_ready"), sem("out_ready")
        out_stored = [sem("out_stored0"), sem("out_stored1")]

        with nc.Block() as block:
            @block.sync
            def _(sp):
                sp.dma_start(w_fin[:], A["w_final"].partition_broadcast(P)).then_inc(loaded, 16)
                sp.dma_start(slots[:].rearrange("p t c -> p (t c)"), A["slots"]).then_inc(loaded, 16)
                sp.dma_start(wt[:].rearrange("p t c -> p (t c)"), A["weights"]).then_inc(loaded, 16)
                for t in range(TILES):
                    if t >= 2:
                        sp.wait_ge(out_ready, t - 1)
                    sp.dma_start(x2[:, t % 2, :], A["x2"][t * P:(t + 1) * P, :]).then_inc(x_loaded[t % 2], 16)
                    if t:
                        sp.wait_ge(out_ready, t)
                        sp.dma_start(A["y"][(t - 1) * P:t * P, :], out[:, (t - 1) % 2, :]).then_inc(out_stored[(t - 1) % 2], 16)
                sp.wait_ge(out_ready, TILES)
                sp.dma_start(A["y"][(TILES - 1) * P:TILES * P, :], out[:, (TILES - 1) % 2, :]).then_inc(out_stored[(TILES - 1) % 2], 16)
                sp.wait_ge(out_stored[0], 16 * ((TILES + 1) // 2))
                sp.wait_ge(out_stored[1], 16 * (TILES // 2))

            @block.gpsimd
            def _(pool):
                pool.wait_ge(loaded, 48)
                for t in range(TILES):
                    if t >= 2:
                        pool.wait_ge(out_ready, t - 1)
                    for c, dst in ((0, ya), (1, yb)):
                        pool.indirect_dma_start(out=dst[:, t % 2, :], out_offset=None, in_=A["ys"],
                                                in_offset=bass.IndirectOffsetOnAxis(ap=slots[:, t, c:c + 1], axis=0)).then_inc(y_loaded[t % 2], 16)

            @block.scalar
            def _(act):
                for t in range(TILES):
                    act.wait_ge(sum_ready, t + 1)
                    act.activation(squares[:], out[:, t % 2, :], ACT.Square, accum_out=sq[:]).then_inc(sq_ready, 1)

            @block.vector
            def _(dve):
                v = nc.vector
                ch = Chain(dve, steps, 0)
                dve.wait_ge(loaded, 48)
                for t in range(TILES):
                    p = t % 2
                    dve.wait_ge(x_loaded[p], 16 * (t // 2 + 1))
                    dve.wait_ge(y_loaded[p], 32 * (t // 2 + 1))
                    if t >= 2:
                        dve.wait_ge(out_stored[p], 16 * (t // 2))
                    ch.link(v.scalar_tensor_tensor(out[:, p, :], ya[:, p, :], wt[:, t, 0:1], x2[:, p, :], ALU.mult, ALU.add))
                    v.scalar_tensor_tensor(out[:, p, :], yb[:, p, :], wt[:, t, 1:2], out[:, p, :], ALU.mult, ALU.add).then_inc(sum_ready, 1)
                    dve.wait_ge(sq_ready, t + 1)
                    rsqrt(nc, ch, rs[:, 0:1], sq[:], rs[:, 1:2], 1.0 / D, EPS)
                    v.scalar_tensor_tensor(out[:, p, :], out[:, p, :], rs[:, 0:1], w_fin[:], ALU.mult, ALU.mult).then_inc(out_ready, 1)


SCRATCH = {"proj": (RPAD + CONV_W - 1, PROJ_W), "mix": (RPAD, 2 * H * DV), "gates_s": (2, BS, H),
           "rows_s": (3, BS, H * DK), "q_s": (BS, H * DV), "coef": (P, 2), "o_s": (BS * H, DV),
           "x2": (RPAD, D), "hn": (RPAD, D), "ys": (SLOTS, D), "weights": (P, 2 * TILES)}
INT_SCRATCH = {"slot_tok": (SLOTS + 2 * P, 1), "slots": (P, 2 * TILES), "owner": (1, SLOT_TILES)}
OUTS = {"y": (RPAD, D), "p_conv": (CONV_W - 1, CONV_CH), "p_gdn": (H, DK, DV), "p_k": (LP, H * DV), "p_v": (LP, H * DV),
        "s_conv": (BS, CONV_W - 1, CONV_CH), "s_gdn": (BS * H, DK, DV), "s_k": (BS, H * DV), "s_v": (BS, H * DV)}


def program(nc, A):
    with ExitStack() as ctx:
        ps = ctx.enter_context(nc.psum_tensor("ps", [P, 8, 512], F32))
        phase_project(nc, ps, A, ctx)
        phase_recurrence_and_decode(nc, ps, A, ctx)
        phase_sample_gdn(nc, ps, A, ctx)
        phase_attention(nc, ps, A, ctx)
        phase_mix(nc, ps, A, ctx)
        phase_experts(nc, ps, A, ctx)
        phase_combine(nc, ps, A, ctx)


def constants():
    r = np.arange(P)
    f = np.float32
    c = {"ident": np.eye(P, dtype=f), "ones": np.ones((P, P), f), "upper": (r[:, None] <= r[None, :]).astype(f)}
    levels = np.zeros((P, 7, P), f)
    for l in range(7):
        s = 1 << l
        b = r // s
        levels[:, l, :] = (b[:, None] // 2 == b[None, :] // 2) & (b[:, None] % 2 == 1) & (b[None, :] % 2 == 0)
    c["levels"] = levels
    c["rowmask"] = (r[:, None] + P * np.arange(TILES)[None, :] < LP).astype(f)
    row = r[:, None] + P * np.arange(TILES)[None, :]
    c["valid"] = (row < ROWS).astype(f)
    c["dump"] = np.where(row < ROWS, 0, SLOTS + r[:, None])[:, :, None] + np.where(row < ROWS, 0, P)[:, :, None] * np.arange(2)
    c["dump"] = c["dump"].astype(f)
    c["tok"] = row.astype(np.int32)
    c["e_no"] = np.ascontiguousarray(np.broadcast_to(np.arange(NE, dtype=f), (P, NE)))
    c["e_group"] = np.ascontiguousarray(np.broadcast_to((np.arange(NE) // EPG).astype(f), (P, NE)))
    c["tile_no"] = np.arange(SLOT_TILES, dtype=f)[None, :]
    c["slot_fill"] = np.full((SLOTS + 2 * P, 1), RPAD - 1, np.int32)
    c["first"] = np.where(r == 0, f(0), f(-BIG))[:, None]
    c["strict"] = (r[:, None] < r[None, :]).astype(f)
    c["causal"] = np.where(r[:, None] >= r[None, :], f(0), f(-BIG))
    inv_freq = f(ROPE_THETA) ** (-np.arange(HALF, dtype=f) * f(2) / f(4 * HALF // 2))
    pos = np.where(np.arange(RPAD) < LP, np.arange(RPAD), PAST).astype(f)
    ang = (pos[:, None] * inv_freq[None, :]).reshape(TILES, P, HALF).transpose(1, 0, 2)
    c["cos"], c["sin"] = np.ascontiguousarray(np.cos(ang)), np.ascontiguousarray(np.sin(ang))
    c["cos_s"], c["sin_s"] = (np.ascontiguousarray(np.broadcast_to(c[n][LP % P, TILES - 1], (BS, HALF))) for n in ("cos", "sin"))
    return c


def kernel(**inputs):
    import numpy as _np
    import concourse.bacc as _bacc
    from concourse import mybir as _mybir
    from concourse.bass_utils import run_bass_kernel_spmd as _run

    nc = _bacc.Bacc("TRN2", target_bir_lowering=False, num_devices=1)
    i = {n: _np.ascontiguousarray(a) for n, a in inputs.items()}
    arrays = {
        "x": _np.concatenate([i["meta_tokens"], i["x_prompt"][0], i["x_sample"][:, 0],
                              _np.zeros((RPAD + P - ROWS, D), i["x_prompt"].dtype)], axis=0),
        "w_in": i["w_in"][0], "w_norm_mix": i["w_norm_mix"][0], "w_conv": i["w_conv"][0],
        "w_gnorm": i["w_gnorm"][0], "a_log": i["a_log"][0], "dt_bias": i["dt_bias"][0],
        "state_conv": i["state_conv"][0], "state_gdn": i["state_gdn"][0].reshape(BS * H, DK, DV), "w_subln": i["w_subln"][0],
        "cache_k": i["cache_k"][0].reshape(-1, PAGE, H * 2 * DQ), "cache_v": i["cache_v"][0].reshape(-1, PAGE, H * DV),
        "page_table": i["page_table"].reshape(1, BS * N_PAGES), "w_out": i["w_out"][0], "w_norm_ffn": i["w_norm_ffn"][0],
        "w_final": i["w_final"], **{n: i[n][0] for n in ("w_group", "w_expert", "w_gate", "w_up", "w_down")},
        **{n: i[n][0] for n in ("lambda_q1", "lambda_k1", "lambda_q2", "lambda_k2")},
    }
    arrays.update(constants())
    A = {}
    for n, a in arrays.items():
        A[n] = nc.dram_tensor("in_" + n, a.shape, _mybir.dt.from_np(a.dtype), kind="ExternalInput").ap()
    for n, shape in SCRATCH.items():
        A[n] = nc.dram_tensor("scr_" + n, shape, F32, kind="Internal").ap()
    for n, shape in INT_SCRATCH.items():
        A[n] = nc.dram_tensor("scr_" + n, shape, I32, kind="Internal").ap()
    for n, shape in OUTS.items():
        A[n] = nc.dram_tensor("out_" + n, shape, F32, kind="ExternalOutput").ap()
    program(nc, A)
    r = _run(nc, [{"in_" + n: a for n, a in arrays.items()}], core_ids=[0]).results[0]
    o = {n: r["out_" + n] for n in OUTS}
    return (o["y"][N_META:LP].reshape(1, SEQ, D), o["y"][LP:ROWS].reshape(BS, 1, D),
            o["p_conv"].reshape(1, 1, CONV_W - 1, CONV_CH), o["p_gdn"].reshape(1, 1, H, DK, DV),
            o["p_k"].reshape(1, 1, LP, H, 2 * DQ), o["p_v"].reshape(1, 1, LP, H, DV),
            o["s_conv"].reshape(1, BS, CONV_W - 1, CONV_CH), o["s_gdn"].reshape(1, BS, H, DK, DV),
            o["s_k"].reshape(1, BS, 1, H, 2 * DQ), o["s_v"].reshape(1, BS, 1, H, DV))
```

```python
import math
from contextlib import ExitStack, contextmanager

import numpy as np

import concourse.bass as bass
from concourse import mybir

F32 = mybir.dt.float32
I32 = mybir.dt.int32
U32 = mybir.dt.uint32
ALU = mybir.AluOpType
ACT = mybir.ActivationFunctionType
AX_X = mybir.AxisListType.X

P = 128
D = 1024
KD = D // P
SEQ, N_META = 1024, 16
LP = SEQ + N_META
BS = 8
ROWS = LP + BS
TILES = -(-ROWS // P)
RPAD = TILES * P
EPS = 1e-6
H = 4
DK = DV = 128
DQ = 64
CONV_W = 4
CONV_CH = 3 * H * DK
C_Z = CONV_CH
C_A = C_Z + H * DV
C_B = C_A + H
C_DQ = C_B + H
C_DK = C_DQ + H * 2 * DQ
C_DV = C_DK + H * 2 * DQ
PROJ_W = C_DV + H * DV
HALF = DQ // 4 // 2
ROPE_THETA = 500000.0
PAST, PAGE = 8192, 128
N_PAGES = PAST // PAGE
LAM_INIT = 0.8 - 0.6 * math.exp(-0.3 * 0)
G, EPG, NE, FE = 4, 8, 32, 256
SLOT_TILES = (2 * ROWS) // P + NE
SLOTS = SLOT_TILES * P
BIG = 1e30


@contextmanager
def own_semaphores(nc):
    held = []

    def own(name):
        held.append(nc.alloc_semaphore(name))
        return held[-1]

    yield own
    nc.clear_and_free_semaphores(held)
    nc.all_engine_barrier()


def tiles(eng, n=TILES):
    yield 0, 0, 0
    with eng.Fori(0, (n - 1) // 2) as u:
        yield 2 * u + 1, 1, u
        yield 2 * u + 2, 0, u + 1


class Chain:

    def __init__(self, eng, sem, per):
        self.eng, self.sem, self.per, self.base, self.n = eng, sem, per, 0, 0

    def begin(self, t):
        self.base, self.n = t * self.per, 0

    def done(self, ins):
        self.n += 1
        ins.then_inc(self.sem, 1)

    def sync(self):
        self.eng.wait_ge(self.sem, self.base + self.n)

    def link(self, ins):
        self.done(ins)
        self.sync()

    def end(self):
        assert self.n == self.per, f"{self.sem}: {self.n} steps, {self.per} declared"


RSQRT_STEPS = 12


def rsqrt(nc, ch, y, x, tmp, scale, bias, times=1.0):
    v = nc.vector
    ch.link(v.tensor_scalar(x, x, scale, bias, ALU.mult, ALU.add))
    ch.link(v.tensor_scalar(tmp.bitcast(I32), x.bitcast(I32), 1, None, ALU.logical_shift_right))
    ch.link(v.tensor_scalar(y.bitcast(I32), tmp.bitcast(I32), -1, 0x5F3759DF, ALU.mult, ALU.add))
    for step in range(3):
        last = times if step == 2 else 1.0
        ch.link(v.tensor_tensor(tmp, y, y, ALU.mult))
        ch.link(v.scalar_tensor_tensor(tmp, tmp, -0.5 * last, x, ALU.mult, ALU.mult))
        ch.link(v.scalar_tensor_tensor(y, tmp, 1.5 * last, y, ALU.add, ALU.mult))


def bc(ap, *shape):
    return ap.to_broadcast(list(shape))


def phase_project(nc, ps, A, keep):
    with ExitStack() as ctx, own_semaphores(nc) as own:
        def sb(n, s, d=F32):
            return ctx.enter_context(nc.sbuf_tensor("pj_" + n, s, d))

        def sem(n):
            return own("pj_" + n)

        def kept(n):
            return keep.enter_context(nc.semaphore("pj_" + n))

        w_in = sb("w_in", [P, KD, PROJ_W])
        w_norm = sb("w_norm", [P, D])
        ident = sb("ident", [P, P])
        x = sb("x", [P, 2, D])
        xn = sb("xn", [P, D])
        xT = sb("xT", [P, 2, D])
        proj = sb("proj", [P, 2, PROJ_W])
        sq = sb("sq", [P, 1])
        rs = sb("rs", [P, 2])
        squares = sb("squares", [P, D])
        zero = sb("zero", [4, (CONV_W - 1) * PROJ_W // 4])

        w_loaded = [sem(f"w_loaded{i}") for i in range(KD)]
        c_loaded = sem("c_loaded")
        x_loaded = [sem("x_loaded0"), sem("x_loaded1")]
        cleared, zeroed = sem("cleared"), kept("zeroed")
        sq_ready = sem("sq_ready")
        steps = sem("dve_steps")
        xn_ready = sem("xn_ready")
        xnT_ready = sem("xnT_ready")
        xT_ready = sem("xT_ready")
        mm_done = sem("mm_done")
        act_evac = sem("act_evac")
        dve_evac = sem("dve_evac")
        stored, proj_free = kept("stored"), sem("proj_free")
        NCH = 8
        cols = [(n * 512, min(512, PROJ_W - n * 512)) for n in range(NCH)]

        with nc.Block() as block:
            @block.sync
            def _(sp):
                def load(t, par):
                    sp.dma_start(x[:, par, :], A["x"][bass.ds(t * P, P), :]).then_inc(x_loaded[par], 16)

                load(0, 0)
                sp.dma_start(ident[:], A["ident"]).then_inc(c_loaded, 16)
                sp.dma_start(w_norm[:], A["w_norm_mix"].partition_broadcast(P)).then_inc(c_loaded, 16)
                for c in range(KD):
                    sp.dma_start(w_in[:, c, :], A["w_in"][c * P:(c + 1) * P, :]).then_inc(w_loaded[c], 16)
                for t, par, k in tiles(sp):
                    if not isinstance(t, int):
                        sp.wait_ge(xn_ready, t)
                    load(t + 1, 1 - par)

            @block.gpsimd
            def _(pool):
                pool.sem_inc(proj_free, 2)
                pool.memset(zero[:], 0.0).then_inc(cleared, 1)
                pool.wait_ge(cleared, 1)
                pool.dma_start(A["proj"][0:CONV_W - 1, :].rearrange("i n -> (i n)").rearrange("(p n) -> p n", p=4), zero[:]).then_inc(zeroed, 16)
                pool.wait_ge(zeroed, 16)
                for t, par, k in tiles(pool):
                    pool.wait_ge(act_evac, 4 * t + 4)
                    pool.wait_ge(dve_evac, 4 * t + 4)
                    if not isinstance(t, int):
                        pool.wait_ge(stored, 16 * t)
                        pool.sem_inc(proj_free, 1)
                    pool.dma_start(A["proj"][bass.ds(t * P + CONV_W - 1, P), :],
                                   proj[:, par, :]).then_inc(stored, 16)
                pool.wait_ge(stored, 16 * TILES)

            @block.scalar
            def _(act):
                def square(t, par, k):
                    act.wait_ge(x_loaded[par], 16 * (k + 1))
                    act.activation(squares[:], x[:, par, :], ACT.Square, accum_out=sq[:]).then_inc(sq_ready, 1)

                square(0, 0, 0)
                for t, par, k in tiles(act):
                    act.wait_ge(xnT_ready, t + 1)
                    act.activation(xT[:, par, :].rearrange("p (a b) -> p a b", a=2), ps[:, 0:2, :], ACT.Copy).then_inc(xT_ready, 1)
                    act.wait_ge(proj_free, t + 1)
                    for n in range(0, NCH, 2):
                        o, w = cols[n]
                        act.wait_ge(mm_done, 8 * t + n + 1)
                        act.activation(proj[:, par, o:o + w], ps[:, 2 + n % 4, 0:w], ACT.Copy).then_inc(act_evac, 1)
                        if n == 0:
                            act.wait_ge(xn_ready, t + 1)
                            square(t + 1, 1 - par, k + par)

            @block.vector
            def _(dve):
                ch = Chain(dve, steps, 12)

                def norm(t, par):
                    ch.begin(t)
                    dve.wait_ge(sq_ready, t + 1)
                    rsqrt(nc, ch, rs[:, 0:1], sq[:], rs[:, 1:2], 1.0 / D, EPS)
                    ch.end()
                    if not isinstance(t, int) or t > 0:
                        dve.wait_ge(xnT_ready, t)
                    nc.vector.scalar_tensor_tensor(xn[:], x[:, par, :], rs[:, 0:1], w_norm[:],
                                                   ALU.mult, ALU.mult).then_inc(xn_ready, 1)

                dve.wait_ge(c_loaded, 32)
                norm(0, 0)
                for t, par, k in tiles(dve):
                    dve.wait_ge(proj_free, t + 1)
                    for n in range(1, NCH, 2):
                        o, w = cols[n]
                        dve.wait_ge(mm_done, 8 * t + n + 1)
                        nc.vector.tensor_copy(proj[:, par, o:o + w], ps[:, 2 + n % 4, 0:w]).then_inc(dve_evac, 1)
                        if n == 1:
                            norm(t + 1, 1 - par)

            @block.tensor
            def _(pe):
                pe.wait_ge(c_loaded, 32)
                for t, par, k in tiles(pe):
                    pe.wait_ge(xn_ready, t + 1)
                    if not isinstance(t, int):
                        pe.wait_ge(xT_ready, t)
                    for c in range(KD):
                        last = pe.transpose(ps[:, c // 4, (c % 4) * P:(c % 4 + 1) * P], xn[:, c * P:(c + 1) * P], ident[:])
                    last.then_inc(xnT_ready, 1)
                    pe.wait_ge(xT_ready, t + 1)
                    for n in range(NCH):
                        o, w = cols[n]
                        if not (isinstance(t, int) and n < 4):
                            pe.wait_ge(dve_evac if n % 2 else act_evac, 4 * t + n // 2 - 1)
                        for c in range(KD):
                            if isinstance(t, int) and n == 0:
                                pe.wait_ge(w_loaded[c], 16)
                            last = pe.matmul(ps[:, 2 + n % 4, 0:w], xT[:, par, c * P:(c + 1) * P],
                                             w_in[:, c, o:o + w], start=(c == 0), stop=(c == KD - 1))
                        last.then_inc(mm_done, 1)


CHUNK = 4
CHUNKS = N_PAGES // CHUNK
PRE_LOADS = 11 + CHUNK
RING = 4


def phase_recurrence_and_decode(nc, ps, A, keep):
    with ExitStack() as ctx, own_semaphores(nc) as own:
        def sb(n, s, d=F32):
            return ctx.enter_context(nc.sbuf_tensor("gd_" + n, s, d))

        def sem(n):
            return own("gd_" + n)

        def kept(n):
            return keep.enter_context(nc.semaphore("gd_" + n))

        HP = [P, H, P]
        HW = H * P
        ident, upper, ones = sb("ident", [P, P]), sb("upper", [P, P]), sb("ones", [P, P])
        levels = sb("levels", [P, 7, P])
        w_conv = sb("w_conv", [P, CONV_W, CONV_CH])
        w_gn = sb("w_gn", [P, DV])
        rowmask = sb("rowmask", [P, TILES])
        a_log, dt_bias = sb("a_log", [P, H]), sb("dt_bias", [P, H])
        ab = sb("ab", [P, TILES, 2 * H])
        ga, gb, gc = sb("ga", [P, TILES, H]), sb("gb", [P, TILES, H]), sb("gc", [P, TILES, H])
        gate, beta = sb("gate", [P, TILES, H]), sb("beta", [P, TILES, H])
        gu, bu = sb("gu", [P, TILES, H]), sb("bu", [P, TILES, H])
        cs = sb("cs", [P, CONV_W, CONV_CH])
        z = sb("z", [P, HW])
        th = sb("th", [P, CONV_CH])
        qkv = sb("qkv", [P, 3, HW])
        ss, rn, rt = sb("ss", [P, 8]), sb("rn", [P, 8]), sb("rt", [P, 8])
        gcol, glg, eg, beg, egl = (sb(n, [P, H]) for n in ("gcol", "glg", "eg", "beg", "egl"))
        egrow = sb("egrow", HP)
        dt = sb("dt", HP)
        kT, qT, qgT = sb("kT", HP), sb("qT", HP), sb("qgT", HP)
        vb, kbg, kw = sb("vb", HP), sb("kbg", HP), sb("kw", HP)
        ug, ib = kbg, kw
        LT, qkT = sb("LT", HP), sb("qkT", HP)
        TT = sb("TT", [P, 2, H, P])
        prod = sb("prod", HP)
        nwT, u, S = sb("nwT", HP), sb("u", HP), sb("S", HP)
        osq, on, zt, zs = prod, sb("on", HP), sb("zt", [P, HW]), sb("zs", [P, HW])

        C = 2 * H
        NP1 = N_PAGES + 1
        pages, lane = sb("pages", [P, BS * CHUNKS], I32), sb("lane", [P, BS * CHUNKS], I32)
        keys, vals = sb("keys", [P, RING, CHUNK, HW]), sb("vals", [P, RING, CHUNK, HW])
        q, kn, vn = sb("q", [P, BS, HW]), sb("kn", [P, HW]), sb("vn", [P, HW])
        first, coef = sb("first", [P, 1]), sb("coef", [P, 2])
        s, e = sb("s", [P, NP1, C]), sb("e", [P, NP1, C])
        w = sb("w", [P, NP1, H])
        m, mx, l, lt, r = (sb(n, [P, C]) for n in ("m", "mx", "l", "lt", "r"))
        o = sb("o", [H, HW])
        od, dsq, w_sub = sb("od", [BS * H, DV]), sb("dsq", [BS * H, DV]), sb("w_sub", [BS * H, DV])
        s1, r1, r2 = sb("s1", [BS * H, 1]), sb("r1", [BS * H, 1]), sb("r2", [BS * H, 1])
        qk_s = vals[0:BS, 0, 0:2, :].rearrange("p a c -> p (a c)")
        rot = vals[0:BS, 1, 0, :].rearrange("p (a c j) -> p a c j", a=4, j=HALF)
        cos, sin = vals[0:BS, 1, 1, 0:HALF], vals[0:BS, 1, 1, HALF:2 * HALF]
        lams = vals[:, 2, 0, 0:4 * DQ].rearrange("p (i j) -> p i j", i=4)
        lprod = vals[:, 2, 1, 0:2 * DQ].rearrange("p (i j) -> p i j", i=2)
        lsum, lexp = vals[:, 2, 2, 0:2], vals[:, 2, 2, 2:4]
        pre_loaded, rot_ready, pre_stored, q_loaded, lam_ready = (sem(n) for n in ("pre_loaded", "rot_ready", "pre_stored", "q_loaded", "lam_ready"))
        new_loaded, vn_loaded = sem("new_loaded"), sem("vn_loaded")
        k_loaded, v_loaded = [kept(f"k_loaded{i}") for i in range(RING)], [kept(f"v_loaded{i}") for i in range(RING)]
        k_index, v_index = sb("k_index", [P, RING, 1], I32), sb("v_index", [P, RING, 1], I32)
        pages_ready, k_picked, v_picked = sem("pages_ready"), sem("k_picked"), sem("v_picked")
        k_mult, k_mult_pool, k_used, v_used = sem("k_mult"), sem("k_mult_pool"), sem("k_used"), sem("v_used")
        dsteps, waited = sem("dsteps"), sem("waited")
        m_ready, mx_ready, s_ready, e_ready, l_ready, lt_ready = (sem(n) for n in ("m_ready", "mx_ready", "s_ready", "e_ready", "l_ready", "lt_ready"))
        w_ready, pv_done, od_ready, od_stored = sem("w_ready"), sem("pv_done"), sem("od_ready"), sem("od_stored")
        od_loaded, dn_ready, od_clear = sem("od_loaded"), sem("dn_ready"), sem("od_clear")

        c_loaded = sem("c_loaded")
        in_loaded = sem("in_loaded")
        cs_used, z_used = sem("cs_used"), sem("z_used")
        steps, psteps, asteps = sem("dve_steps"), sem("pool_steps"), sem("act_steps")
        gate_a, gate_b, gate_c = sem("gate_exp"), sem("gate_log"), sem("gates_ready")
        conv23, pconv = sem("conv23_ready"), sem("pool_conv_steps")
        conv_ready, th_ready = sem("conv_ready"), sem("tanh_ready")
        ug_ready, g_ps = sem("ug_ready"), sem("g_ps")
        qk_ready, qkT_ps, kqT_ready = sem("qk_ready"), sem("qkT_ps"), sem("kqT_ready")
        d_in, d_ready, eg_ready = sem("d_in"), sem("d_ready"), sem("eg_ready")
        operands = sem("operands_ready")
        kk_ps = sem("kk_ps")
        t_ready, p_ps, p_ready, dT_ps = sem("t_ready"), sem("p_ps"), sem("p_ready"), sem("dT_ps")
        w_ps, nw_ready, u_ps, u_ready = sem("w_ps"), sem("nw_ready"), sem("u_ps"), sem("u_ready")
        o_ps, osq_ready, zs_ready, zt_ready = sem("o_ps"), sem("osq_ready"), sem("zs_ready"), sem("zt_ready")
        on_free = sem("on_free")
        on_ready, on_stored, out_done = sem("on_ready"), kept("on_stored"), sem("out_done")

        def bank(b):
            return ps[:, b, :].rearrange("p (h j) -> p h j", h=H)

        def turns(eng, end=BS):
            yield 0, True, False
            with eng.Fori(1, end) as t:
                yield t, True, True
            for t in range(end, BS):
                yield t, True, True
            yield BS, False, True

        with nc.Block() as block:
            @block.sync
            def _(sp):
                for dst, src in ((ident[:], A["ident"]), (upper[:], A["upper"]), (ones[:], A["ones"]),
                                 (levels[:], A["levels"]), (rowmask[:], A["rowmask"]),
                                 (w_conv[:].rearrange("p i c -> p (i c)"), A["w_conv"].rearrange("i c -> (i c)").partition_broadcast(P)),
                                 (w_gn[:], A["w_gnorm"].partition_broadcast(P)),
                                 (a_log[:], A["a_log"].partition_broadcast(P)),
                                 (dt_bias[:], A["dt_bias"].partition_broadcast(P)),
                                 (ab[:], A["proj"][CONV_W - 1:CONV_W - 1 + RPAD, C_A:C_A + 2 * H].rearrange("(t p) c -> p t c", p=P))):
                    sp.dma_start(dst, src).then_inc(c_loaded, 16)
                def load(t):
                    sp.wait_ge(cs_used, t + 1)
                    for i in range(CONV_W):
                        sp.dma_start(cs[:, i, :], A["proj"][bass.ds(t * P + i, P), 0:CONV_CH]).then_inc(in_loaded, 16)
                    sp.wait_ge(z_used, t + 1)
                    sp.dma_start(z[:], A["proj"][bass.ds(t * P + CONV_W - 1, P), C_Z:C_Z + HW]).then_inc(in_loaded, 16)

                load(0)
                row0 = CONV_W - 1 + LP
                for dst, src in [(qk_s, A["proj"][row0:row0 + BS, C_DQ:C_DQ + 2 * HW]), (cos, A["cos_s"]), (sin, A["sin_s"]),
                                 (lane[:], A["lane"]), (first[:], A["first"]), (w_sub[:], A["w_subln"].partition_broadcast(BS * H)),
                                 (A["s_v"], A["proj"][row0:row0 + BS, C_DV:C_DV + HW])] + \
                                [(pages[g * P // CHUNK:(g + 1) * P // CHUNK, :], A["page_table"][g, :].partition_broadcast(P // CHUNK)) for g in range(CHUNK)] + \
                                [(lams[:, i, :], A[n].partition_broadcast(P)) for i, n in enumerate(("lambda_q1", "lambda_q2", "lambda_k1", "lambda_k2"))]:
                    sp.dma_start(dst, src).then_inc(pre_loaded, 16)
                sp.wait_ge(rot_ready, 1)
                sp.wait_ge(lam_ready, 3)
                for dst, src in [(A["q_s"], qk_s[:, 0:HW]), (A["s_k"], qk_s[:, HW:2 * HW]), (A["coef"], coef[:])]:
                    sp.dma_start(dst, src).then_inc(pre_stored, 16)
                sp.wait_ge(pre_stored, 48)
                sp.wait_ge(pre_loaded, 16 * PRE_LOADS)
                sp.dma_start(q[:].rearrange("p b c -> p (b c)"), A["q_s"].rearrange("b c -> (b c)").partition_broadcast(P)).then_inc(q_loaded, 16)

                for t, with_k, with_v in turns(sp):
                    if with_k:
                        if with_v:
                            sp.wait_ge(w_ready, t)
                        sp.dma_start(kn[:], A["s_k"][bass.ds(t, 1), :].rearrange("b c -> (b c)").partition_broadcast(P)).then_inc(new_loaded, 16)
                    if with_v:
                        sp.wait_ge(pv_done, t)
                        sp.dma_start(vn[:], A["s_v"][bass.ds(t - 1, 1), :].rearrange("b c -> (b c)").partition_broadcast(P)).then_inc(vn_loaded, 16)
                    if with_k:
                        load(t + 1)
                sp.wait_ge(od_stored, 16 * H * BS)
                sp.dma_start(od[:], A["o_s"]).then_inc(od_loaded, 16)
                sp.wait_ge(dn_ready, 1)
                for b in range(BS):
                    sp.dma_start(A["mix"][LP + b, HW:2 * HW].rearrange("(h j) -> h j", h=H), od[b * H:(b + 1) * H, :]).then_inc(out_done, 16)
                sp.wait_ge(on_stored, 16 * TILES)
                sp.dma_start(A["p_gdn"].rearrange("h k v -> k h v"), S[:]).then_inc(out_done, 16)
                last = TILES - 1
                r0 = LP - last * P
                sp.dma_start(A["gates_s"][0], gu[r0:r0 + BS, last, :]).then_inc(out_done, 16)
                sp.dma_start(A["gates_s"][1], bu[r0:r0 + BS, last, :]).then_inc(out_done, 16)
                sp.wait_ge(out_done, 48 + 16 * BS)

            @block.gpsimd
            def _(pool):
                ch = Chain(pool, psteps, 6)
                pool.sem_inc(cs_used, 1)
                pool.sem_inc(z_used, 1)
                pool.sem_inc(k_used, RING)
                pool.sem_inc(v_used, RING)

                def multiply(t, i):
                    pool.wait_ge(k_loaded[i % RING], 16 * (CHUNKS // RING * t + i // RING + 1))
                    pool.sem_inc(waited, 1)
                    pool.tensor_tensor(keys[:, i % RING], keys[:, i % RING], bc(q[:, bass.ds(t, 1), :], P, CHUNK, HW), ALU.mult).then_inc(k_mult_pool, 1)

                def gather(cache, buf, index, picked, done, used, b, i):
                    step = CHUNKS * b + i
                    pool.wait_ge(used, step + 1)
                    pool.sem_inc(waited, 1)
                    pool.tensor_copy(index[:, i % RING, :], pages[:, bass.ds(step, 1)]).then_inc(picked, 1)
                    pool.wait_ge(picked, step + 1)
                    pool.sem_inc(waited, 1)
                    pool.indirect_dma_start(out=buf[:, i % RING, :, :].rearrange("p a c -> p (a c)"), out_offset=None,
                                            in_=A[cache].rearrange("g (l a) c -> (g l) (a c)", a=CHUNK),
                                            in_offset=bass.IndirectOffsetOnAxis(ap=index[:, i % RING, :], axis=0)).then_inc(done[i % RING], 16)

                def keys_of(t, i):
                    gather("cache_k", keys, k_index, k_picked, k_loaded, k_used, t, i)

                def values_of(t, i):
                    gather("cache_v", vals, v_index, v_picked, v_loaded, v_used, t, i)

                pool.sem_inc(on_free, 1)
                pool.wait_ge(pages_ready, 1)
                for i in range(RING):
                    keys_of(0, i)
                pool.wait_ge(c_loaded, 160)
                pool.wait_ge(gate_c, 1)
                pool.wait_ge(q_loaded, 16)
                conv = Chain(pool, pconv, 2)

                def conv_tap(t, i):
                    if i == 2:
                        conv.begin(t)
                        pool.wait_ge(in_loaded, 80 * (t + 1))
                    if i is None:
                        conv.sync()
                        conv.end()
                        pool.tensor_tensor(cs[:, 2, :], cs[:, 2, :], cs[:, 3, :], ALU.add).then_inc(conv23, 1)
                    else:
                        conv.done(pool.tensor_tensor(cs[:, i, :], cs[:, i, :], w_conv[:, i, :], ALU.mult))

                for i in (2, 3, None):
                    conv_tap(0, i)
                for t, with_k, with_v in turns(pool, BS - 1):
                    def refill_keys(*steps):
                        for i in steps:
                            if with_k:
                                keys_of(t, i + RING)

                    def refill_values(*steps):
                        for i in steps:
                            if with_v:
                                values_of(t - 1, i + RING)

                    def products(i):
                        if with_k:
                            multiply(t, i)

                    def taps(i):
                        if with_k:
                            conv_tap(t + 1, i)

                    ch.begin(t)
                    products(1)
                    refill_values(0, 1)
                    products(3)
                    refill_values(2, 3)
                    pool.wait_ge(eg_ready, t + 1)
                    pool.wait_ge(qk_ready, t + 1)
                    ch.done(pool.tensor_tensor(beg[:], beta[:, bass.ds(t, 1), :].rearrange("p t h -> p (t h)"), eg[:], ALU.mult))
                    ch.done(pool.tensor_tensor(vb[:], qkv[:, 2, :].rearrange("p (h j) -> p h j", h=H),
                                               bc(beta[:, bass.ds(t, 1), :].rearrange("p t (h o) -> p (t h) o", o=1), *HP), ALU.mult))
                    pool.wait_ge(d_ready, t + 1)
                    ch.link(pool.tensor_tensor(kw[:], qkv[:, 1, :].rearrange("p (h j) -> p h j", h=H),
                                               bc(egl[:].rearrange("p (h o) -> p h o", o=1), *HP), ALU.mult))
                    ch.link(pool.tensor_tensor(kbg[:], qkv[:, 1, :].rearrange("p (h j) -> p h j", h=H),
                                               bc(beg[:].rearrange("p (h o) -> p h o", o=1), *HP), ALU.mult))
                    pool.wait_ge(kqT_ready, t + 1)
                    pool.tensor_tensor(qgT[:], qT[:], egrow[:], ALU.mult).then_inc(operands, 1)
                    refill_keys(0, 1)
                    refill_values(4)
                    refill_keys(2)
                    products(5)
                    pool.wait_ge(zt_ready, t + 1)
                    ch.link(pool.tensor_tensor(zs[:], zt[:], z[:], ALU.mult))
                    ch.link(pool.tensor_tensor(zs[:], zs[:], z[:], ALU.add))
                    pool.sem_inc(z_used, 1)
                    ch.end()
                    refill_values(5)
                    refill_keys(3)
                    refill_values(6)
                    refill_keys(4)
                    products(7)
                    if with_v:
                        pool.wait_ge(on_stored, 16 * t)
                        pool.sem_inc(on_free, 1)
                    refill_values(7)
                    refill_keys(5)
                    taps(2)
                    refill_values(8)
                    refill_keys(6)
                    products(9)
                    refill_values(9)
                    taps(3)
                    refill_keys(7)
                    refill_values(10)
                    refill_keys(8, 9)
                    products(11)
                    refill_keys(10)
                    refill_values(11)
                    taps(None)
                    products(13)
                    refill_keys(11)
                    more_keys = with_k and (not isinstance(t, int) or t < BS - 1)
                    for i in range(RING):
                        if more_keys:
                            keys_of(t + 1, i)
                        if with_k:
                            values_of(t, i)
                    if with_k:
                        pool.wait_ge(m_ready, t + 1)
                        pool.sem_inc(waited, 1)
                        pool.partition_all_reduce(mx[:], m[:], P, bass.bass_isa.ReduceOp.max).then_inc(mx_ready, 1)
                        pool.wait_ge(l_ready, t + 1)
                        pool.sem_inc(waited, 1)
                        pool.partition_all_reduce(lt[:], l[:], P, bass.bass_isa.ReduceOp.add).then_inc(lt_ready, 1)
                    pool.wait_ge(on_ready, t + 1)
                    pool.dma_start(A["mix"][bass.ds(t * P, P), 0:HW], on[:].rearrange("p h j -> p (h j)")).then_inc(on_stored, 16)

            @block.scalar
            def _(act):
                act.wait_ge(c_loaded, 160)
                act.wait_ge(gate_a, 1)
                act.activation(ga[:], gc[:], ACT.Abs).then_inc(gate_a, 1)
                act.wait_ge(gate_a, 2)
                act.activation(gb[:], ga[:], ACT.Exp, scale=-1.0).then_inc(gate_a, 1)
                act.activation(a_log[:], a_log[:], ACT.Exp).then_inc(gate_a, 1)
                act.activation(bu[:], ab[:, :, H:2 * H], ACT.Exp, scale=-1.0).then_inc(gate_a, 1)
                act.wait_ge(gate_b, 1)
                act.activation(gb[:], gb[:], ACT.Ln).then_inc(gate_b, 1)
                act.sem_inc(od_clear, 1)
                act.wait_ge(lam_ready, 1)
                act.activation(lexp, lsum, ACT.Exp).then_inc(lam_ready, 1)
                for t, with_k, with_v in turns(act):
                    act.wait_ge(conv_ready, t + 1)
                    act.activation(th[:], cs[:, 0, :], ACT.Tanh).then_inc(th_ready, 1)
                    act.wait_ge(zs_ready, t + 1)
                    act.activation(zt[:], z[:], ACT.Tanh, scale=0.5).then_inc(zt_ready, 1)
                    act.wait_ge(g_ps, t + 1)
                    act.activation(eg[:], ps[:, 5, 0:H], ACT.Exp).then_inc(asteps, 1)
                    act.activation(gcol[:], ps[:, 5, 0:H], ACT.Copy).then_inc(asteps, 1)
                    act.activation(egrow[:], bank(1), ACT.Exp).then_inc(eg_ready, 1)
                    act.wait_ge(d_in, t + 1)
                    act.activation(egl[:], glg[:], ACT.Exp).then_inc(asteps, 1)
                    act.activation(dt[:], dt[:], ACT.Exp).then_inc(d_ready, 1)
                    act.wait_ge(qkT_ps, t + 1)
                    act.activation(kT[:], bank(3), ACT.Copy).then_inc(asteps, 1)
                    act.activation(qT[:], bank(4), ACT.Copy).then_inc(kqT_ready, 1)
                    act.wait_ge(w_ps, t + 1)
                    act.activation(nwT[:], bank(6), ACT.Copy, scale=-1.0).then_inc(nw_ready, 1)
                    act.wait_ge(u_ps, t + 1)
                    act.activation(u[:], bank(5), ACT.Copy).then_inc(u_ready, 1)
                    act.wait_ge(o_ps, t + 1)
                    act.activation(osq[:], bank(7), ACT.Square).then_inc(osq_ready, 1)
                    if with_k:
                        act.wait_ge(s_ready, t + 1)
                        act.activation(e[:], s[:], ACT.Exp, scale=DQ ** -0.5).then_inc(e_ready, 1)
                    if with_v:
                        act.wait_ge(pv_done, t + 1)
                        act.wait_ge(od_clear, t)
                        act.activation(o[:], ps[0:H, 0, :], ACT.Copy).then_inc(od_ready, 1)
                        act.wait_ge(od_ready, t + 1)
                        for h in range(H):
                            act.dma_start(A["o_s"][bass.ds((t - 1) * H + h, 1), :], o[h:h + 1, h * DV:(h + 1) * DV]).then_inc(od_stored, 16)
                        act.wait_ge(od_stored, 16 * H * t)
                        act.sem_inc(od_clear, 1)

            @block.vector
            def _(dve):
                v = nc.vector
                ch = Chain(dve, steps, DVE_GDN_STEPS)
                pre = Chain(dve, own("gd_gate_steps"), 0)
                dve.wait_ge(c_loaded, 160)
                v.tensor_tensor(gc[:], ab[:, :, 0:H], bc(dt_bias[:].rearrange("p (o h) -> p o h", o=1), P, TILES, H), ALU.add).then_inc(gate_a, 1)
                dve.wait_ge(gate_a, 5)
                pre.link(v.tensor_scalar(gc[:], gc[:], 0.0, None, ALU.max))
                v.tensor_scalar(gb[:], gb[:], 1.0, None, ALU.add).then_inc(gate_b, 1)
                pre.link(v.tensor_scalar(bu[:], bu[:], 1.0, None, ALU.add))
                pre.link(v.reciprocal(bu[:], bu[:]))
                pre.link(v.tensor_tensor(beta[:], bu[:], bc(rowmask[:].rearrange("p (t o) -> p t o", o=1), P, TILES, H), ALU.mult))
                dve.wait_ge(gate_b, 2)
                pre.link(v.tensor_tensor(gc[:], gc[:], gb[:], ALU.add))
                pre.link(v.scalar_tensor_tensor(gu[:], gc[:], -1.0, bc(a_log[:].rearrange("p (o h) -> p o h", o=1), P, TILES, H), ALU.mult, ALU.mult))
                pre.link(v.tensor_tensor(gate[:], gu[:], bc(rowmask[:].rearrange("p (t o) -> p t o", o=1), P, TILES, H), ALU.mult))
                pre.link(v.tensor_scalar(w_conv[:], w_conv[:], 0.5, None, ALU.mult))
                pre.link(v.tensor_scalar(w_gn[:], w_gn[:], 0.5, None, ALU.mult))
                v.memset(S[:], 0.0).then_inc(gate_c, 1)
                dve.wait_ge(pre_loaded, 16 * PRE_LOADS)
                v.scalar_tensor_tensor(pages[:], pages[:], P // CHUNK, lane[:], ALU.mult, ALU.add).then_inc(pages_ready, 1)
                pre.link(v.tensor_tensor(lprod, lams[:, 0:2, :], lams[:, 2:4, :], ALU.mult))
                v.tensor_reduce(lsum, lprod, AX_X, ALU.add).then_inc(lam_ready, 1)
                x = qk_s.rearrange("p (c j) -> p c j", j=DQ)
                x1, x2 = x[:, :, 0:HALF], x[:, :, HALF:2 * HALF]
                cb, sb_ = (bc(a.rearrange("p (o j) -> p o j", o=1), BS, 16, HALF) for a in (cos, sin))
                pre.done(v.tensor_tensor(rot[:, 0], x1, cb, ALU.mult))
                pre.done(v.tensor_tensor(rot[:, 1], x2, sb_, ALU.mult))
                pre.done(v.tensor_tensor(rot[:, 2], x2, cb, ALU.mult))
                pre.link(v.tensor_tensor(rot[:, 3], x1, sb_, ALU.mult))
                pre.done(v.tensor_tensor(x1, rot[:, 0], rot[:, 1], ALU.subtract))
                v.tensor_tensor(x2, rot[:, 2], rot[:, 3], ALU.add).then_inc(rot_ready, 1)
                dve.wait_ge(lam_ready, 2)
                pre.done(v.memset(coef[:, 0:1], 1.0))
                pre.link(v.tensor_tensor(coef[:, 1:2], lexp[:, 1:2], lexp[:, 0:1], ALU.subtract))
                v.tensor_scalar(coef[:, 1:2], coef[:, 1:2], -LAM_INIT, None, ALU.add).then_inc(lam_ready, 1)
                dve.wait_ge(lam_ready, 3)
                dve.wait_ge(gate_c, 1)
                dve.wait_ge(q_loaded, 16)
                dve.sem_inc(zs_ready, 1)

                MINE = CHUNKS // 2 + 1

                def keys_times_query(t, i):
                    dve.wait_ge(k_loaded[i % RING], 16 * (CHUNKS // RING * t + i // RING + 1))
                    v.tensor_tensor(keys[:, i % RING], keys[:, i % RING], bc(q[:, bass.ds(t, 1), :], P, CHUNK, HW), ALU.mult).then_inc(k_mult, 1)

                def score(t, i):
                    if i % 2 and i < CHUNKS - 1:
                        dve.wait_ge(k_mult_pool, (CHUNKS - MINE) * t + i // 2 + 1)
                    else:
                        dve.wait_ge(k_mult, MINE * t + (i + 1) // 2 + 1)
                    v.tensor_reduce(s[:, CHUNK * i:CHUNK * (i + 1), :], keys[:, i % RING].rearrange("p a (c j) -> p a c j", j=DQ), AX_X, ALU.add).then_inc(k_used, 1)

                for t, with_k, with_v in turns(dve):
                    base = D_STEPS * t
                    ch.begin(t)
                    dve.wait_ge(in_loaded, 80 * (t + 1))
                    ch.done(v.tensor_tensor(cs[:, 0, :], cs[:, 0, :], w_conv[:, 0, :], ALU.mult))
                    ch.link(v.tensor_tensor(cs[:, 1, :], cs[:, 1, :], w_conv[:, 1, :], ALU.mult))
                    ch.link(v.tensor_tensor(cs[:, 0, :], cs[:, 0, :], cs[:, 1, :], ALU.add))
                    dve.wait_ge(conv23, t + 1)
                    v.tensor_tensor(cs[:, 0, :], cs[:, 0, :], cs[:, 2, :], ALU.add).then_inc(conv_ready, 1)
                    if with_k:
                        keys_times_query(t, 0)
                    gt = gate[:, bass.ds(t, 1), :].rearrange("p t (h o) -> p (t h) o", o=1)
                    bt = beta[:, bass.ds(t, 1), :].rearrange("p t (h o) -> p (t h) o", o=1)
                    ch.done(v.tensor_tensor(ug[:], bc(upper[:].rearrange("p (o j) -> p o j", o=1), *HP), bc(gt, *HP), ALU.mult))
                    v.tensor_tensor(ib[:], bc(ident[:].rearrange("p (o j) -> p o j", o=1), *HP), bc(bt, *HP), ALU.mult).then_inc(ug_ready, 1)
                    dve.wait_ge(th_ready, t + 1)
                    qk = qkv[:, 0:2, :].rearrange("p a (h j) -> p (a h) j", h=H)
                    sq = th[:, 0:2 * HW].rearrange("p (h j) -> p h j", j=P)
                    ch.link(v.scalar_tensor_tensor(qkv[:].rearrange("p a j -> p (a j)"), th[:], 1.0, cs[:, 0, :], ALU.add, ALU.mult))
                    dve.sem_inc(cs_used, 1)
                    ch.link(v.tensor_tensor(sq, qk, qk, ALU.mult))
                    ch.link(v.tensor_reduce(ss[:], sq, AX_X, ALU.add))
                    rsqrt(nc, ch, rn[:], ss[:], rt[:], 1.0, EPS)
                    ch.link(v.tensor_scalar(rn[:, 0:H], rn[:, 0:H], DK ** -0.5, None, ALU.mult))
                    v.tensor_tensor(qk, qk, bc(rn[:].rearrange("p (h o) -> p h o", o=1), P, 2 * H, P), ALU.mult).then_inc(qk_ready, 1)
                    dve.wait_ge(eg_ready, t + 1)
                    gcb = bc(gcol[:].rearrange("p (h o) -> p h o", o=1), *HP)
                    ch.done(v.tensor_tensor(glg[:].rearrange("p (h o) -> p h o", o=1), bank(1)[:, :, P - 1:P], gcol[:].rearrange("p (h o) -> p h o", o=1), ALU.subtract))
                    ch.link(v.tensor_tensor(dt[:], bank(1), gcb, ALU.subtract))
                    v.tensor_scalar(dt[:], dt[:], 0.0, None, ALU.min).then_inc(d_in, 1)
                    if with_k:
                        score(t, 0)
                        score(t, 1)
                    dve.wait_ge(d_ready, t + 1)
                    ch.link(v.tensor_tensor(dt[:], dt[:], bc(upper[:].rearrange("p (o j) -> p o j", o=1), *HP), ALU.mult))
                    idb = ident[:].rearrange("p (o j) -> p o j", o=1)
                    ch.done(v.tensor_copy(TT[:].rearrange("p a h j -> p (a h) j"), bc(idb, P, 2 * H, P)))
                    if with_k:
                        keys_times_query(t, 2)
                        score(t, 2)
                    dve.wait_ge(kk_ps, t + 1)
                    ch.done(v.tensor_tensor(qkT[:], bank(6), dt[:], ALU.mult))
                    ch.link(v.tensor_tensor(LT[:], bank(5), dt[:], ALU.mult))
                    v.tensor_tensor(LT[:], LT[:], bank(2), ALU.mult).then_inc(t_ready, 1)
                    for lev in range(7):
                        dve.wait_ge(p_ps, 7 * t + lev + 1)
                        v.tensor_tensor(prod[:], bank(7), bc(levels[:, lev:lev + 1, :], *HP), ALU.mult).then_inc(p_ready, 1)
                        if with_k:
                            score(t, lev + 3)
                        dve.wait_ge(dT_ps, 7 * t + lev + 1)
                        v.tensor_tensor(TT[:].rearrange("p a h j -> p a (h j)"), TT[:].rearrange("p a h j -> p a (h j)"), ps[:, 3:5, :], ALU.subtract).then_inc(t_ready, 1)
                        if with_k and lev % 2 == 0:
                            keys_times_query(t, lev + 4)
                    if with_k:
                        for i in range(10, CHUNKS):
                            if (i % 2 == 0 and i > 10) or i == CHUNKS - 1:
                                keys_times_query(t, i)
                            score(t, i)
                        dve.wait_ge(new_loaded, 16 * (t + 1))
                        v.tensor_tensor(kn[:], kn[:], q[:, bass.ds(t, 1), :].rearrange("p b c -> p (b c)"), ALU.mult).then_inc(dsteps, 1)
                        dve.wait_ge(dsteps, base + 1)
                        v.tensor_reduce(s[:, N_PAGES, :], kn[:].rearrange("p (c j) -> p c j", j=DQ), AX_X, ALU.add).then_inc(dsteps, 1)
                        dve.wait_ge(dsteps, base + 2)
                        v.tensor_scalar(s[:, N_PAGES, :], s[:, N_PAGES, :], first[:], None, ALU.add).then_inc(dsteps, 1)
                        dve.wait_ge(dsteps, base + 3)
                        dve.wait_ge(k_used, CHUNKS * (t + 1) + RING)
                        v.tensor_reduce(m[:], s[:].rearrange("p g c -> p c g"), AX_X, ALU.max).then_inc(m_ready, 1)
                    dve.wait_ge(o_ps, t + 1)
                    for h in range(H):
                        ch.done(v.scalar_tensor_tensor(S[:, h, :], S[:, h, :], egrow[:, h, P - 1:P], bank(3)[:, h, :], ALU.mult, ALU.add))
                    dve.wait_ge(osq_ready, t + 1)
                    ch.link(v.tensor_reduce(ss[:, 0:H], osq[:], AX_X, ALU.add))
                    rsqrt(nc, ch, rn[:, 0:H], ss[:, 0:H], rt[:, 0:H], 1.0 / DV, EPS)
                    if with_k:
                        dve.wait_ge(mx_ready, t + 1)
                        v.tensor_tensor(s[:], s[:], bc(mx[:].rearrange("p (o c) -> p o c", o=1), P, NP1, C), ALU.subtract).then_inc(s_ready, 1)
                    dve.wait_ge(on_free, t + 1)
                    ch.link(v.tensor_tensor(on[:], bank(7), bc(rn[:, 0:H].rearrange("p (h o) -> p h o", o=1), *HP), ALU.mult))
                    ch.link(v.tensor_tensor(on[:], on[:], bc(w_gn[:].rearrange("p (o j) -> p o j", o=1), *HP), ALU.mult))
                    dve.wait_ge(psteps, 6 * t + 6)
                    v.tensor_tensor(on[:].rearrange("p h j -> p (h j)"), on[:].rearrange("p h j -> p (h j)"), zs[:], ALU.mult).then_inc(on_ready, 1)
                    ch.end()
                    dve.sem_inc(zs_ready, 1)
                    if not with_k:
                        continue
                    dve.wait_ge(e_ready, t + 1)
                    v.tensor_reduce(l[:], e[:].rearrange("p g c -> p c g"), AX_X, ALU.add).then_inc(l_ready, 1)
                    dve.wait_ge(lt_ready, t + 1)
                    v.reciprocal(r[:], lt[:]).then_inc(dsteps, 1)
                    dve.wait_ge(dsteps, base + 4)
                    v.tensor_tensor(r[:].rearrange("p (h c) -> p h c", c=2), r[:].rearrange("p (h c) -> p h c", c=2), bc(coef[:].rearrange("p (o c) -> p o c", o=1), P, H, 2), ALU.mult).then_inc(dsteps, 1)
                    dve.wait_ge(dsteps, base + 5)
                    v.tensor_tensor(e[:], e[:], bc(r[:].rearrange("p (o c) -> p o c", o=1), P, NP1, C), ALU.mult).then_inc(dsteps, 1)
                    dve.wait_ge(dsteps, base + 6)
                    dve.wait_ge(pv_done, t + 1)
                    e2 = e[:].rearrange("p g (h c) -> p g h c", c=2)
                    v.tensor_tensor(w[:], e2[:, :, :, 0], e2[:, :, :, 1], ALU.add).then_inc(w_ready, 1)
                fin = Chain(dve, own("de_final"), 0)
                dve.wait_ge(od_loaded, 16)
                fin.link(v.tensor_tensor(dsq[:], od[:], od[:], ALU.mult))
                fin.link(v.tensor_reduce(s1[:], dsq[:], AX_X, ALU.add))
                rsqrt(nc, fin, r1[:], s1[:], r2[:], 1.0 / DV, EPS, times=1.0 - LAM_INIT)
                v.scalar_tensor_tensor(od[:], od[:], r1[:], w_sub[:], ALU.mult, ALU.mult).then_inc(dn_ready, 1)

            @block.tensor
            def _(pe):
                pe.wait_ge(c_loaded, 160)
                pe.sem_inc(pv_done, 1)
                pe.sem_inc(od_ready, 1)
                pe.wait_ge(pre_stored, 48)

                def weigh(t, c0, c1):
                    if c0 == 0:
                        pe.wait_ge(w_ready, t)
                        pe.wait_ge(od_ready, t)
                    for g in range(int(c0 * CHUNK), int(c1 * CHUNK)):
                        c, j = g // CHUNK, g % CHUNK
                        if j == 0:
                            pe.wait_ge(v_loaded[c % RING], 16 * (CHUNKS // RING * (t - 1) + c // RING + 1))
                        last = pe.matmul(ps[0:H, 0, :], w[:, g, :], vals[:, c % RING, j, :], start=(g == 0), stop=False)
                        if j == CHUNK - 1:
                            last.then_inc(v_used, 1)
                    if c1 == CHUNKS:
                        pe.wait_ge(vn_loaded, 16 * t)
                        pe.matmul(ps[0:H, 0, :], w[:, N_PAGES, :], vn[:], start=False, stop=True).then_inc(pv_done, 1)

                for t, with_k, with_v in turns(pe):
                    if with_v:
                        weigh(t, 0, 2)
                    pe.wait_ge(ug_ready, t + 1)
                    pe.wait_ge(gate_c, 1)
                    pe.matmul(ps[:, 5, 0:H], upper[:], gate[:, bass.ds(t, 1), :].rearrange("p t h -> p (t h)"), start=True, stop=True)
                    pe.matmul(ps[:, 1, :], ones[:], ug[:].rearrange("p h j -> p (h j)"), start=True, stop=True)
                    pe.matmul(ps[:, 2, :], ones[:], ib[:].rearrange("p h j -> p (h j)"), start=True, stop=True).then_inc(g_ps, 1)
                    if with_v:
                        weigh(t, 2, 4)
                    pe.wait_ge(qk_ready, t + 1)
                    for h in range(H):
                        pe.transpose(bank(3)[:, h, :], qkv[:, 1, h * P:(h + 1) * P], ident[:])
                    for h in range(H):
                        last = pe.transpose(bank(4)[:, h, :], qkv[:, 0, h * P:(h + 1) * P], ident[:])
                    last.then_inc(qkT_ps, 1)
                    pe.wait_ge(kqT_ready, t + 1)
                    for h in range(H):
                        pe.matmul(bank(5)[:, h, :], kT[:, h, :], kT[:, h, :], start=True, stop=True)
                    for h in range(H):
                        last = pe.matmul(bank(6)[:, h, :], kT[:, h, :], qT[:, h, :], start=True, stop=True)
                    last.then_inc(kk_ps, 1)
                    if with_v:
                        weigh(t, 4, 5)
                    for lev in range(7):
                        pe.wait_ge(t_ready, 8 * t + lev + 1)
                        for h in range(H):
                            last = pe.matmul(bank(7)[:, h, :], LT[:, h, :], TT[:, 0, h, :], start=True, stop=True)
                        last.then_inc(p_ps, 1)
                        if with_v:
                            weigh(t, 5 + lev, 5.5 + lev)
                        pe.wait_ge(p_ready, 7 * t + lev + 1)
                        for h in range(H):
                            pe.matmul(bank(3)[:, h, :], TT[:, 1, h, :], prod[:, h, :], start=True, stop=True)
                            last = pe.matmul(bank(4)[:, h, :], prod[:, h, :], TT[:, 1, h, :], start=True, stop=True)
                        last.then_inc(dT_ps, 1)
                        if with_v:
                            weigh(t, 5.5 + lev, 6 + lev)
                    pe.wait_ge(t_ready, 8 * t + 8)
                    pe.wait_ge(operands, t + 1)
                    for h in range(H):
                        last = pe.matmul(bank(6)[:, h, :], kbg[:, h, :], TT[:, 1, h, :], start=True, stop=True)
                    last.then_inc(w_ps, 1)
                    if with_v:
                        weigh(t, 12, 12.5)
                    pe.wait_ge(nw_ready, t + 1)
                    for h in range(H):
                        pe.matmul(bank(5)[:, h, :], TT[:, 1, h, :], vb[:, h, :], start=True, stop=False)
                        last = pe.matmul(bank(5)[:, h, :], nwT[:, h, :], S[:, h, :], start=False, stop=True)
                    last.then_inc(u_ps, 1)
                    for h in range(H):
                        pe.matmul(bank(7)[:, h, :], qgT[:, h, :], S[:, h, :], start=True, stop=False)
                        if h == 0:
                            pe.wait_ge(u_ready, t + 1)
                        pe.matmul(bank(7)[:, h, :], qkT[:, h, :], u[:, h, :], start=False, stop=True)
                    for h in range(H):
                        last = pe.matmul(bank(3)[:, h, :], kw[:, h, :], u[:, h, :], start=True, stop=True)
                    last.then_inc(o_ps, 1)
                    if with_v:
                        weigh(t, 12.5, CHUNKS)


DVE_GDN_STEPS = 45
D_STEPS = 6


def phase_sample_gdn(nc, ps, A, keep):
    N = BS * H
    with ExitStack() as ctx, own_semaphores(nc) as own:
        def sb(n, s, d=F32):
            return ctx.enter_context(nc.sbuf_tensor("sg_" + n, s, d))

        def sem(n):
            return own("sg_" + n)

        ident, ones = sb("ident", [P, P]), sb("ones", [P, P])
        state = sb("state", [P, N, DV])
        taps, w_conv = sb("taps", [BS, CONV_W, CONV_CH]), sb("w_conv", [BS, CONV_W, CONV_CH])
        th, qkv, sq = sb("th", [BS, CONV_CH]), sb("qkv", [BS, 3, H * DK]), sb("sq", [BS, 8, DK])
        ss, rn, rt = sb("ss", [BS, 8]), sb("rn", [BS, 8]), sb("rt", [BS, 8])
        z, zt, w_gn = sb("z", [N, DV]), sb("zt", [N, DV]), sb("w_gn", [N, DV])
        gate, beta, eg = sb("gate", [N, 1]), sb("beta", [N, 1]), sb("eg", [N, 1])
        rows = sb("rows", [N, 3, DK])
        kT, qT = sb("kT", [P, N]), sb("qT", [P, N])
        diag, eb = sb("diag", [N, N]), sb("eb", [P, N])
        colT, u, spread = sb("colT", [P, N]), sb("u", [N, DV]), sb("spread", [N, N, DV])
        o, osq = sb("o", [N, DV]), sb("osq", [N, DV])
        s1, r1, r2 = sb("s1", [N, 1]), sb("r1", [N, 1]), sb("r2", [N, 1])
        loaded, rows_out, rows_in = sem("loaded"), sem("rows_out"), sem("rows_in")
        steps, conv_ready, th_ready, qkv_ready = sem("steps"), sem("conv_ready"), sem("th_ready"), sem("qkv_ready")
        eg_ready, zt_ready, diag_ready = sem("eg_ready"), sem("zt_ready"), sem("diag_ready")
        turned, turned_sb, ks_ps, ks_sb, ks_row = sem("turned"), sem("turned_sb"), sem("ks_ps"), sem("ks_sb"), sem("ks_row")
        u_ready, outer, state_ready = sem("u_ready"), sem("outer"), sem("state_ready")
        qs_ps, qs_sb, qs_row, o_ready, stored = sem("qs_ps"), sem("qs_sb"), sem("qs_row"), sem("o_ready"), sem("stored")
        row0 = CONV_W - 1 + LP

        with nc.Block() as block:
            @block.sync
            def _(sp):
                n = 0
                for dst, src in [(taps[:, 0:CONV_W - 1, :], A["state_conv"]),
                                 (taps[:, CONV_W - 1, :], A["proj"][row0:row0 + BS, 0:CONV_CH]),
                                 (w_conv[:].rearrange("p i c -> p (i c)"), A["w_conv"].rearrange("i c -> (i c)").partition_broadcast(BS)),
                                 (gate[:], A["gates_s"][0].rearrange("b (h o) -> (b h) o", o=1)),
                                 (beta[:], A["gates_s"][1].rearrange("b (h o) -> (b h) o", o=1)),
                                 (w_gn[:], A["w_gnorm"].partition_broadcast(N)),
                                 (ident[:], A["ident"]), (ones[:], A["ones"])]:
                    sp.dma_start(dst, src).then_inc(loaded, 16)
                for b in range(BS):
                    sp.dma_start(z[b * H:(b + 1) * H, :], A["proj"][row0 + b, C_Z:C_Z + H * DV].rearrange("(h j) -> h j", h=H)).then_inc(loaded, 16)
                sp.dma_start(state[:], A["state_gdn"].rearrange("i k v -> k i v")).then_inc(loaded, 16)
                sp.dma_start(A["s_conv"][:, 0:CONV_W - 2, :], A["state_conv"][:, 1:CONV_W - 1, :]).then_inc(stored, 16)
                sp.dma_start(A["s_conv"][:, CONV_W - 2, :], A["proj"][row0:row0 + BS, 0:CONV_CH]).then_inc(stored, 16)
                sp.dma_start(A["p_conv"], A["proj"][row0 - (CONV_W - 1):row0, 0:CONV_CH]).then_inc(stored, 16)
                sp.wait_ge(qkv_ready, 2)
                sp.dma_start(A["rows_s"].rearrange("a b c -> b a c"), qkv[:]).then_inc(rows_out, 16)
                sp.wait_ge(rows_out, 16)
                sp.dma_start(rows[:], A["rows_s"].rearrange("a b (h j) -> (b h) a j", h=H)).then_inc(rows_in, 16)
                sp.wait_ge(state_ready, 1)
                sp.dma_start(A["s_gdn"].rearrange("i k v -> k i v"), state[:]).then_inc(stored, 16)
                sp.wait_ge(o_ready, 1)
                for b in range(BS):
                    sp.dma_start(A["mix"][LP + b, 0:H * DV].rearrange("(h j) -> h j", h=H), o[b * H:(b + 1) * H, :]).then_inc(stored, 16)
                sp.wait_ge(stored, 16 * (4 + BS))

            @block.scalar
            def _(act):
                act.wait_ge(loaded, 16 * (9 + BS))
                act.activation(eg[:], gate[:], ACT.Exp).then_inc(eg_ready, 1)
                act.activation(zt[:], z[:], ACT.Tanh, scale=0.5).then_inc(zt_ready, 1)
                act.wait_ge(conv_ready, 1)
                act.activation(th[:], taps[:, 0, :], ACT.Tanh).then_inc(th_ready, 1)
                act.wait_ge(turned, 1)
                act.activation(kT[:], ps[:, 0, 0:N], ACT.Copy).then_inc(turned_sb, 1)
                act.activation(qT[:], ps[:, 1, 0:N], ACT.Copy).then_inc(turned_sb, 1)
                act.wait_ge(diag_ready, 2)
                act.activation(eb[:], ps[:, 2, 0:N], ACT.Copy).then_inc(turned_sb, 1)
                act.wait_ge(ks_ps, 1)
                act.activation(colT[:], ps[:, 3, 0:N], ACT.Copy).then_inc(ks_sb, 1)
                act.wait_ge(qs_ps, 1)
                act.activation(colT[:], ps[:, 0, 0:N], ACT.Copy).then_inc(qs_sb, 1)

            @block.vector
            def _(dve):
                v = nc.vector
                ch = Chain(dve, steps, 0)
                dve.wait_ge(loaded, 16 * (9 + BS))
                ch.link(v.tensor_scalar(w_conv[:], w_conv[:], 0.5, None, ALU.mult))
                ch.link(v.tensor_tensor(taps[:], taps[:], w_conv[:], ALU.mult))
                ch.link(v.tensor_tensor(taps[:, 0:2, :], taps[:, 0:2, :], taps[:, 2:4, :], ALU.add))
                v.tensor_tensor(taps[:, 0, :], taps[:, 0, :], taps[:, 1, :], ALU.add).then_inc(conv_ready, 1)
                dve.wait_ge(th_ready, 1)
                v.scalar_tensor_tensor(qkv[:].rearrange("p a j -> p (a j)"), th[:], 1.0, taps[:, 0, :], ALU.add, ALU.mult).then_inc(qkv_ready, 1)
                dve.wait_ge(qkv_ready, 1)
                qk = qkv[:, 0:2, :].rearrange("p a (h j) -> p (a h) j", h=H)
                ch.link(v.tensor_tensor(sq[:], qk, qk, ALU.mult))
                ch.link(v.tensor_reduce(ss[:], sq[:], AX_X, ALU.add))
                rsqrt(nc, ch, rn[:], ss[:], rt[:], 1.0, EPS)
                ch.link(v.tensor_scalar(rn[:, 0:H], rn[:, 0:H], DK ** -0.5, None, ALU.mult))
                v.tensor_tensor(qk, qk, bc(rn[:].rearrange("p (h o) -> p h o", o=1), BS, 2 * H, DK), ALU.mult).then_inc(qkv_ready, 1)
                dve.wait_ge(eg_ready, 1)
                v.tensor_scalar(diag[:], ident[0:N, 0:N], eg[:], None, ALU.mult).then_inc(diag_ready, 1)
                dve.wait_ge(ks_row, 1)
                ch.link(v.tensor_scalar(u[:], ps[0:N, 4, 0:DV], eg[:], None, ALU.mult))
                ch.link(v.tensor_tensor(u[:], rows[:, 2, :], u[:], ALU.subtract))
                ch.link(v.tensor_scalar(u[:], u[:], beta[:], None, ALU.mult))
                v.tensor_tensor(spread[:], bc(ident[0:N, 0:N].rearrange("p (i o) -> p i o", o=1), N, N, DV),
                                bc(u[:].rearrange("p (o j) -> p o j", o=1), N, N, DV), ALU.mult).then_inc(u_ready, 1)
                dve.wait_ge(turned_sb, 3)
                ch.link(v.tensor_tensor(state[:], state[:], bc(eb[:].rearrange("p (i o) -> p i o", o=1), P, N, DV), ALU.mult))
                dve.wait_ge(outer, 1)
                v.tensor_tensor(state[:].rearrange("p (c i) j -> p c (i j)", c=8), state[:].rearrange("p (c i) j -> p c (i j)", c=8), ps[:, :, :], ALU.add).then_inc(state_ready, 1)
                ch.link(v.tensor_scalar(zt[:], zt[:], 1.0, None, ALU.add))
                ch.link(v.tensor_tensor(zt[:], zt[:], z[:], ALU.mult))
                ch.link(v.tensor_tensor(zt[:], zt[:], w_gn[:], ALU.mult))
                dve.wait_ge(qs_row, 1)
                ch.link(v.tensor_copy(o[:], ps[0:N, 1, 0:DV]))
                ch.link(v.tensor_tensor(osq[:], o[:], o[:], ALU.mult))
                ch.link(v.tensor_reduce(s1[:], osq[:], AX_X, ALU.add))
                rsqrt(nc, ch, r1[:], s1[:], r2[:], 1.0 / DV, EPS, times=0.5)
                v.scalar_tensor_tensor(o[:], o[:], r1[:], zt[:], ALU.mult, ALU.mult).then_inc(o_ready, 1)

            @block.tensor
            def _(pe):
                pe.wait_ge(loaded, 16 * (9 + BS))
                pe.wait_ge(rows_in, 16)
                pe.transpose(ps[:, 0, 0:N], rows[:, 1, :], ident[0:N, 0:N])
                pe.transpose(ps[:, 1, 0:N], rows[:, 0, :], ident[0:N, 0:N]).then_inc(turned, 1)
                pe.wait_ge(diag_ready, 1)
                pe.matmul(ps[:, 2, 0:N], ones[0:N, :], diag[:], start=True, stop=True).then_inc(diag_ready, 1)
                pe.wait_ge(turned_sb, 1)
                for i in range(N):
                    last = pe.matmul(ps[:, 3, i:i + 1], state[:, i, :], kT[:, i:i + 1], start=True, stop=True)
                last.then_inc(ks_ps, 1)
                pe.wait_ge(ks_sb, 1)
                pe.transpose(ps[0:N, 4, 0:P], colT[:], ident[:]).then_inc(ks_row, 1)
                pe.wait_ge(u_ready, 1)
                pe.wait_ge(turned_sb, 3)
                for c in range(8):
                    last = pe.matmul(ps[:, c, :], rows[:, 1, :], spread[:, 4 * c:4 * c + 4, :].rearrange("p i j -> p (i j)"), start=True, stop=True)
                last.then_inc(outer, 1)
                pe.wait_ge(state_ready, 1)
                for i in range(N):
                    last = pe.matmul(ps[:, 0, i:i + 1], state[:, i, :], qT[:, i:i + 1], start=True, stop=True)
                last.then_inc(qs_ps, 1)
                pe.wait_ge(qs_sb, 1)
                pe.transpose(ps[0:N, 1, 0:P], colT[:], ident[:]).then_inc(qs_row, 1)


ATT_STEPS = 15


def phase_attention(nc, ps, A, keep):
    with ExitStack() as ctx, own_semaphores(nc) as own:
        def sb(n, s, d=F32):
            return ctx.enter_context(nc.sbuf_tensor("at_" + n, s, d))

        def sem(n):
            return own("at_" + n)

        HW = H * DV
        ident, causal = sb("ident", [P, P]), sb("causal", [P, P])
        qk = sb("qk", [P, TILES, 2 * HW])
        vals = sb("vals", [P, TILES, HW])
        cos, sin = sb("cos", [P, TILES, HALF]), sb("sin", [P, TILES, HALF])
        rot = sb("rot", [P, 4, TILES, 16, HALF])
        coef = sb("coef", [P, 2])
        w_sub = sb("w_sub", [P, DV])
        KT, qT = sb("KT", [P, H, RPAD]), sb("qT", [P, H, RPAD])
        prob, w = sb("prob", [P, 2, RPAD]), sb("w", [P, 2, RPAD])
        wT = sb("wT", [P, 2, 4 * P])
        nmax, sums, rcp = sb("nmax", [P, 2]), sb("sums", [P, 2]), sb("rcp", [P, 2])
        av, osq, ao = sb("av", [P, H, DV]), sb("osq", [P, H, DV]), sb("ao", [P, 2, H, DV])
        ss, rn, rt = sb("ss", [P, H]), sb("rn", [P, H]), sb("rt", [P, H])
        loaded, steps, rot_ready = sem("loaded"), sem("steps"), sem("rot_ready")
        kq_ps, kT_ready, qT_ready, v_loaded = sem("kq_ps"), sem("kT_ready"), sem("qT_ready"), sem("v_loaded")
        s_ps, max_ready, e_ready, w_ready = sem("s_ps"), sem("max_ready"), sem("e_ready"), sem("w_ready")
        av_copied = sem("av_copied")
        wT_ps, wT_ready, av_ps, osq_ready = sem("wT_ps"), sem("wT_ready"), sem("av_ps"), sem("osq_ready")
        ao_ready, ao_stored, stored = sem("ao_ready"), [sem("ao_stored0"), sem("ao_stored1")], sem("stored")
        flat = ps[:].rearrange("p b j -> p (b j)")
        units = [(t, h) for t in range(TILES) for h in range(H)]
        groups = [[(j, min(j + 4, t + 1)) for j in range(0, t + 1, 4)] for t, h in units]
        group_no = [sum(len(g) for g in groups[:n]) for n in range(len(units))]

        def turn_banks(t):
            return 2 * (t % 4)

        def score_columns(c, k0, k1):
            return flat[:, c * 1536 + k0:c * 1536 + k1]

        last_tile = TILES - 1
        tail = LP - last_tile * P

        with nc.Block() as block:
            @block.sync
            def _(sp):
                rows = A["proj"][CONV_W - 1:CONV_W - 1 + RPAD, :].rearrange("(t p) c -> p t c", p=P)
                for dst, src in [(qk[:], rows[:, :, C_DQ:C_DQ + 2 * HW]), (ident[:], A["ident"]), (causal[:], A["causal"]), (cos[:], A["cos"]), (sin[:], A["sin"]),
                                 (w_sub[:], A["w_subln"].partition_broadcast(P)), (coef[:], A["coef"])]:
                    sp.dma_start(dst, src).then_inc(loaded, 16)
                sp.dma_start(vals[:], rows[:, :, C_DV:C_DV + HW]).then_inc(v_loaded, 16)
                sp.wait_ge(loaded, 16 * 7)
                sp.wait_ge(v_loaded, 16)
                sp.wait_ge(rot_ready, 1)
                for dst, src in [(A["p_k"][0:last_tile * P, :].rearrange("(t p) c -> p t c", p=P), qk[:, 0:last_tile, HW:2 * HW]),
                                 (A["p_v"][0:last_tile * P, :].rearrange("(t p) c -> p t c", p=P), vals[:, 0:last_tile, :]),
                                 (A["p_k"][last_tile * P:LP, :], qk[0:tail, last_tile, HW:2 * HW]),
                                 (A["p_v"][last_tile * P:LP, :], vals[0:tail, last_tile, :])]:
                    sp.dma_start(dst, src).then_inc(stored, 16)
                for t in range(TILES):
                    sp.wait_ge(ao_ready, t + 1)
                    for r0, r1 in ((0, P),) if t < last_tile else ((0, tail), (tail + BS, P)):
                        sp.dma_start(A["mix"][t * P + r0:t * P + r1, HW:2 * HW], ao[r0:r1, t % 2, :, :].rearrange("p h j -> p (h j)")).then_inc(ao_stored[t % 2], 16)
                sp.wait_ge(ao_stored[0], 16 * ((TILES + 1) // 2 + 1))
                sp.wait_ge(ao_stored[1], 16 * (TILES // 2))
                sp.wait_ge(stored, 16 * 4)

            @block.scalar
            def _(act):
                act.wait_ge(loaded, 16 * 7)

                def exp(n, c):
                    t, h = units[n]
                    wd = (t + 1) * P
                    act.wait_ge(max_ready, 2 * n + c + 1)
                    if n:
                        act.wait_ge(w_ready, n)
                    act.activation(prob[:, c, 0:wd], score_columns(c, 0, wd), ACT.Exp, bias=nmax[:, c:c + 1],
                                   accum_out=sums[:, c:c + 1]).then_inc(e_ready, 1)

                for t in range(TILES):
                    act.wait_ge(kq_ps, t + 1)
                    act.activation(KT[:, :, t * P:(t + 1) * P], ps[:, turn_banks(t), :].rearrange("p (h j) -> p h j", h=H), ACT.Copy).then_inc(kT_ready, 1)
                for n in range(-1, len(units)):
                    for i in range(max(2, len(groups[n])) if n >= 0 else 2):
                        if n >= 0 and i < len(groups[n]):
                            g = group_no[n] + i
                            j0, j1 = groups[n][i]
                            act.wait_ge(wT_ps, g + 1)
                            act.activation(wT[:, g % 2, 0:(j1 - j0) * P], ps[:, 6, 0:(j1 - j0) * P], ACT.Copy).then_inc(wT_ready, 1)
                        if i < 2 and n + 1 < len(units):
                            exp(n + 1, i)
                    if n >= 0 and units[n][1] == H - 1:
                        t = units[n][0]
                        act.wait_ge(av_ps, n + 1)
                        if t:
                            act.wait_ge(ao_ready, t)
                        act.activation(av[:], ps[:, 7, :].rearrange("p (h j) -> p h j", h=H), ACT.Copy).then_inc(av_copied, 1)
                        act.wait_ge(av_copied, t + 1)
                        act.activation(osq[:], av[:], ACT.Square).then_inc(osq_ready, 1)

            @block.vector
            def _(dve):
                v = nc.vector
                ch = Chain(dve, steps, 0)
                dve.wait_ge(loaded, 16 * 7)
                x = qk[:].rearrange("p t (c j) -> p t c j", j=DQ)
                x1, x2 = x[:, :, :, 0:HALF], x[:, :, :, HALF:2 * HALF]
                sh = (P, TILES, 16, HALF)
                cb, sb_ = (bc(a[:].rearrange("p t (o j) -> p t o j", o=1), *sh) for a in (cos, sin))
                ch.done(v.tensor_tensor(rot[:, 0], x1, cb, ALU.mult))
                ch.done(v.tensor_tensor(rot[:, 1], x2, sb_, ALU.mult))
                ch.done(v.tensor_tensor(rot[:, 2], x2, cb, ALU.mult))
                ch.link(v.tensor_tensor(rot[:, 3], x1, sb_, ALU.mult))
                ch.done(v.tensor_tensor(x1, rot[:, 0], rot[:, 1], ALU.subtract))
                v.tensor_tensor(x2, rot[:, 2], rot[:, 3], ALU.add).then_inc(rot_ready, 1)

                for t in range(TILES):
                    dve.wait_ge(kq_ps, t + 1)
                    v.tensor_scalar(qT[:, :, t * P:(t + 1) * P], ps[:, turn_banks(t) + 1, :].rearrange("p (h j) -> p h j", h=H), DQ ** -0.5, None, ALU.mult).then_inc(qT_ready, 1)

                def maximum(n, c):
                    t, h = units[n]
                    dve.wait_ge(s_ps, 2 * n + c + 1)
                    v.tensor_reduce(nmax[:, c:c + 1], score_columns(c, 0, (t + 1) * P), AX_X, ALU.max, negate=True).then_inc(max_ready, 1)

                def weights(n):
                    wd = (units[n][0] + 1) * P
                    dve.wait_ge(e_ready, 2 * n + 2)
                    ch.link(v.reciprocal(rcp[:], sums[:]))
                    ch.link(v.tensor_tensor(rcp[:], rcp[:], coef[:], ALU.mult))
                    if n >= 2:
                        dve.wait_ge(wT_ps, group_no[n - 1])
                    ch.link(v.tensor_scalar(w[:, n % 2, 0:wd], prob[:, 1, 0:wd], rcp[:, 1:2], None, ALU.mult))
                    v.scalar_tensor_tensor(w[:, n % 2, 0:wd], prob[:, 0, 0:wd], rcp[:, 0:1], w[:, n % 2, 0:wd], ALU.mult, ALU.add).then_inc(w_ready, 1)

                def norm(t):
                    dve.wait_ge(osq_ready, t + 1)
                    ch.link(v.tensor_reduce(ss[:], osq[:], AX_X, ALU.add))
                    rsqrt(nc, ch, rn[:], ss[:], rt[:], 1.0 / DV, EPS, times=1.0 - LAM_INIT)
                    if t >= 2:
                        dve.wait_ge(ao_stored[t % 2], 16 * (t // 2))
                    ch.link(v.tensor_tensor(ao[:, t % 2], av[:], bc(rn[:].rearrange("p (h o) -> p h o", o=1), P, H, DV), ALU.mult))
                    v.tensor_tensor(ao[:, t % 2], ao[:, t % 2], bc(w_sub[:].rearrange("p (o j) -> p o j", o=1), P, H, DV), ALU.mult).then_inc(ao_ready, 1)

                for c in range(2):
                    maximum(0, c)
                for n, (t, h) in enumerate(units):
                    weights(n)
                    if n + 1 < len(units):
                        for c in range(2):
                            maximum(n + 1, c)
                    if h == 0 and t:
                        norm(t - 1)
                norm(last_tile)

            @block.tensor
            def _(pe):
                pe.wait_ge(loaded, 16 * 7)
                pe.wait_ge(rot_ready, 1)

                for t in range(TILES):
                    if t >= 4:
                        pe.wait_ge(kT_ready, t - 3)
                        pe.wait_ge(qT_ready, t - 3)
                    for i, o in enumerate((HW, 0)):
                        for h in range(H):
                            last = pe.transpose(ps[:, turn_banks(t) + i, h * P:(h + 1) * P], qk[:, t, o + h * P:o + (h + 1) * P], ident[:])
                    last.then_inc(kq_ps, 1)
                pe.wait_ge(kT_ready, TILES)
                pe.wait_ge(qT_ready, TILES)

                def scores(n, c):
                    t, h = units[n]
                    wd = (t + 1) * P
                    if n:
                        pe.wait_ge(e_ready, 2 * n + c - 1)
                    q = qT[DQ * c:DQ * (c + 1), h, t * P:(t + 1) * P]
                    for k0 in range(0, wd, 512):
                        k1 = min(k0 + 512, wd)
                        pe.matmul(score_columns(c, k0, k1), q, KT[DQ * c:DQ * (c + 1), h, k0:k1], start=True, stop=k1 != wd, skip_group_check=True)
                    pe.matmul(score_columns(c, wd - P, wd), ident[:], causal[:], start=False, stop=True, skip_group_check=True).then_inc(s_ps, 1)

                def turn_weights(n, i):
                    j0, j1 = groups[n][i]
                    g = group_no[n] + i
                    if g:
                        pe.wait_ge(wT_ready, g)
                    for j in range(j0, j1):
                        last = pe.transpose(ps[:, 6, (j - j0) * P:(j - j0 + 1) * P], w[:, n % 2, j * P:(j + 1) * P], ident[:])
                    last.then_inc(wT_ps, 1)

                def weigh(n, i):
                    (t, h), (j0, j1) = units[n], groups[n][i]
                    g = group_no[n] + i
                    pe.wait_ge(wT_ready, g + 1)
                    if h == 0 and i == 0 and t:
                        pe.wait_ge(av_copied, t)
                    for j in range(j0, j1):
                        last = pe.matmul(ps[:, 7, h * P:(h + 1) * P], wT[:, g % 2, (j - j0) * P:(j - j0 + 1) * P], vals[:, j, h * DV:(h + 1) * DV],
                                         start=(j == 0), stop=(j == t))
                    if j1 == t + 1:
                        last.then_inc(av_ps, 1)

                for c in range(2):
                    scores(0, c)
                pe.wait_ge(v_loaded, 16)
                for n in range(len(units)):
                    if n + 1 < len(units):
                        scores(n + 1, 0)
                    pe.wait_ge(w_ready, n + 1)
                    turn_weights(n, 0)
                    if n + 1 < len(units):
                        scores(n + 1, 1)
                    for i in range(len(groups[n])):
                        if i + 1 < len(groups[n]):
                            turn_weights(n, i + 1)
                        weigh(n, i)




def phase_mix(nc, ps, A, keep):
    with ExitStack() as ctx, own_semaphores(nc) as own:
        def sb(n, s, d=F32):
            return ctx.enter_context(nc.sbuf_tensor("mx_" + n, s, d))

        def sem(n):
            return own("mx_" + n)

        def kept(n):
            return keep.enter_context(nc.semaphore("mx_" + n))

        NL = G + NE
        ident, ones, strict = sb("ident", [P, P]), sb("ones", [P, P]), sb("strict", [P, P])
        w_out, w_r, w_norm = sb("w_out", [P, KD, D]), sb("w_r", [P, KD, NL]), sb("w_norm", [P, D])
        x, mix = sb("x", [P, 2, D]), sb("mix", [P, 2, D])
        mixT, hnT = sb("mixT", [P, D]), sb("hnT", [P, D])
        x2, hn, squares = sb("x2", [P, 2, D]), sb("hn", [P, 2, D]), sb("squares", [P, D])
        sq, rs = sb("sq", [P, 1]), sb("rs", [P, 2])
        valid, dump, tok = sb("valid", [P, TILES]), sb("dump", [P, TILES, 2]), sb("tok", [P, TILES], I32)
        e_no, e_group = sb("e_no", [P, NE]), sb("e_group", [P, NE])
        lg, le, geq = sb("lg", [P, 8]), sb("le", [P, NE]), sb("geq", [P, NE])
        g8, gi8, e8, ei8 = sb("g8", [P, 8]), sb("gi8", [P, 8], U32), sb("e8", [P, 8]), sb("ei8", [P, 8], U32)
        gi, ei, ngm, gx, gs, gw = sb("gi", [P, 1]), sb("ei", [P, 2]), sb("ngm", [P, 1]), sb("gx", [P, G]), sb("gs", [P, 1]), sb("gw", [P, 1])
        dd, ex, pp = sb("dd", [P, 1]), sb("ex", [P, 1]), sb("pp", [P, 2])
        oh, wt = sb("oh", [P, TILES, 2, NE]), sb("wt", [P, TILES, 2])
        both, pre, rank = sb("both", [P, TILES, NE]), sb("pre", [P, TILES + 1, NE]), sb("rank", [P, TILES, NE])
        cnt, cnt_i, ntile, inc, inc2 = sb("cnt", [P, NE]), sb("cnt_i", [P, NE], I32), sb("ntile", [P, NE]), sb("inc", [P, NE]), sb("inc2", [P, NE])
        pick, slot, slot_i = sb("pick", [P, TILES, 2, NE]), sb("slot", [P, TILES, 2]), sb("slot_i", [P, TILES, 2], I32)
        slot_c = sb("slot_c", [P, TILES, 2], I32)
        tile_no, le_cmp, ownr, own_i = sb("tile_no", [1, SLOT_TILES]), sb("le_cmp", [1, SLOT_TILES, NE]), sb("own", [1, SLOT_TILES]), sb("own_i", [1, SLOT_TILES], I32)

        loaded = sem("loaded")
        in_loaded = [sem("in_loaded0"), sem("in_loaded1")]
        steps, waited = sem("steps"), sem("waited")
        mixT_ps, mixT_ready, x2_ps, x2_ready = sem("mixT_ps"), sem("mixT_ready"), sem("x2_ps"), sem("x2_ready")
        sq_ready, hn_ready, hnT_ps, hnT_ready, lg_ps = sem("sq_ready"), sem("hn_ready"), sem("hnT_ps"), sem("hnT_ready"), sem("lg_ps")
        g_in, g_out, tile_done = sem("g_in"), sem("g_out"), sem("tile_done")
        x2_stored, out_free = kept("x2_stored"), sem("out_free")
        pre_ready, rank_ps, slots_ready, scattered = sem("pre_ready"), sem("rank_ps"), sem("slots_ready"), kept("scattered")
        own_ready, stored = sem("own_ready"), sem("stored")
        norm_steps, lg_read = sem("norm_steps"), sem("lg_read")
        NC = 14

        def ahead(eng):
            yield from tiles(eng, TILES - 2)
            yield TILES - 2, 1, (TILES - 2) // 2
            yield TILES - 1, 0, (TILES - 1) // 2

        def more(t, n):
            return not isinstance(t, int) or t + n < TILES


        with nc.Block() as block:
            @block.sync
            def _(sp):
                consts = [(ident[:], A["ident"]), (ones[:], A["ones"]), (strict[:], A["strict"]),
                          (w_out[:], A["w_out"].rearrange("(c p) n -> p c n", p=P)),
                          (w_r[:, :, 0:G], A["w_group"].rearrange("(c p) n -> p c n", p=P)),
                          (w_r[:, :, G:NL], A["w_expert"].rearrange("(c p) n -> p c n", p=P)),
                          (w_norm[:], A["w_norm_ffn"].partition_broadcast(P)), (valid[:], A["valid"]), (dump[:], A["dump"]),
                          (tok[:], A["tok"]), (e_no[:], A["e_no"]), (e_group[:], A["e_group"]), (tile_no[:], A["tile_no"]),
                          (A["slot_tok"], A["slot_fill"])]
                assert len(consts) == NC
                for dst, src in consts:
                    sp.dma_start(dst, src).then_inc(loaded, 16)
                def load(t, par):
                    sp.dma_start(x[:, par, :], A["x"][bass.ds(t * P, P), :]).then_inc(in_loaded[par], 16)
                    sp.dma_start(mix[:, par, :], A["mix"][bass.ds(t * P, P), :]).then_inc(in_loaded[par], 16)

                load(0, 0)
                load(1, 1)
                for t, par, k in tiles(sp, TILES - 2):
                    sp.wait_ge(x2_ready, t + 1)
                    load(t + 2, par)
                sp.wait_ge(slots_ready, 2)
                sp.dma_start(A["slots"], slot_c[:].rearrange("p t c -> p (t c)")).then_inc(stored, 16)
                sp.dma_start(A["weights"], wt[:].rearrange("p t c -> p (t c)")).then_inc(stored, 16)
                sp.wait_ge(own_ready, 1)
                sp.dma_start(A["owner"], own_i[:]).then_inc(stored, 16)
                sp.wait_ge(stored, 48)

            @block.gpsimd
            def _(pool):
                pool.sem_inc(out_free, 2)
                for t, par, k in tiles(pool):
                    if not isinstance(t, int):
                        pool.wait_ge(x2_stored, 32 * t)
                        pool.sem_inc(out_free, 1)
                    pool.wait_ge(hn_ready, t + 1)
                    pool.dma_start(A["x2"][bass.ds(t * P, P), :], x2[:, par, :]).then_inc(x2_stored, 16)
                    pool.dma_start(A["hn"][bass.ds(t * P, P), :], hn[:, par, :]).then_inc(x2_stored, 16)
                pool.wait_ge(x2_stored, 32 * TILES)
                pool.wait_ge(slots_ready, 2)
                for t in range(TILES):
                    for c in range(2):
                        pool.indirect_dma_start(out=A["slot_tok"], out_offset=bass.IndirectOffsetOnAxis(ap=slot_i[:, t, c:c + 1], axis=0),
                                                in_=tok[:, t:t + 1], in_offset=None).then_inc(scattered, 16)
                pool.wait_ge(scattered, 32 * TILES)

            @block.scalar
            def _(act):
                def copy_mixT(t):
                    act.wait_ge(mixT_ps, t + 1)
                    act.activation(mixT[:].rearrange("p (a b) -> p a b", a=2), ps[:, 0:2, :], ACT.Copy).then_inc(mixT_ready, 1)

                def square(t, par):
                    act.wait_ge(x2_ready, t + 1)
                    act.activation(squares[:], x2[:, par, :], ACT.Square, accum_out=sq[:]).then_inc(sq_ready, 1)

                copy_mixT(0)
                copy_mixT(1)
                square(0, 0)
                for t, par, k in ahead(act):
                    if more(t, 1):
                        square(t + 1, 1 - par)
                    act.wait_ge(hnT_ps, t + 1)
                    act.activation(hnT[:].rearrange("p (a b) -> p a b", a=2), ps[:, 4:6, :], ACT.Copy).then_inc(hnT_ready, 1)
                    if more(t, 2):
                        copy_mixT(t + 2)
                    act.wait_ge(g_in, 2 * t + 1)
                    act.activation(gx[:], lg[:, 0:G], ACT.Exp, bias=ngm[:], accum_out=gs[:]).then_inc(g_out, 1)
                    act.wait_ge(g_in, 2 * t + 2)
                    act.activation(ex[:], dd[:], ACT.Exp).then_inc(g_out, 1)

            @block.vector
            def _(dve):
                v = nc.vector
                norm_ch, ch = Chain(dve, norm_steps, RSQRT_STEPS), Chain(dve, steps, MIX_STEPS)
                pre_ch = Chain(dve, own("mx_pre_steps"), 0)
                dve.wait_ge(loaded, 16 * NC)
                pre_ch.link(v.memset(lg[:], -BIG))

                def residual_and_norm(t, par, k):
                    norm_ch.begin(t)
                    dve.wait_ge(in_loaded[par], 32 * (k + 1))
                    dve.wait_ge(x2_ps, t + 1)
                    dve.wait_ge(out_free, t + 1)
                    v.tensor_tensor(x2[:, par, :].rearrange("p (a b) -> p a b", a=2), x[:, par, :].rearrange("p (a b) -> p a b", a=2), ps[:, 2:4, :], ALU.add).then_inc(x2_ready, 1)
                    dve.wait_ge(sq_ready, t + 1)
                    rsqrt(nc, norm_ch, rs[:, 0:1], sq[:], rs[:, 1:2], 1.0 / D, EPS)
                    norm_ch.end()
                    v.scalar_tensor_tensor(hn[:, par, :], x2[:, par, :], rs[:, 0:1], w_norm[:], ALU.mult, ALU.mult).then_inc(hn_ready, 1)

                residual_and_norm(0, 0, 0)
                for t, par, k in ahead(dve):
                    if more(t, 1):
                        residual_and_norm(t + 1, 1 - par, k + par)
                    ch.begin(t)
                    dve.wait_ge(lg_ps, t + 1)
                    ch.link(v.tensor_copy(lg[:, 0:G], ps[:, 6, 0:G]))
                    dve.sem_inc(waited, 1)
                    ch.link(v.max(g8[:], lg[:]))
                    v.tensor_scalar(ngm[:], g8[:, 0:1], -1.0, None, ALU.mult).then_inc(g_in, 1)
                    ch.link(v.max_index(gi8[:], g8[:], lg[:]))
                    ch.link(v.tensor_copy(gi[:], gi8[:, 0:1]))
                    ch.link(v.tensor_scalar(geq[:], e_group[:], gi[:], None, ALU.is_equal))
                    ch.link(v.tensor_scalar(geq[:], geq[:], -1.0, BIG, ALU.add, ALU.mult))
                    ch.link(v.tensor_tensor(le[:], ps[:, 6, G:NL], geq[:], ALU.add))
                    dve.sem_inc(lg_read, 1)
                    dve.sem_inc(waited, 1)
                    ch.link(v.max(e8[:], le[:]))
                    v.tensor_tensor(dd[:], e8[:, 1:2], e8[:, 0:1], ALU.subtract).then_inc(g_in, 1)
                    ch.link(v.max_index(ei8[:], e8[:], le[:]))
                    ch.link(v.tensor_copy(ei[:], ei8[:, 0:2]))
                    for c in range(2):
                        ch.done(v.tensor_scalar(oh[:, bass.ds(t, 1), c, :].rearrange("p t e -> p (t e)"), e_no[:], ei[:, c:c + 1], None, ALU.is_equal))
                    dve.wait_ge(g_out, 2 * t + 2)
                    ch.done(v.reciprocal(gw[:], gs[:]))
                    ch.link(v.tensor_scalar(pp[:, 0:1], ex[:], 1.0, None, ALU.add))
                    ch.link(v.reciprocal(pp[:, 0:1], pp[:, 0:1]))
                    ch.link(v.tensor_tensor(pp[:, 0:1], pp[:, 0:1], gw[:], ALU.mult))
                    ch.link(v.tensor_tensor(pp[:, 1:2], pp[:, 0:1], ex[:], ALU.mult))
                    ch.link(v.tensor_copy(wt[:, bass.ds(t, 1), :].rearrange("p t c -> p (t c)"), pp[:]))
                    ch.end()
                vb = bc(valid[:].rearrange("p (t c e) -> p t c e", c=1, e=1), P, TILES, 2, NE)
                pc = pre_ch
                pc.link(v.tensor_tensor(oh[:], oh[:], vb, ALU.mult))
                pc.link(v.tensor_tensor(both[:], oh[:, :, 0, :], oh[:, :, 1, :], ALU.add))
                pc.link(v.memset(pre[:, 0, :], 0.0))
                for t in range(TILES):
                    ins = v.tensor_tensor(pre[:, t + 1, :], pre[:, t, :], both[:, t, :], ALU.add)
                    pc.link(ins)
                dve.sem_inc(pre_ready, 1)
                dve.wait_ge(rank_ps, 1)
                pc.link(v.tensor_copy(cnt[:], ps[:, 1, 0:NE]))
                pc.link(v.tensor_scalar(cnt_i[:], cnt[:], float(P - 1), None, ALU.add))
                pc.link(v.tensor_scalar(cnt_i[:], cnt_i[:], 7, None, ALU.logical_shift_right))
                pc.link(v.tensor_copy(ntile[:], cnt_i[:]))
                pc.link(v.tensor_copy(inc[:], ntile[:]))
                a, b = inc, inc2
                for s in (1, 2, 4, 8, 16):
                    pc.done(v.tensor_copy(b[:, 0:s], a[:, 0:s]))
                    pc.link(v.tensor_tensor(b[:, s:NE], a[:, s:NE], a[:, 0:NE - s], ALU.add))
                    a, b = b, a
                pc.link(v.tensor_tensor(b[:], a[:], ntile[:], ALU.subtract))
                pc.link(v.tensor_scalar(b[:], b[:], float(P), None, ALU.mult))
                pc.link(v.tensor_tensor(rank[:], ps[:, 0, 0:TILES * NE].rearrange("p (t e) -> p t e", t=TILES), bc(b[:].rearrange("p (o e) -> p o e", o=1), P, TILES, NE), ALU.add))
                for c in range(2):
                    pc.link(v.tensor_tensor(pick[:, :, c, :], oh[:, :, c, :], rank[:], ALU.mult))
                pc.link(v.tensor_reduce(slot[:], pick[:], AX_X, ALU.add))
                pc.link(v.tensor_tensor(slot[:], slot[:], dump[:], ALU.add))
                pc.link(v.tensor_copy(slot_i[:], slot[:]))
                v.tensor_scalar(slot_c[:], slot[:], float(SLOTS - 1), None, ALU.min).then_inc(slots_ready, 1)
                v.tensor_tensor(wt[:], wt[:], bc(valid[:].rearrange("p (t c) -> p t c", c=1), P, TILES, 2), ALU.mult).then_inc(slots_ready, 1)
                pc.link(v.tensor_tensor(le_cmp[:], bc(a[0:1, :].rearrange("p (o e) -> p o e", o=1), 1, SLOT_TILES, NE),
                                        bc(tile_no[:].rearrange("p (j o) -> p j o", o=1), 1, SLOT_TILES, NE), ALU.is_le))
                pc.link(v.tensor_reduce(ownr[:], le_cmp[:], AX_X, ALU.add))
                v.tensor_scalar(own_i[:], ownr[:], float(NE - 1), None, ALU.min).then_inc(own_ready, 1)

            @block.tensor
            def _(pe):
                pe.wait_ge(loaded, 16 * NC)
                def turn_mix(t, par, k):
                    pe.wait_ge(in_loaded[par], 32 * (k + 1))
                    for c in range(KD):
                        last = pe.transpose(ps[:, c // 4, (c % 4) * P:(c % 4 + 1) * P], mix[:, par, c * P:(c + 1) * P], ident[:])
                    last.then_inc(mixT_ps, 1)

                def project(t):
                    pe.wait_ge(mixT_ready, t + 1)
                    if not isinstance(t, int) or t > 0:
                        pe.wait_ge(x2_ready, t)
                    for n in range(2):
                        for c in range(KD):
                            last = pe.matmul(ps[:, 2 + n, :], mixT[:, c * P:(c + 1) * P], w_out[:, c, n * 512:(n + 1) * 512], start=(c == 0), stop=(c == KD - 1))
                    last.then_inc(x2_ps, 1)

                turn_mix(0, 0, 0)
                project(0)
                turn_mix(1, 1, 0)
                for t, par, k in ahead(pe):
                    if more(t, 1):
                        project(t + 1)
                    pe.wait_ge(hn_ready, t + 1)
                    for c in range(KD):
                        last = pe.transpose(ps[:, 4 + c // 4, (c % 4) * P:(c % 4 + 1) * P], hn[:, par, c * P:(c + 1) * P], ident[:])
                    last.then_inc(hnT_ps, 1)
                    if more(t, 2):
                        turn_mix(t + 2, par, k + 1)
                    pe.wait_ge(hnT_ready, t + 1)
                    if not isinstance(t, int) or t > 0:
                        pe.wait_ge(lg_read, t)
                    for c in range(KD):
                        last = pe.matmul(ps[:, 6, 0:NL], hnT[:, c * P:(c + 1) * P], w_r[:, c, :], start=(c == 0), stop=(c == KD - 1))
                    last.then_inc(lg_ps, 1)
                pe.wait_ge(pre_ready, 1)
                flat = both[:].rearrange("p t e -> p (t e)")
                pe.matmul(ps[:, 0, 0:TILES * NE], strict[:], flat, start=True, stop=False)
                pe.matmul(ps[:, 0, 0:TILES * NE], ones[:], pre[:, 0:TILES, :].rearrange("p t e -> p (t e)"), start=False, stop=True)
                pe.matmul(ps[:, 1, 0:NE], ones[:], pre[:, TILES, :], start=True, stop=True).then_inc(rank_ps, 1)


MIX_STEPS = 18


def phase_experts(nc, ps, A, keep):
    with ExitStack() as ctx, own_semaphores(nc) as own:
        def sb(n, s, d=F32):
            return ctx.enter_context(nc.sbuf_tensor("ex_" + n, s, d))

        def sem(n):
            return own("ex_" + n)

        def kept(n):
            return keep.enter_context(nc.semaphore("ex_" + n))

        NF = FE // P
        ident = sb("ident", [P, P])
        owner = sb("owner", [1, SLOT_TILES], I32)
        rows_of = sb("rows_of", [P, SLOT_TILES + 2], I32)
        idx = [sb(f"idx{i}", [P, 1], I32) for i in range(2)]
        w_gu, w_d = sb("w_gu", [P, 2, KD, 2 * FE]), sb("w_d", [P, 2, NF, D])
        xg, xT = sb("xg", [P, 2, D]), sb("xT", [P, 2, D])
        th, act_g, hh, hhT = sb("th", [P, FE]), sb("act_g", [P, FE]), sb("hh", [P, FE]), sb("hhT", [P, FE])
        y = sb("y", [P, 2, D])
        loaded, waited = sem("loaded"), sem("waited")
        gu_loaded, d_loaded = [sem("gu_loaded0"), sem("gu_loaded1")], [sem("d_loaded0"), sem("d_loaded1")]
        idx_ready, x_loaded, x_used = sem("idx_ready"), [kept("x_loaded0"), kept("x_loaded1")], sem("x_used")
        xT_ready, gu_ps, th_ready, ag_ready, hh_ready = sem("xT_ready"), sem("gu_ps"), sem("th_ready"), sem("ag_ready"), sem("hh_ready")
        hhT_ps, hhT_ready, y_ps, y0_ready, y1_ready = sem("hhT_ps"), sem("hhT_ready"), sem("y_ps"), sem("y0_ready"), sem("y1_ready")
        y_stored, y_free = kept("y_stored"), sem("y_free")

        with nc.Block() as block:
            @block.sync
            def _(sp):
                sp.dma_start(ident[:], A["ident"]).then_inc(loaded, 16)
                sp.dma_start(owner[:], A["owner"]).then_inc(loaded, 16)
                with nc.allow_non_contiguous_dma(reason="slot lists are 4 bytes per slot"):
                    sp.dma_start(rows_of[:], A["slot_tok"].rearrange("(j p) o -> p (j o)", p=P)).then_inc(loaded, 16)
                sp.wait_ge(loaded, 48)
                with sp.Fori(0, SLOT_TILES // 2) as u:
                    for par in range(2):
                        j = 2 * u + par
                        e = sp.value_load(owner[0:1, bass.ds(j, 1)], min_val=0, max_val=NE - 1)
                        sp.wait_ge(gu_ps, j + 1)
                        sp.dma_start(w_gu[:, par, :, 0:FE], A["w_gate"][bass.ds(e, 1)].rearrange("e (p c) f -> (e p) c f", c=KD)).then_inc(gu_loaded[par], 16)
                        sp.dma_start(w_gu[:, par, :, FE:2 * FE], A["w_up"][bass.ds(e, 1)].rearrange("e (p c) f -> (e p) c f", c=KD)).then_inc(gu_loaded[par], 16)
                        sp.wait_ge(y_ps, j + 1)
                        sp.dma_start(w_d[:, par, :, :], A["w_down"][bass.ds(e, 1)].rearrange("e (p c) n -> (e p) c n", c=NF)).then_inc(d_loaded[par], 16)

            @block.gpsimd
            def _(pool):
                pool.wait_ge(loaded, 48)
                pool.sem_inc(y_free, 2)

                def gather(j, par):
                    pool.wait_ge(x_used, j + 1)
                    pool.tensor_copy(idx[par][:], rows_of[:, bass.ds(j, 1)]).then_inc(idx_ready, 1)
                    pool.wait_ge(idx_ready, j + 1)
                    pool.sem_inc(waited, 1)
                    pool.indirect_dma_start(out=xg[:, par, :], out_offset=None, in_=A["hn"],
                                            in_offset=bass.IndirectOffsetOnAxis(ap=idx[par][:], axis=0)).then_inc(x_loaded[par], 16)

                def store(j, par, first_one):
                    pool.wait_ge(y0_ready, j + 2)
                    pool.wait_ge(y1_ready, j + 2)
                    if not first_one:
                        pool.wait_ge(y_stored, 16 * j)
                        pool.sem_inc(y_free, 1)
                    pool.dma_start(A["ys"][bass.ds(j * P, P), :], y[:, par, :]).then_inc(y_stored, 16)

                gather(0, 0)
                gather(1, 1)
                gather(2, 0)
                store(0, 0, True)
                gather(3, 1)
                store(1, 1, False)
                with pool.Fori(1, SLOT_TILES // 2) as u:
                    for par in range(2):
                        if par == 0:
                            gather(2 * u + 2, 0)
                        store(2 * u + par, par, False)
                        if par == 0:
                            gather(2 * u + 3, 1)
                pool.wait_ge(y_stored, 16 * SLOT_TILES)
                pool.wait_ge(x_loaded[0], 16 * (SLOT_TILES // 2 + 1))
                pool.wait_ge(x_loaded[1], 16 * (SLOT_TILES // 2 + 1))

            @block.scalar
            def _(act):
                def turned(j, par):
                    act.wait_ge(x_used, j + 3)
                    act.activation(xT[:, par, :].rearrange("p (a b) -> p a b", a=2), ps[:, 0:2, :], ACT.Copy).then_inc(xT_ready, 1)

                turned(0, 0)
                with act.Fori(0, SLOT_TILES // 2) as u:
                    for par in range(2):
                        j = 2 * u + par
                        act.wait_ge(gu_ps, j + 3)
                        act.activation(th[:], ps[:, 2, 0:FE], ACT.Tanh, scale=0.5).then_inc(th_ready, 1)
                        turned(j + 1, 1 - par)
                        act.wait_ge(y_ps, j + 3)
                        act.wait_ge(y_free, j + 1)
                        act.activation(y[:, par, 0:512], ps[:, 4, :], ACT.Copy).then_inc(y0_ready, 1)

            @block.vector
            def _(dve):
                v = nc.vector
                with dve.Fori(0, SLOT_TILES // 2) as u:
                    for par in range(2):
                        j = 2 * u + par
                        dve.wait_ge(th_ready, j + 1)
                        v.scalar_tensor_tensor(act_g[:], th[:], 1.0, ps[:, 2, 0:FE], ALU.add, ALU.mult).then_inc(ag_ready, 1)
                        dve.wait_ge(ag_ready, j + 1)
                        v.scalar_tensor_tensor(hh[:], act_g[:], 0.5, ps[:, 2, FE:2 * FE], ALU.mult, ALU.mult).then_inc(hh_ready, 1)
                        dve.wait_ge(hhT_ps, j + 1)
                        v.tensor_copy(hhT[:], ps[:, 3, 0:FE]).then_inc(hhT_ready, 1)
                        dve.wait_ge(y_ps, j + 3)
                        dve.wait_ge(y_free, j + 1)
                        v.tensor_copy(y[:, par, 512:1024], ps[:, 5, :]).then_inc(y1_ready, 1)

            @block.tensor
            def _(pe):
                pe.wait_ge(loaded, 48)
                pe.sem_inc(gu_ps, 2)
                pe.sem_inc(y_ps, 2)
                pe.sem_inc(x_used, 2)
                pe.sem_inc(y0_ready, 1)
                pe.sem_inc(y1_ready, 1)

                def turn(j, par, k):
                    pe.wait_ge(x_loaded[par], 16 * (k + 1))
                    xv = xg[:, par, :].rearrange("p (i c) -> p c i", c=KD)
                    for c in range(KD):
                        last = pe.transpose(ps[:, c // 4, (c % 4) * P:(c % 4 + 1) * P], xv[:, c, :], ident[:])
                    last.then_inc(x_used, 1)

                turn(0, 0, 0)
                with pe.Fori(0, SLOT_TILES // 2) as u:
                    for par in range(2):
                        j = 2 * u + par
                        pe.wait_ge(gu_loaded[par], 32 * (u + 1))
                        pe.wait_ge(xT_ready, j + 1)
                        for c in range(KD):
                            last = pe.matmul(ps[:, 2, :], xT[:, par, c * P:(c + 1) * P], w_gu[:, par, c, :], start=(c == 0), stop=(c == KD - 1))
                        last.then_inc(gu_ps, 1)
                        turn(j + 1, 1 - par, u + par)
                        pe.wait_ge(hh_ready, j + 1)
                        hv = hh[:].rearrange("p (i c) -> p c i", c=NF)
                        for c in range(NF):
                            last = pe.transpose(ps[:, 3, c * P:(c + 1) * P], hv[:, c, :], ident[:])
                        last.then_inc(hhT_ps, 1)
                        pe.wait_ge(hhT_ready, j + 1)
                        pe.wait_ge(d_loaded[par], 16 * (u + 1))
                        pe.wait_ge(y0_ready, j + 1)
                        pe.wait_ge(y1_ready, j + 1)
                        for n in range(2):
                            for c in range(NF):
                                last = pe.matmul(ps[:, 4 + n, :], hhT[:, c * P:(c + 1) * P], w_d[:, par, c, n * 512:(n + 1) * 512], start=(c == 0), stop=(c == NF - 1))
                        last.then_inc(y_ps, 1)


def phase_combine(nc, ps, A, keep):
    with ExitStack() as ctx, own_semaphores(nc) as own:
        def sb(n, s, d=F32):
            return ctx.enter_context(nc.sbuf_tensor("co_" + n, s, d))

        def sem(n):
            return own("co_" + n)

        def kept(n):
            return keep.enter_context(nc.semaphore("co_" + n))

        w_fin = sb("w_fin", [P, D])
        slots, wt = sb("slots", [P, TILES, 2], I32), sb("wt", [P, TILES, 2])
        idx = sb("idx", [P, 2, 2], I32)
        x2, ya, yb, out = sb("x2", [P, 2, D]), sb("ya", [P, 2, D]), sb("yb", [P, 2, D]), sb("out", [P, 2, D])
        wts = sb("wts", [P, 2])
        squares, sq, rs = sb("squares", [P, D]), sb("sq", [P, 1]), sb("rs", [P, 2])
        loaded, steps = sem("loaded"), sem("steps")
        x_loaded, y_loaded = [sem("x_loaded0"), sem("x_loaded1")], [kept("y_loaded0"), kept("y_loaded1")]
        idx_ready, used, sum_ready, sq_ready, out_ready = sem("idx_ready"), sem("used"), sem("sum_ready"), sem("sq_ready"), sem("out_ready")
        out_stored = [sem("out_stored0"), sem("out_stored1")]

        with nc.Block() as block:
            @block.sync
            def _(sp):
                sp.dma_start(w_fin[:], A["w_final"].partition_broadcast(P)).then_inc(loaded, 16)
                sp.dma_start(slots[:].rearrange("p t c -> p (t c)"), A["slots"]).then_inc(loaded, 16)
                sp.dma_start(wt[:].rearrange("p t c -> p (t c)"), A["weights"]).then_inc(loaded, 16)
                for t in range(TILES):
                    if t >= 2:
                        sp.wait_ge(out_ready, t - 1)
                    sp.dma_start(x2[:, t % 2, :], A["x2"][t * P:(t + 1) * P, :]).then_inc(x_loaded[t % 2], 16)
                    if t:
                        sp.wait_ge(out_ready, t)
                        sp.dma_start(A["y"][(t - 1) * P:t * P, :], out[:, (t - 1) % 2, :]).then_inc(out_stored[(t - 1) % 2], 16)
                sp.wait_ge(out_ready, TILES)
                sp.dma_start(A["y"][(TILES - 1) * P:TILES * P, :], out[:, (TILES - 1) % 2, :]).then_inc(out_stored[(TILES - 1) % 2], 16)
                sp.wait_ge(out_stored[0], 16 * ((TILES + 1) // 2))
                sp.wait_ge(out_stored[1], 16 * (TILES // 2))

            @block.gpsimd
            def _(pool):
                pool.wait_ge(loaded, 48)
                for t in range(TILES):
                    if t >= 2:
                        pool.wait_ge(out_ready, t - 1)
                    for c, dst in ((0, ya), (1, yb)):
                        pool.indirect_dma_start(out=dst[:, t % 2, :], out_offset=None, in_=A["ys"],
                                                in_offset=bass.IndirectOffsetOnAxis(ap=slots[:, t, c:c + 1], axis=0)).then_inc(y_loaded[t % 2], 16)

            @block.scalar
            def _(act):
                for t in range(TILES):
                    act.wait_ge(sum_ready, t + 1)
                    act.activation(squares[:], out[:, t % 2, :], ACT.Square, accum_out=sq[:]).then_inc(sq_ready, 1)

            @block.vector
            def _(dve):
                v = nc.vector
                ch = Chain(dve, steps, 0)
                dve.wait_ge(loaded, 48)
                for t in range(TILES):
                    p = t % 2
                    dve.wait_ge(x_loaded[p], 16 * (t // 2 + 1))
                    dve.wait_ge(y_loaded[p], 32 * (t // 2 + 1))
                    if t >= 2:
                        dve.wait_ge(out_stored[p], 16 * (t // 2))
                    ch.link(v.scalar_tensor_tensor(out[:, p, :], ya[:, p, :], wt[:, t, 0:1], x2[:, p, :], ALU.mult, ALU.add))
                    v.scalar_tensor_tensor(out[:, p, :], yb[:, p, :], wt[:, t, 1:2], out[:, p, :], ALU.mult, ALU.add).then_inc(sum_ready, 1)
                    dve.wait_ge(sq_ready, t + 1)
                    rsqrt(nc, ch, rs[:, 0:1], sq[:], rs[:, 1:2], 1.0 / D, EPS)
                    v.scalar_tensor_tensor(out[:, p, :], out[:, p, :], rs[:, 0:1], w_fin[:], ALU.mult, ALU.mult).then_inc(out_ready, 1)


SCRATCH = {"proj": (RPAD + CONV_W - 1, PROJ_W), "mix": (RPAD, 2 * H * DV), "gates_s": (2, BS, H),
           "rows_s": (3, BS, H * DK), "q_s": (BS, H * DV), "coef": (P, 2), "o_s": (BS * H, DV),
           "x2": (RPAD, D), "hn": (RPAD, D), "ys": (SLOTS, D), "weights": (P, 2 * TILES)}
INT_SCRATCH = {"slot_tok": (SLOTS + 2 * P, 1), "slots": (P, 2 * TILES), "owner": (1, SLOT_TILES)}
OUTS = {"y": (RPAD, D), "p_conv": (CONV_W - 1, CONV_CH), "p_gdn": (H, DK, DV), "p_k": (LP, H * DV), "p_v": (LP, H * DV),
        "s_conv": (BS, CONV_W - 1, CONV_CH), "s_gdn": (BS * H, DK, DV), "s_k": (BS, H * DV), "s_v": (BS, H * DV)}


def program(nc, A):
    with ExitStack() as ctx:
        ps = ctx.enter_context(nc.psum_tensor("ps", [P, 8, 512], F32))
        phase_project(nc, ps, A, ctx)
        phase_recurrence_and_decode(nc, ps, A, ctx)
        phase_sample_gdn(nc, ps, A, ctx)
        phase_attention(nc, ps, A, ctx)
        phase_mix(nc, ps, A, ctx)
        phase_experts(nc, ps, A, ctx)
        phase_combine(nc, ps, A, ctx)


def constants():
    r = np.arange(P)
    f = np.float32
    c = {"ident": np.eye(P, dtype=f), "ones": np.ones((P, P), f), "upper": (r[:, None] <= r[None, :]).astype(f)}
    levels = np.zeros((P, 7, P), f)
    for l in range(7):
        s = 1 << l
        b = r // s
        levels[:, l, :] = (b[:, None] // 2 == b[None, :] // 2) & (b[:, None] % 2 == 1) & (b[None, :] % 2 == 0)
    c["levels"] = levels
    c["rowmask"] = (r[:, None] + P * np.arange(TILES)[None, :] < LP).astype(f)
    row = r[:, None] + P * np.arange(TILES)[None, :]
    c["valid"] = (row < ROWS).astype(f)
    c["dump"] = np.where(row < ROWS, 0, SLOTS + r[:, None])[:, :, None] + np.where(row < ROWS, 0, P)[:, :, None] * np.arange(2)
    c["dump"] = c["dump"].astype(f)
    c["tok"] = row.astype(np.int32)
    c["e_no"] = np.ascontiguousarray(np.broadcast_to(np.arange(NE, dtype=f), (P, NE)))
    c["e_group"] = np.ascontiguousarray(np.broadcast_to((np.arange(NE) // EPG).astype(f), (P, NE)))
    c["tile_no"] = np.arange(SLOT_TILES, dtype=f)[None, :]
    c["slot_fill"] = np.full((SLOTS + 2 * P, 1), RPAD - 1, np.int32)
    c["first"] = np.where(r == 0, f(0), f(-BIG))[:, None]
    c["lane"] = np.ascontiguousarray(np.broadcast_to((r % (P // CHUNK)).astype(np.int32)[:, None], (P, BS * CHUNKS)))
    c["strict"] = (r[:, None] < r[None, :]).astype(f)
    c["causal"] = np.where(r[:, None] >= r[None, :], f(0), f(-BIG))
    inv_freq = f(ROPE_THETA) ** (-np.arange(HALF, dtype=f) * f(2) / f(4 * HALF // 2))
    pos = np.where(np.arange(RPAD) < LP, np.arange(RPAD), PAST).astype(f)
    ang = (pos[:, None] * inv_freq[None, :]).reshape(TILES, P, HALF).transpose(1, 0, 2)
    c["cos"], c["sin"] = np.ascontiguousarray(np.cos(ang)), np.ascontiguousarray(np.sin(ang))
    c["cos_s"], c["sin_s"] = (np.ascontiguousarray(np.broadcast_to(c[n][LP % P, TILES - 1], (BS, HALF))) for n in ("cos", "sin"))
    return c


def kernel(**inputs):
    import numpy as _np
    import concourse.bacc as _bacc
    from concourse import mybir as _mybir
    from concourse.bass_utils import run_bass_kernel_spmd as _run

    nc = _bacc.Bacc("TRN2", target_bir_lowering=False, num_devices=1)
    i = {n: _np.ascontiguousarray(a) for n, a in inputs.items()}
    arrays = {
        "x": _np.concatenate([i["meta_tokens"], i["x_prompt"][0], i["x_sample"][:, 0],
                              _np.zeros((RPAD + P - ROWS, D), i["x_prompt"].dtype)], axis=0),
        "w_in": i["w_in"][0], "w_norm_mix": i["w_norm_mix"][0], "w_conv": i["w_conv"][0],
        "w_gnorm": i["w_gnorm"][0], "a_log": i["a_log"][0], "dt_bias": i["dt_bias"][0],
        "state_conv": i["state_conv"][0], "state_gdn": i["state_gdn"][0].reshape(BS * H, DK, DV), "w_subln": i["w_subln"][0],
        "cache_k": i["cache_k"][0].reshape(-1, PAGE, H * 2 * DQ), "cache_v": i["cache_v"][0].reshape(-1, PAGE, H * DV),
        "page_table": i["page_table"].reshape(BS * CHUNKS, CHUNK).T, "w_out": i["w_out"][0], "w_norm_ffn": i["w_norm_ffn"][0],
        "w_final": i["w_final"], **{n: i[n][0] for n in ("w_group", "w_expert", "w_gate", "w_up", "w_down")},
        **{n: i[n][0] for n in ("lambda_q1", "lambda_k1", "lambda_q2", "lambda_k2")},
    }
    arrays["page_table"] = _np.ascontiguousarray(arrays["page_table"])
    arrays.update(constants())
    A = {}
    for n, a in arrays.items():
        A[n] = nc.dram_tensor("in_" + n, a.shape, _mybir.dt.from_np(a.dtype), kind="ExternalInput").ap()
    for n, shape in SCRATCH.items():
        A[n] = nc.dram_tensor("scr_" + n, shape, F32, kind="Internal").ap()
    for n, shape in INT_SCRATCH.items():
        A[n] = nc.dram_tensor("scr_" + n, shape, I32, kind="Internal").ap()
    for n, shape in OUTS.items():
        A[n] = nc.dram_tensor("out_" + n, shape, F32, kind="ExternalOutput").ap()
    program(nc, A)
    r = _run(nc, [{"in_" + n: a for n, a in arrays.items()}], core_ids=[0]).results[0]
    o = {n: r["out_" + n] for n in OUTS}
    return (o["y"][N_META:LP].reshape(1, SEQ, D), o["y"][LP:ROWS].reshape(BS, 1, D),
            o["p_conv"].reshape(1, 1, CONV_W - 1, CONV_CH), o["p_gdn"].reshape(1, 1, H, DK, DV),
            o["p_k"].reshape(1, 1, LP, H, 2 * DQ), o["p_v"].reshape(1, 1, LP, H, DV),
            o["s_conv"].reshape(1, BS, CONV_W - 1, CONV_CH), o["s_gdn"].reshape(1, BS, H, DK, DV),
            o["s_k"].reshape(1, BS, 1, H, 2 * DQ), o["s_v"].reshape(1, BS, 1, H, DV))
```

```python
import math
from contextlib import ExitStack, contextmanager

import numpy as np

import concourse.bass as bass
from concourse import mybir

F32 = mybir.dt.float32
I32 = mybir.dt.int32
U32 = mybir.dt.uint32
ALU = mybir.AluOpType
ACT = mybir.ActivationFunctionType
AX_X = mybir.AxisListType.X

P = 128
D = 1024
KD = D // P
SEQ, N_META = 1024, 16
LP = SEQ + N_META
BS = 8
ROWS = LP + BS
TILES = -(-ROWS // P)
RPAD = TILES * P
EPS = 1e-6
H = 4
DK = DV = 128
DQ = 64
CONV_W = 4
CONV_CH = 3 * H * DK
C_Z = CONV_CH
C_A = C_Z + H * DV
C_B = C_A + H
C_DQ = C_B + H
C_DK = C_DQ + H * 2 * DQ
C_DV = C_DK + H * 2 * DQ
PROJ_W = C_DV + H * DV
HALF = DQ // 4 // 2
ROPE_THETA = 500000.0
PAST, PAGE = 8192, 128
N_PAGES = PAST // PAGE
LAM_INIT = 0.8 - 0.6 * math.exp(-0.3 * 0)
G, EPG, NE, FE = 4, 8, 32, 256
SLOT_TILES = (2 * ROWS) // P + NE
SLOTS = SLOT_TILES * P
BIG = 1e30


@contextmanager
def own_semaphores(nc):
    held = []

    def own(name):
        held.append(nc.alloc_semaphore(name))
        return held[-1]

    yield own
    nc.clear_and_free_semaphores(held)
    nc.all_engine_barrier()


def tiles(eng, n=TILES):
    yield 0, 0, 0
    with eng.Fori(0, (n - 1) // 2) as u:
        yield 2 * u + 1, 1, u
        yield 2 * u + 2, 0, u + 1


class Chain:

    def __init__(self, eng, sem, per):
        self.eng, self.sem, self.per, self.base, self.n = eng, sem, per, 0, 0

    def begin(self, t):
        self.base, self.n = t * self.per, 0

    def done(self, ins):
        self.n += 1
        ins.then_inc(self.sem, 1)

    def sync(self):
        self.eng.wait_ge(self.sem, self.base + self.n)

    def link(self, ins):
        self.done(ins)
        self.sync()

    def end(self):
        assert self.n == self.per, f"{self.sem}: {self.n} steps, {self.per} declared"


RSQRT_STEPS = 12


def rsqrt(nc, ch, y, x, tmp, scale, bias, times=1.0):
    v = nc.vector
    ch.link(v.tensor_scalar(x, x, scale, bias, ALU.mult, ALU.add))
    ch.link(v.tensor_scalar(tmp.bitcast(I32), x.bitcast(I32), 1, None, ALU.logical_shift_right))
    ch.link(v.tensor_scalar(y.bitcast(I32), tmp.bitcast(I32), -1, 0x5F3759DF, ALU.mult, ALU.add))
    for step in range(3):
        last = times if step == 2 else 1.0
        ch.link(v.tensor_tensor(tmp, y, y, ALU.mult))
        ch.link(v.scalar_tensor_tensor(tmp, tmp, -0.5 * last, x, ALU.mult, ALU.mult))
        ch.link(v.scalar_tensor_tensor(y, tmp, 1.5 * last, y, ALU.add, ALU.mult))


def bc(ap, *shape):
    return ap.to_broadcast(list(shape))


def phase_project(nc, ps, A, keep):
    with ExitStack() as ctx, own_semaphores(nc) as own:
        def sb(n, s, d=F32):
            return ctx.enter_context(nc.sbuf_tensor("pj_" + n, s, d))

        def sem(n):
            return own("pj_" + n)

        def kept(n):
            return keep.enter_context(nc.semaphore("pj_" + n))

        w_in = sb("w_in", [P, KD, PROJ_W])
        w_norm = sb("w_norm", [P, D])
        ident = sb("ident", [P, P])
        x = sb("x", [P, 2, D])
        xn = sb("xn", [P, D])
        xT = sb("xT", [P, 2, D])
        proj = sb("proj", [P, 2, PROJ_W])
        sq = sb("sq", [P, 1])
        rs = sb("rs", [P, 2])
        squares = sb("squares", [P, D])
        zero = sb("zero", [4, (CONV_W - 1) * PROJ_W // 4])

        w_loaded = [sem(f"w_loaded{i}") for i in range(8)]
        c_loaded = sem("c_loaded")
        x_loaded = [sem("x_loaded0"), sem("x_loaded1")]
        cleared, zeroed = sem("cleared"), kept("zeroed")
        sq_ready = sem("sq_ready")
        steps = sem("dve_steps")
        xn_ready = sem("xn_ready")
        xnT_ready = sem("xnT_ready")
        xT_ready = sem("xT_ready")
        mm_done = sem("mm_done")
        act_evac = sem("act_evac")
        dve_evac = sem("dve_evac")
        stored, proj_free = kept("stored"), sem("proj_free")
        NCH = 8
        cols = [(n * 512, min(512, PROJ_W - n * 512)) for n in range(NCH)]

        with nc.Block() as block:
            @block.sync
            def _(sp):
                def load(t, par):
                    sp.dma_start(x[:, par, :], A["x"][bass.ds(t * P, P), :]).then_inc(x_loaded[par], 16)

                load(0, 0)
                sp.dma_start(ident[:], A["ident"]).then_inc(c_loaded, 16)
                sp.dma_start(w_norm[:], A["w_norm_mix"].partition_broadcast(P)).then_inc(c_loaded, 16)
                for n, (o, w) in enumerate(cols):
                    sp.dma_start(w_in[:, :, o:o + w], A["w_in"][:, o:o + w].rearrange("(c p) n -> p c n", p=P)).then_inc(w_loaded[n], 16)
                for t, par, k in tiles(sp):
                    if not isinstance(t, int):
                        sp.wait_ge(xn_ready, t)
                    load(t + 1, 1 - par)

            @block.gpsimd
            def _(pool):
                pool.sem_inc(proj_free, 2)
                pool.memset(zero[:], 0.0).then_inc(cleared, 1)
                pool.wait_ge(cleared, 1)
                pool.dma_start(A["proj"][0:CONV_W - 1, :].rearrange("i n -> (i n)").rearrange("(p n) -> p n", p=4), zero[:]).then_inc(zeroed, 16)
                pool.wait_ge(zeroed, 16)
                for t, par, k in tiles(pool):
                    pool.wait_ge(act_evac, 4 * t + 4)
                    pool.wait_ge(dve_evac, 4 * t + 4)
                    if not isinstance(t, int):
                        pool.wait_ge(stored, 16 * t)
                        pool.sem_inc(proj_free, 1)
                    pool.dma_start(A["proj"][bass.ds(t * P + CONV_W - 1, P), :],
                                   proj[:, par, :]).then_inc(stored, 16)
                pool.wait_ge(stored, 16 * TILES)

            @block.scalar
            def _(act):
                def square(t, par, k):
                    act.wait_ge(x_loaded[par], 16 * (k + 1))
                    act.activation(squares[:], x[:, par, :], ACT.Square, accum_out=sq[:]).then_inc(sq_ready, 1)

                square(0, 0, 0)
                for t, par, k in tiles(act):
                    act.wait_ge(xnT_ready, t + 1)
                    act.activation(xT[:, par, :].rearrange("p (a b) -> p a b", a=2), ps[:, 0:2, :], ACT.Copy).then_inc(xT_ready, 1)
                    act.wait_ge(proj_free, t + 1)
                    for n in range(0, NCH, 2):
                        o, w = cols[n]
                        act.wait_ge(mm_done, 8 * t + n + 1)
                        act.activation(proj[:, par, o:o + w], ps[:, 2 + n % 4, 0:w], ACT.Copy).then_inc(act_evac, 1)
                        if n == 0:
                            act.wait_ge(xn_ready, t + 1)
                            square(t + 1, 1 - par, k + par)

            @block.vector
            def _(dve):
                ch = Chain(dve, steps, 12)

                def norm(t, par):
                    ch.begin(t)
                    dve.wait_ge(sq_ready, t + 1)
                    rsqrt(nc, ch, rs[:, 0:1], sq[:], rs[:, 1:2], 1.0 / D, EPS)
                    ch.end()
                    if not isinstance(t, int) or t > 0:
                        dve.wait_ge(xnT_ready, t)
                    nc.vector.scalar_tensor_tensor(xn[:], x[:, par, :], rs[:, 0:1], w_norm[:],
                                                   ALU.mult, ALU.mult).then_inc(xn_ready, 1)

                dve.wait_ge(c_loaded, 32)
                norm(0, 0)
                for t, par, k in tiles(dve):
                    dve.wait_ge(proj_free, t + 1)
                    for n in range(1, NCH, 2):
                        o, w = cols[n]
                        dve.wait_ge(mm_done, 8 * t + n + 1)
                        nc.vector.tensor_copy(proj[:, par, o:o + w], ps[:, 2 + n % 4, 0:w]).then_inc(dve_evac, 1)
                        if n == 1:
                            norm(t + 1, 1 - par)

            @block.tensor
            def _(pe):
                pe.wait_ge(c_loaded, 32)
                for t, par, k in tiles(pe):
                    pe.wait_ge(xn_ready, t + 1)
                    if not isinstance(t, int):
                        pe.wait_ge(xT_ready, t)
                    for c in range(KD):
                        last = pe.transpose(ps[:, c // 4, (c % 4) * P:(c % 4 + 1) * P], xn[:, c * P:(c + 1) * P], ident[:])
                    last.then_inc(xnT_ready, 1)
                    pe.wait_ge(xT_ready, t + 1)
                    for n in range(NCH):
                        o, w = cols[n]
                        if not (isinstance(t, int) and n < 4):
                            pe.wait_ge(dve_evac if n % 2 else act_evac, 4 * t + n // 2 - 1)
                        if isinstance(t, int):
                            pe.wait_ge(w_loaded[n], 16)
                        for c in range(KD):
                            last = pe.matmul(ps[:, 2 + n % 4, 0:w], xT[:, par, c * P:(c + 1) * P],
                                             w_in[:, c, o:o + w], start=(c == 0), stop=(c == KD - 1))
                        last.then_inc(mm_done, 1)


CHUNK = 4
CHUNKS = N_PAGES // CHUNK
PRE_LOADS = 11 + CHUNK
RING = 4


def phase_recurrence_and_decode(nc, ps, A, keep):
    with ExitStack() as ctx, own_semaphores(nc) as own:
        def sb(n, s, d=F32):
            return ctx.enter_context(nc.sbuf_tensor("gd_" + n, s, d))

        def sem(n):
            return own("gd_" + n)

        def kept(n):
            return keep.enter_context(nc.semaphore("gd_" + n))

        HP = [P, H, P]
        HW = H * P
        ident, upper, ones = sb("ident", [P, P]), sb("upper", [P, P]), sb("ones", [P, P])
        levels = sb("levels", [P, 7, P])
        w_conv = sb("w_conv", [P, CONV_W, CONV_CH])
        w_gn = sb("w_gn", [P, DV])
        rowmask = sb("rowmask", [P, TILES])
        a_log, dt_bias = sb("a_log", [P, H]), sb("dt_bias", [P, H])
        ab = sb("ab", [P, TILES, 2 * H])
        ga, gb, gc = sb("ga", [P, TILES, H]), sb("gb", [P, TILES, H]), sb("gc", [P, TILES, H])
        gate, beta = sb("gate", [P, TILES, H]), sb("beta", [P, TILES, H])
        gu, bu = sb("gu", [P, TILES, H]), sb("bu", [P, TILES, H])
        cs = sb("cs", [P, CONV_W, CONV_CH])
        z = sb("z", [P, HW])
        th = sb("th", [P, CONV_CH])
        qkv = sb("qkv", [P, 3, HW])
        ss, rn, rt = sb("ss", [P, 8]), sb("rn", [P, 8]), sb("rt", [P, 8])
        gcol, glg, eg, beg, egl = (sb(n, [P, H]) for n in ("gcol", "glg", "eg", "beg", "egl"))
        egrow = sb("egrow", HP)
        dt = sb("dt", HP)
        kT, qT, qgT = sb("kT", HP), sb("qT", HP), sb("qgT", HP)
        vb, kbg, kw = sb("vb", HP), sb("kbg", HP), sb("kw", HP)
        ug, ib = kbg, kw
        LT, qkT = sb("LT", HP), sb("qkT", HP)
        TT = sb("TT", [P, 2, H, P])
        prod = sb("prod", HP)
        nwT, u, S = sb("nwT", HP), sb("u", HP), sb("S", HP)
        osq, on, zt, zs = prod, sb("on", HP), sb("zt", [P, HW]), sb("zs", [P, HW])

        C = 2 * H
        NP1 = N_PAGES + 1
        pages, lane = sb("pages", [P, BS * CHUNKS], I32), sb("lane", [P, BS * CHUNKS], I32)
        keys, vals = sb("keys", [P, RING, CHUNK, HW]), sb("vals", [P, RING, CHUNK, HW])
        q, kn, vn = sb("q", [P, BS, HW]), sb("kn", [P, HW]), sb("vn", [P, HW])
        first, coef = sb("first", [P, 1]), sb("coef", [P, 2])
        s, e = sb("s", [P, NP1, C]), sb("e", [P, NP1, C])
        w = sb("w", [P, NP1, H])
        m, mx, l, lt, r = (sb(n, [P, C]) for n in ("m", "mx", "l", "lt", "r"))
        o = sb("o", [H, HW])
        od, dsq, w_sub = sb("od", [BS * H, DV]), sb("dsq", [BS * H, DV]), sb("w_sub", [BS * H, DV])
        s1, r1, r2 = sb("s1", [BS * H, 1]), sb("r1", [BS * H, 1]), sb("r2", [BS * H, 1])
        qk_s = vals[0:BS, 0, 0:2, :].rearrange("p a c -> p (a c)")
        rot = vals[0:BS, 1, 0, :].rearrange("p (a c j) -> p a c j", a=4, j=HALF)
        cos, sin = vals[0:BS, 1, 1, 0:HALF], vals[0:BS, 1, 1, HALF:2 * HALF]
        lams = vals[:, 2, 0, 0:4 * DQ].rearrange("p (i j) -> p i j", i=4)
        lprod = vals[:, 2, 1, 0:2 * DQ].rearrange("p (i j) -> p i j", i=2)
        lsum, lexp = vals[:, 2, 2, 0:2], vals[:, 2, 2, 2:4]
        pre_loaded, rot_ready, pre_stored, q_loaded, lam_ready = (sem(n) for n in ("pre_loaded", "rot_ready", "pre_stored", "q_loaded", "lam_ready"))
        new_loaded, vn_loaded = sem("new_loaded"), sem("vn_loaded")
        k_loaded, v_loaded = [kept(f"k_loaded{i}") for i in range(RING)], [kept(f"v_loaded{i}") for i in range(RING)]
        k_index, v_index = sb("k_index", [P, RING, 1], I32), sb("v_index", [P, RING, 1], I32)
        pages_ready, k_picked, v_picked = sem("pages_ready"), sem("k_picked"), sem("v_picked")
        k_mult, k_mult_pool, k_used, v_used = sem("k_mult"), sem("k_mult_pool"), sem("k_used"), sem("v_used")
        dsteps, waited = sem("dsteps"), sem("waited")
        m_ready, mx_ready, s_ready, e_ready, l_ready, lt_ready = (sem(n) for n in ("m_ready", "mx_ready", "s_ready", "e_ready", "l_ready", "lt_ready"))
        w_ready, pv_done, od_ready, od_stored = sem("w_ready"), sem("pv_done"), sem("od_ready"), sem("od_stored")
        od_loaded, dn_ready, od_clear = sem("od_loaded"), sem("dn_ready"), sem("od_clear")

        c_loaded = sem("c_loaded")
        in_loaded = sem("in_loaded")
        cs_used, z_used = sem("cs_used"), sem("z_used")
        steps, psteps, asteps = sem("dve_steps"), sem("pool_steps"), sem("act_steps")
        gate_a, gate_b, gate_c = sem("gate_exp"), sem("gate_log"), sem("gates_ready")
        conv23, pconv = sem("conv23_ready"), sem("pool_conv_steps")
        conv_ready, th_ready = sem("conv_ready"), sem("tanh_ready")
        ug_ready, g_ps = sem("ug_ready"), sem("g_ps")
        qk_ready, qkT_ps, kqT_ready = sem("qk_ready"), sem("qkT_ps"), sem("kqT_ready")
        d_in, d_ready, eg_ready = sem("d_in"), sem("d_ready"), sem("eg_ready")
        operands = sem("operands_ready")
        kk_ps = sem("kk_ps")
        t_ready, p_ps, p_ready, dT_ps = sem("t_ready"), sem("p_ps"), sem("p_ready"), sem("dT_ps")
        w_ps, nw_ready, u_ps, u_ready = sem("w_ps"), sem("nw_ready"), sem("u_ps"), sem("u_ready")
        o_ps, osq_ready, zs_ready, zt_ready = sem("o_ps"), sem("osq_ready"), sem("zs_ready"), sem("zt_ready")
        on_free = sem("on_free")
        on_ready, on_stored, out_done = sem("on_ready"), kept("on_stored"), sem("out_done")

        def bank(b):
            return ps[:, b, :].rearrange("p (h j) -> p h j", h=H)

        def turns(eng, end=BS):
            yield 0, True, False
            with eng.Fori(1, end) as t:
                yield t, True, True
            for t in range(end, BS):
                yield t, True, True
            yield BS, False, True

        with nc.Block() as block:
            @block.sync
            def _(sp):
                for dst, src in ((ident[:], A["ident"]), (upper[:], A["upper"]), (ones[:], A["ones"]),
                                 (levels[:], A["levels"]), (rowmask[:], A["rowmask"]),
                                 (w_conv[:].rearrange("p i c -> p (i c)"), A["w_conv"].rearrange("i c -> (i c)").partition_broadcast(P)),
                                 (w_gn[:], A["w_gnorm"].partition_broadcast(P)),
                                 (a_log[:], A["a_log"].partition_broadcast(P)),
                                 (dt_bias[:], A["dt_bias"].partition_broadcast(P)),
                                 (ab[:], A["proj"][CONV_W - 1:CONV_W - 1 + RPAD, C_A:C_A + 2 * H].rearrange("(t p) c -> p t c", p=P))):
                    sp.dma_start(dst, src).then_inc(c_loaded, 16)
                def load(t):
                    sp.wait_ge(cs_used, t + 1)
                    for i in range(CONV_W):
                        sp.dma_start(cs[:, i, :], A["proj"][bass.ds(t * P + i, P), 0:CONV_CH]).then_inc(in_loaded, 16)
                    sp.wait_ge(z_used, t + 1)
                    sp.dma_start(z[:], A["proj"][bass.ds(t * P + CONV_W - 1, P), C_Z:C_Z + HW]).then_inc(in_loaded, 16)

                load(0)
                row0 = CONV_W - 1 + LP
                for dst, src in [(qk_s, A["proj"][row0:row0 + BS, C_DQ:C_DQ + 2 * HW]), (cos, A["cos_s"]), (sin, A["sin_s"]),
                                 (lane[:], A["lane"]), (first[:], A["first"]), (w_sub[:], A["w_subln"].partition_broadcast(BS * H)),
                                 (A["s_v"], A["proj"][row0:row0 + BS, C_DV:C_DV + HW])] + \
                                [(pages[g * P // CHUNK:(g + 1) * P // CHUNK, :], A["page_table"][g, :].partition_broadcast(P // CHUNK)) for g in range(CHUNK)] + \
                                [(lams[:, i, :], A[n].partition_broadcast(P)) for i, n in enumerate(("lambda_q1", "lambda_q2", "lambda_k1", "lambda_k2"))]:
                    sp.dma_start(dst, src).then_inc(pre_loaded, 16)
                sp.wait_ge(rot_ready, 1)
                sp.wait_ge(lam_ready, 3)
                for dst, src in [(A["q_s"], qk_s[:, 0:HW]), (A["s_k"], qk_s[:, HW:2 * HW]), (A["coef"], coef[:])]:
                    sp.dma_start(dst, src).then_inc(pre_stored, 16)
                sp.wait_ge(pre_stored, 48)
                sp.wait_ge(pre_loaded, 16 * PRE_LOADS)
                sp.dma_start(q[:].rearrange("p b c -> p (b c)"), A["q_s"].rearrange("b c -> (b c)").partition_broadcast(P)).then_inc(q_loaded, 16)

                for t, with_k, with_v in turns(sp):
                    if with_k:
                        if with_v:
                            sp.wait_ge(w_ready, t)
                        else:
                            sp.wait_ge(gate_c, 1)
                        sp.dma_start(kn[0:1, :], A["s_k"][bass.ds(t, 1), :]).then_inc(new_loaded, 16)
                    if with_v:
                        sp.wait_ge(pv_done, t)
                        sp.dma_start(vn[0:1, :], A["s_v"][bass.ds(t - 1, 1), :]).then_inc(vn_loaded, 16)
                    if with_k:
                        load(t + 1)
                sp.wait_ge(od_stored, 16 * H * BS)
                sp.dma_start(od[:], A["o_s"]).then_inc(od_loaded, 16)
                sp.wait_ge(dn_ready, 1)
                for b in range(BS):
                    sp.dma_start(A["mix"][LP + b, HW:2 * HW].rearrange("(h j) -> h j", h=H), od[b * H:(b + 1) * H, :]).then_inc(out_done, 16)
                sp.wait_ge(on_stored, 16 * TILES)
                sp.dma_start(A["p_gdn"].rearrange("h k v -> k h v"), S[:]).then_inc(out_done, 16)
                last = TILES - 1
                r0 = LP - last * P
                sp.dma_start(A["gates_s"][0], gu[r0:r0 + BS, last, :]).then_inc(out_done, 16)
                sp.dma_start(A["gates_s"][1], bu[r0:r0 + BS, last, :]).then_inc(out_done, 16)
                sp.wait_ge(out_done, 48 + 16 * BS)

            @block.gpsimd
            def _(pool):
                ch = Chain(pool, psteps, 6)
                pool.sem_inc(cs_used, 1)
                pool.sem_inc(z_used, 1)
                pool.sem_inc(k_used, RING)
                pool.sem_inc(v_used, RING)

                def multiply(t, i):
                    pool.wait_ge(k_loaded[i % RING], 16 * (CHUNKS // RING * t + i // RING + 1))
                    pool.sem_inc(waited, 1)
                    pool.tensor_tensor(keys[:, i % RING], keys[:, i % RING], bc(q[:, bass.ds(t, 1), :], P, CHUNK, HW), ALU.mult).then_inc(k_mult_pool, 1)

                def gather(cache, buf, index, picked, done, used, b, i):
                    step = CHUNKS * b + i
                    pool.wait_ge(used, step + 1)
                    pool.sem_inc(waited, 1)
                    pool.tensor_copy(index[:, i % RING, :], pages[:, bass.ds(step, 1)]).then_inc(picked, 1)
                    pool.wait_ge(picked, step + 1)
                    pool.sem_inc(waited, 1)
                    pool.indirect_dma_start(out=buf[:, i % RING, :, :].rearrange("p a c -> p (a c)"), out_offset=None,
                                            in_=A[cache].rearrange("g (l a) c -> (g l) (a c)", a=CHUNK),
                                            in_offset=bass.IndirectOffsetOnAxis(ap=index[:, i % RING, :], axis=0)).then_inc(done[i % RING], 16)

                def keys_of(t, i):
                    gather("cache_k", keys, k_index, k_picked, k_loaded, k_used, t, i)

                def values_of(t, i):
                    gather("cache_v", vals, v_index, v_picked, v_loaded, v_used, t, i)

                pool.sem_inc(on_free, 1)
                pool.wait_ge(c_loaded, 160)
                pool.wait_ge(gate_c, 1)
                conv = Chain(pool, pconv, 2)

                def conv_tap(t, i):
                    if i == 2:
                        conv.begin(t)
                        pool.wait_ge(in_loaded, 80 * (t + 1))
                    if i is None:
                        conv.sync()
                        conv.end()
                        pool.tensor_tensor(cs[:, 2, :], cs[:, 2, :], cs[:, 3, :], ALU.add).then_inc(conv23, 1)
                    else:
                        conv.done(pool.tensor_tensor(cs[:, i, :], cs[:, i, :], w_conv[:, i, :], ALU.mult))

                for i in (2, 3):
                    conv_tap(0, i)
                pool.wait_ge(pages_ready, 1)
                pool.wait_ge(q_loaded, 16)
                keys_of(0, 0)
                conv_tap(0, None)
                for i in range(1, RING):
                    keys_of(0, i)
                for t, with_k, with_v in turns(pool, BS - 1):
                    def refill_keys(*steps):
                        for i in steps:
                            if with_k:
                                keys_of(t, i + RING)

                    def refill_values(*steps):
                        for i in steps:
                            if with_v:
                                values_of(t - 1, i + RING)

                    def products(i):
                        if with_k:
                            multiply(t, i)

                    def taps(i):
                        if with_k:
                            conv_tap(t + 1, i)

                    ch.begin(t)
                    products(1)
                    refill_values(0, 1)
                    products(3)
                    refill_values(2, 3)
                    pool.wait_ge(eg_ready, t + 1)
                    pool.wait_ge(qk_ready, t + 1)
                    ch.done(pool.tensor_tensor(beg[:], beta[:, bass.ds(t, 1), :].rearrange("p t h -> p (t h)"), eg[:], ALU.mult))
                    ch.done(pool.tensor_tensor(vb[:], qkv[:, 2, :].rearrange("p (h j) -> p h j", h=H),
                                               bc(beta[:, bass.ds(t, 1), :].rearrange("p t (h o) -> p (t h) o", o=1), *HP), ALU.mult))
                    pool.wait_ge(d_ready, t + 1)
                    ch.link(pool.tensor_tensor(kw[:], qkv[:, 1, :].rearrange("p (h j) -> p h j", h=H),
                                               bc(egl[:].rearrange("p (h o) -> p h o", o=1), *HP), ALU.mult))
                    ch.link(pool.tensor_tensor(kbg[:], qkv[:, 1, :].rearrange("p (h j) -> p h j", h=H),
                                               bc(beg[:].rearrange("p (h o) -> p h o", o=1), *HP), ALU.mult))
                    pool.wait_ge(kqT_ready, t + 1)
                    pool.tensor_tensor(qgT[:], qT[:], egrow[:], ALU.mult).then_inc(operands, 1)
                    refill_keys(0, 1)
                    refill_values(4)
                    refill_keys(2)
                    products(5)
                    pool.wait_ge(zt_ready, t + 1)
                    ch.link(pool.tensor_tensor(zs[:], zt[:], z[:], ALU.mult))
                    ch.link(pool.tensor_tensor(zs[:], zs[:], z[:], ALU.add))
                    pool.sem_inc(z_used, 1)
                    ch.end()
                    refill_values(5)
                    refill_keys(3)
                    refill_values(6)
                    refill_keys(4)
                    products(7)
                    if with_v:
                        pool.wait_ge(on_stored, 16 * t)
                        pool.sem_inc(on_free, 1)
                    refill_values(7)
                    refill_keys(5)
                    taps(2)
                    refill_values(8)
                    refill_keys(6)
                    products(9)
                    refill_values(9)
                    taps(3)
                    refill_keys(7)
                    refill_values(10)
                    refill_keys(8, 9)
                    products(11)
                    refill_keys(10)
                    refill_values(11)
                    products(13)
                    refill_keys(11)
                    taps(None)
                    more_keys = with_k and (not isinstance(t, int) or t < BS - 1)
                    for i in range(RING):
                        if more_keys:
                            keys_of(t + 1, i)
                        if with_k:
                            values_of(t, i)
                    if with_k:
                        pool.wait_ge(m_ready, t + 1)
                        pool.sem_inc(waited, 1)
                        pool.partition_all_reduce(mx[:], m[:], P, bass.bass_isa.ReduceOp.max).then_inc(mx_ready, 1)
                        pool.wait_ge(l_ready, t + 1)
                        pool.sem_inc(waited, 1)
                        pool.partition_all_reduce(lt[:], l[:], P, bass.bass_isa.ReduceOp.add).then_inc(lt_ready, 1)
                    pool.wait_ge(on_ready, t + 1)
                    pool.dma_start(A["mix"][bass.ds(t * P, P), 0:HW], on[:].rearrange("p h j -> p (h j)")).then_inc(on_stored, 16)

            @block.scalar
            def _(act):
                act.wait_ge(c_loaded, 160)
                act.wait_ge(gate_a, 1)
                act.activation(ga[:], gc[:], ACT.Abs).then_inc(gate_a, 1)
                act.wait_ge(gate_a, 2)
                act.activation(gb[:], ga[:], ACT.Exp, scale=-1.0).then_inc(gate_a, 1)
                act.activation(a_log[:], a_log[:], ACT.Exp).then_inc(gate_a, 1)
                act.activation(bu[:], ab[:, :, H:2 * H], ACT.Exp, scale=-1.0).then_inc(gate_a, 1)
                act.wait_ge(gate_b, 1)
                act.activation(gb[:], gb[:], ACT.Ln).then_inc(gate_b, 1)
                act.sem_inc(od_clear, 1)
                act.wait_ge(lam_ready, 1)
                act.activation(lexp, lsum, ACT.Exp).then_inc(lam_ready, 1)
                for t, with_k, with_v in turns(act):
                    act.wait_ge(conv_ready, t + 1)
                    act.activation(th[:], cs[:, 0, :], ACT.Tanh).then_inc(th_ready, 1)
                    act.wait_ge(zs_ready, t + 1)
                    act.activation(zt[:], z[:], ACT.Tanh, scale=0.5).then_inc(zt_ready, 1)
                    act.wait_ge(g_ps, t + 1)
                    act.activation(eg[:], ps[:, 5, 0:H], ACT.Exp).then_inc(asteps, 1)
                    act.activation(gcol[:], ps[:, 5, 0:H], ACT.Copy).then_inc(asteps, 1)
                    act.activation(egrow[:], bank(1), ACT.Exp).then_inc(eg_ready, 1)
                    act.wait_ge(d_in, t + 1)
                    act.activation(egl[:], glg[:], ACT.Exp).then_inc(asteps, 1)
                    act.activation(dt[:], dt[:], ACT.Exp).then_inc(d_ready, 1)
                    act.wait_ge(qkT_ps, t + 1)
                    act.activation(kT[:], bank(3), ACT.Copy).then_inc(asteps, 1)
                    act.activation(qT[:], bank(4), ACT.Copy).then_inc(kqT_ready, 1)
                    act.wait_ge(w_ps, t + 1)
                    act.activation(nwT[:], bank(6), ACT.Copy, scale=-1.0).then_inc(nw_ready, 1)
                    act.wait_ge(u_ps, t + 1)
                    act.activation(u[:], bank(5), ACT.Copy).then_inc(u_ready, 1)
                    act.wait_ge(o_ps, t + 1)
                    act.activation(osq[:], bank(7), ACT.Square).then_inc(osq_ready, 1)
                    if with_k:
                        act.wait_ge(s_ready, t + 1)
                        act.activation(e[:], s[:], ACT.Exp, scale=DQ ** -0.5).then_inc(e_ready, 1)
                    if with_v:
                        act.wait_ge(pv_done, t + 1)
                        act.wait_ge(od_clear, t)
                        act.activation(o[:], ps[0:H, 0, :], ACT.Copy).then_inc(od_ready, 1)
                        act.wait_ge(od_ready, t + 1)
                        for h in range(H):
                            act.dma_start(A["o_s"][bass.ds((t - 1) * H + h, 1), :], o[h:h + 1, h * DV:(h + 1) * DV]).then_inc(od_stored, 16)
                        act.wait_ge(od_stored, 16 * H * t)
                        act.sem_inc(od_clear, 1)

            @block.vector
            def _(dve):
                v = nc.vector
                ch = Chain(dve, steps, DVE_GDN_STEPS)
                pre = Chain(dve, own("gd_gate_steps"), 0)
                dve.wait_ge(c_loaded, 160)
                v.tensor_tensor(gc[:], ab[:, :, 0:H], bc(dt_bias[:].rearrange("p (o h) -> p o h", o=1), P, TILES, H), ALU.add).then_inc(gate_a, 1)
                dve.wait_ge(gate_a, 5)
                pre.link(v.tensor_scalar(gc[:], gc[:], 0.0, None, ALU.max))
                v.tensor_scalar(gb[:], gb[:], 1.0, None, ALU.add).then_inc(gate_b, 1)
                pre.link(v.tensor_scalar(bu[:], bu[:], 1.0, None, ALU.add))
                pre.link(v.reciprocal(bu[:], bu[:]))
                pre.link(v.tensor_tensor(beta[:], bu[:], bc(rowmask[:].rearrange("p (t o) -> p t o", o=1), P, TILES, H), ALU.mult))
                dve.wait_ge(gate_b, 2)
                pre.link(v.tensor_tensor(gc[:], gc[:], gb[:], ALU.add))
                pre.link(v.scalar_tensor_tensor(gu[:], gc[:], -1.0, bc(a_log[:].rearrange("p (o h) -> p o h", o=1), P, TILES, H), ALU.mult, ALU.mult))
                pre.link(v.tensor_tensor(gate[:], gu[:], bc(rowmask[:].rearrange("p (t o) -> p t o", o=1), P, TILES, H), ALU.mult))
                pre.link(v.tensor_scalar(w_conv[:], w_conv[:], 0.5, None, ALU.mult))
                pre.link(v.tensor_scalar(w_gn[:], w_gn[:], 0.5, None, ALU.mult))
                pre.link(v.memset(kn[:], 0.0))
                pre.link(v.memset(vn[:], 0.0))
                v.memset(S[:], 0.0).then_inc(gate_c, 1)
                dve.wait_ge(pre_loaded, 16 * PRE_LOADS)
                v.scalar_tensor_tensor(pages[:], pages[:], P // CHUNK, lane[:], ALU.mult, ALU.add).then_inc(pages_ready, 1)
                pre.link(v.tensor_tensor(lprod, lams[:, 0:2, :], lams[:, 2:4, :], ALU.mult))
                v.tensor_reduce(lsum, lprod, AX_X, ALU.add).then_inc(lam_ready, 1)
                x = qk_s.rearrange("p (c j) -> p c j", j=DQ)
                x1, x2 = x[:, :, 0:HALF], x[:, :, HALF:2 * HALF]
                cb, sb_ = (bc(a.rearrange("p (o j) -> p o j", o=1), BS, 16, HALF) for a in (cos, sin))
                pre.done(v.tensor_tensor(rot[:, 0], x1, cb, ALU.mult))
                pre.done(v.tensor_tensor(rot[:, 1], x2, sb_, ALU.mult))
                pre.done(v.tensor_tensor(rot[:, 2], x2, cb, ALU.mult))
                pre.link(v.tensor_tensor(rot[:, 3], x1, sb_, ALU.mult))
                pre.done(v.tensor_tensor(x1, rot[:, 0], rot[:, 1], ALU.subtract))
                v.tensor_tensor(x2, rot[:, 2], rot[:, 3], ALU.add).then_inc(rot_ready, 1)
                dve.wait_ge(lam_ready, 2)
                pre.done(v.memset(coef[:, 0:1], 1.0))
                pre.link(v.tensor_tensor(coef[:, 1:2], lexp[:, 1:2], lexp[:, 0:1], ALU.subtract))
                v.tensor_scalar(coef[:, 1:2], coef[:, 1:2], -LAM_INIT, None, ALU.add).then_inc(lam_ready, 1)
                dve.wait_ge(lam_ready, 3)
                dve.wait_ge(gate_c, 1)
                dve.sem_inc(zs_ready, 1)

                MINE = CHUNKS // 2 + 1

                def keys_times_query(t, i):
                    dve.wait_ge(k_loaded[i % RING], 16 * (CHUNKS // RING * t + i // RING + 1))
                    v.tensor_tensor(keys[:, i % RING], keys[:, i % RING], bc(q[:, bass.ds(t, 1), :], P, CHUNK, HW), ALU.mult).then_inc(k_mult, 1)

                def score(t, i):
                    if i % 2 and i < CHUNKS - 1:
                        dve.wait_ge(k_mult_pool, (CHUNKS - MINE) * t + i // 2 + 1)
                    else:
                        dve.wait_ge(k_mult, MINE * t + (i + 1) // 2 + 1)
                    v.tensor_reduce(s[:, CHUNK * i:CHUNK * (i + 1), :], keys[:, i % RING].rearrange("p a (c j) -> p a c j", j=DQ), AX_X, ALU.add).then_inc(k_used, 1)

                for t, with_k, with_v in turns(dve):
                    base = D_STEPS * t
                    ch.begin(t)
                    dve.wait_ge(in_loaded, 80 * (t + 1))
                    ch.done(v.tensor_tensor(cs[:, 0, :], cs[:, 0, :], w_conv[:, 0, :], ALU.mult))
                    ch.link(v.tensor_tensor(cs[:, 1, :], cs[:, 1, :], w_conv[:, 1, :], ALU.mult))
                    ch.link(v.tensor_tensor(cs[:, 0, :], cs[:, 0, :], cs[:, 1, :], ALU.add))
                    dve.wait_ge(conv23, t + 1)
                    v.tensor_tensor(cs[:, 0, :], cs[:, 0, :], cs[:, 2, :], ALU.add).then_inc(conv_ready, 1)
                    if with_k:
                        if not with_v:
                            dve.wait_ge(q_loaded, 16)
                        keys_times_query(t, 0)
                    gt = gate[:, bass.ds(t, 1), :].rearrange("p t (h o) -> p (t h) o", o=1)
                    bt = beta[:, bass.ds(t, 1), :].rearrange("p t (h o) -> p (t h) o", o=1)
                    ch.done(v.tensor_tensor(ug[:], bc(upper[:].rearrange("p (o j) -> p o j", o=1), *HP), bc(gt, *HP), ALU.mult))
                    v.tensor_tensor(ib[:], bc(ident[:].rearrange("p (o j) -> p o j", o=1), *HP), bc(bt, *HP), ALU.mult).then_inc(ug_ready, 1)
                    dve.wait_ge(th_ready, t + 1)
                    qk = qkv[:, 0:2, :].rearrange("p a (h j) -> p (a h) j", h=H)
                    sq = th[:, 0:2 * HW].rearrange("p (h j) -> p h j", j=P)
                    ch.link(v.scalar_tensor_tensor(qkv[:].rearrange("p a j -> p (a j)"), th[:], 1.0, cs[:, 0, :], ALU.add, ALU.mult))
                    dve.sem_inc(cs_used, 1)
                    ch.link(v.tensor_tensor(sq, qk, qk, ALU.mult))
                    ch.link(v.tensor_reduce(ss[:], sq, AX_X, ALU.add))
                    rsqrt(nc, ch, rn[:], ss[:], rt[:], 1.0, EPS)
                    ch.link(v.tensor_scalar(rn[:, 0:H], rn[:, 0:H], DK ** -0.5, None, ALU.mult))
                    v.tensor_tensor(qk, qk, bc(rn[:].rearrange("p (h o) -> p h o", o=1), P, 2 * H, P), ALU.mult).then_inc(qk_ready, 1)
                    dve.wait_ge(eg_ready, t + 1)
                    gcb = bc(gcol[:].rearrange("p (h o) -> p h o", o=1), *HP)
                    ch.done(v.tensor_tensor(glg[:].rearrange("p (h o) -> p h o", o=1), bank(1)[:, :, P - 1:P], gcol[:].rearrange("p (h o) -> p h o", o=1), ALU.subtract))
                    ch.link(v.tensor_tensor(dt[:], bank(1), gcb, ALU.subtract))
                    v.tensor_scalar(dt[:], dt[:], 0.0, None, ALU.min).then_inc(d_in, 1)
                    if with_k:
                        score(t, 0)
                        score(t, 1)
                    dve.wait_ge(d_ready, t + 1)
                    ch.link(v.tensor_tensor(dt[:], dt[:], bc(upper[:].rearrange("p (o j) -> p o j", o=1), *HP), ALU.mult))
                    idb = ident[:].rearrange("p (o j) -> p o j", o=1)
                    ch.done(v.tensor_copy(TT[:].rearrange("p a h j -> p (a h) j"), bc(idb, P, 2 * H, P)))
                    if with_k:
                        keys_times_query(t, 2)
                        score(t, 2)
                    dve.wait_ge(kk_ps, t + 1)
                    ch.done(v.tensor_tensor(qkT[:], bank(6), dt[:], ALU.mult))
                    ch.link(v.tensor_tensor(LT[:], bank(5), dt[:], ALU.mult))
                    v.tensor_tensor(LT[:], LT[:], bank(2), ALU.mult).then_inc(t_ready, 1)
                    for lev in range(7):
                        dve.wait_ge(p_ps, 7 * t + lev + 1)
                        v.tensor_tensor(prod[:], bank(7), bc(levels[:, lev:lev + 1, :], *HP), ALU.mult).then_inc(p_ready, 1)
                        if with_k:
                            score(t, lev + 3)
                        dve.wait_ge(dT_ps, 7 * t + lev + 1)
                        v.tensor_tensor(TT[:].rearrange("p a h j -> p a (h j)"), TT[:].rearrange("p a h j -> p a (h j)"), ps[:, 3:5, :], ALU.subtract).then_inc(t_ready, 1)
                        if with_k and lev % 2 == 0:
                            keys_times_query(t, lev + 4)
                    if with_k:
                        for i in range(10, CHUNKS):
                            if (i % 2 == 0 and i > 10) or i == CHUNKS - 1:
                                keys_times_query(t, i)
                            score(t, i)
                        dve.wait_ge(new_loaded, 16 * (t + 1))
                        v.tensor_tensor(kn[:], kn[:], q[:, bass.ds(t, 1), :].rearrange("p b c -> p (b c)"), ALU.mult).then_inc(dsteps, 1)
                        dve.wait_ge(dsteps, base + 1)
                        v.tensor_reduce(s[:, N_PAGES, :], kn[:].rearrange("p (c j) -> p c j", j=DQ), AX_X, ALU.add).then_inc(dsteps, 1)
                        dve.wait_ge(dsteps, base + 2)
                        v.tensor_scalar(s[:, N_PAGES, :], s[:, N_PAGES, :], first[:], None, ALU.add).then_inc(dsteps, 1)
                        dve.wait_ge(dsteps, base + 3)
                        dve.wait_ge(k_used, CHUNKS * (t + 1) + RING)
                        v.tensor_reduce(m[:], s[:].rearrange("p g c -> p c g"), AX_X, ALU.max).then_inc(m_ready, 1)
                    dve.wait_ge(o_ps, t + 1)
                    for h in range(H):
                        ch.done(v.scalar_tensor_tensor(S[:, h, :], S[:, h, :], egrow[:, h, P - 1:P], bank(3)[:, h, :], ALU.mult, ALU.add))
                    dve.wait_ge(osq_ready, t + 1)
                    ch.link(v.tensor_reduce(ss[:, 0:H], osq[:], AX_X, ALU.add))
                    rsqrt(nc, ch, rn[:, 0:H], ss[:, 0:H], rt[:, 0:H], 1.0 / DV, EPS)
                    if with_k:
                        dve.wait_ge(mx_ready, t + 1)
                        v.tensor_tensor(s[:], s[:], bc(mx[:].rearrange("p (o c) -> p o c", o=1), P, NP1, C), ALU.subtract).then_inc(s_ready, 1)
                    dve.wait_ge(on_free, t + 1)
                    ch.link(v.tensor_tensor(on[:], bank(7), bc(rn[:, 0:H].rearrange("p (h o) -> p h o", o=1), *HP), ALU.mult))
                    ch.link(v.tensor_tensor(on[:], on[:], bc(w_gn[:].rearrange("p (o j) -> p o j", o=1), *HP), ALU.mult))
                    dve.wait_ge(psteps, 6 * t + 6)
                    v.tensor_tensor(on[:].rearrange("p h j -> p (h j)"), on[:].rearrange("p h j -> p (h j)"), zs[:], ALU.mult).then_inc(on_ready, 1)
                    ch.end()
                    dve.sem_inc(zs_ready, 1)
                    if not with_k:
                        continue
                    dve.wait_ge(e_ready, t + 1)
                    v.tensor_reduce(l[:], e[:].rearrange("p g c -> p c g"), AX_X, ALU.add).then_inc(l_ready, 1)
                    dve.wait_ge(lt_ready, t + 1)
                    v.reciprocal(r[:], lt[:]).then_inc(dsteps, 1)
                    dve.wait_ge(dsteps, base + 4)
                    v.tensor_tensor(r[:].rearrange("p (h c) -> p h c", c=2), r[:].rearrange("p (h c) -> p h c", c=2), bc(coef[:].rearrange("p (o c) -> p o c", o=1), P, H, 2), ALU.mult).then_inc(dsteps, 1)
                    dve.wait_ge(dsteps, base + 5)
                    v.tensor_tensor(e[:], e[:], bc(r[:].rearrange("p (o c) -> p o c", o=1), P, NP1, C), ALU.mult).then_inc(dsteps, 1)
                    dve.wait_ge(dsteps, base + 6)
                    dve.wait_ge(pv_done, t + 1)
                    e2 = e[:].rearrange("p g (h c) -> p g h c", c=2)
                    v.tensor_tensor(w[:], e2[:, :, :, 0], e2[:, :, :, 1], ALU.add).then_inc(w_ready, 1)
                fin = Chain(dve, own("de_final"), 0)
                dve.wait_ge(od_loaded, 16)
                fin.link(v.tensor_tensor(dsq[:], od[:], od[:], ALU.mult))
                fin.link(v.tensor_reduce(s1[:], dsq[:], AX_X, ALU.add))
                rsqrt(nc, fin, r1[:], s1[:], r2[:], 1.0 / DV, EPS, times=1.0 - LAM_INIT)
                v.scalar_tensor_tensor(od[:], od[:], r1[:], w_sub[:], ALU.mult, ALU.mult).then_inc(dn_ready, 1)

            @block.tensor
            def _(pe):
                pe.wait_ge(c_loaded, 160)
                pe.sem_inc(pv_done, 1)
                pe.sem_inc(od_ready, 1)
                pe.wait_ge(pre_stored, 48)

                def weigh(t, c0, c1):
                    if c0 == 0:
                        pe.wait_ge(w_ready, t)
                        pe.wait_ge(od_ready, t)
                    for g in range(int(c0 * CHUNK), int(c1 * CHUNK)):
                        c, j = g // CHUNK, g % CHUNK
                        if j == 0:
                            pe.wait_ge(v_loaded[c % RING], 16 * (CHUNKS // RING * (t - 1) + c // RING + 1))
                        last = pe.matmul(ps[0:H, 0, :], w[:, g, :], vals[:, c % RING, j, :], start=(g == 0), stop=False)
                        if j == CHUNK - 1:
                            last.then_inc(v_used, 1)
                    if c1 == CHUNKS:
                        pe.wait_ge(vn_loaded, 16 * t)
                        pe.matmul(ps[0:H, 0, :], w[:, N_PAGES, :], vn[:], start=False, stop=True).then_inc(pv_done, 1)

                for t, with_k, with_v in turns(pe):
                    if with_v:
                        weigh(t, 0, 2)
                    pe.wait_ge(ug_ready, t + 1)
                    pe.wait_ge(gate_c, 1)
                    pe.matmul(ps[:, 5, 0:H], upper[:], gate[:, bass.ds(t, 1), :].rearrange("p t h -> p (t h)"), start=True, stop=True)
                    pe.matmul(ps[:, 1, :], ones[:], ug[:].rearrange("p h j -> p (h j)"), start=True, stop=True)
                    pe.matmul(ps[:, 2, :], ones[:], ib[:].rearrange("p h j -> p (h j)"), start=True, stop=True).then_inc(g_ps, 1)
                    if with_v:
                        weigh(t, 2, 4)
                    pe.wait_ge(qk_ready, t + 1)
                    for h in range(H):
                        pe.transpose(bank(3)[:, h, :], qkv[:, 1, h * P:(h + 1) * P], ident[:])
                    for h in range(H):
                        last = pe.transpose(bank(4)[:, h, :], qkv[:, 0, h * P:(h + 1) * P], ident[:])
                    last.then_inc(qkT_ps, 1)
                    pe.wait_ge(kqT_ready, t + 1)
                    for h in range(H):
                        pe.matmul(bank(5)[:, h, :], kT[:, h, :], kT[:, h, :], start=True, stop=True)
                    for h in range(H):
                        last = pe.matmul(bank(6)[:, h, :], kT[:, h, :], qT[:, h, :], start=True, stop=True)
                    last.then_inc(kk_ps, 1)
                    if with_v:
                        weigh(t, 4, 5)
                    for lev in range(7):
                        pe.wait_ge(t_ready, 8 * t + lev + 1)
                        for h in range(H):
                            last = pe.matmul(bank(7)[:, h, :], LT[:, h, :], TT[:, 0, h, :], start=True, stop=True)
                        last.then_inc(p_ps, 1)
                        if with_v:
                            weigh(t, 5 + lev, 5.5 + lev)
                        pe.wait_ge(p_ready, 7 * t + lev + 1)
                        for h in range(H):
                            pe.matmul(bank(3)[:, h, :], TT[:, 1, h, :], prod[:, h, :], start=True, stop=True)
                            last = pe.matmul(bank(4)[:, h, :], prod[:, h, :], TT[:, 1, h, :], start=True, stop=True)
                        last.then_inc(dT_ps, 1)
                        if with_v:
                            weigh(t, 5.5 + lev, 6 + lev)
                    pe.wait_ge(t_ready, 8 * t + 8)
                    pe.wait_ge(operands, t + 1)
                    for h in range(H):
                        last = pe.matmul(bank(6)[:, h, :], kbg[:, h, :], TT[:, 1, h, :], start=True, stop=True)
                    last.then_inc(w_ps, 1)
                    if with_v:
                        weigh(t, 12, 12.5)
                    pe.wait_ge(nw_ready, t + 1)
                    for h in range(H):
                        pe.matmul(bank(5)[:, h, :], TT[:, 1, h, :], vb[:, h, :], start=True, stop=False)
                        last = pe.matmul(bank(5)[:, h, :], nwT[:, h, :], S[:, h, :], start=False, stop=True)
                    last.then_inc(u_ps, 1)
                    for h in range(H):
                        pe.matmul(bank(7)[:, h, :], qgT[:, h, :], S[:, h, :], start=True, stop=False)
                        if h == 0:
                            pe.wait_ge(u_ready, t + 1)
                        pe.matmul(bank(7)[:, h, :], qkT[:, h, :], u[:, h, :], start=False, stop=True)
                    for h in range(H):
                        last = pe.matmul(bank(3)[:, h, :], kw[:, h, :], u[:, h, :], start=True, stop=True)
                    last.then_inc(o_ps, 1)
                    if with_v:
                        weigh(t, 12.5, CHUNKS)


DVE_GDN_STEPS = 45
D_STEPS = 6


def phase_sample_gdn(nc, ps, A, keep, all_qk, vals):
    N = BS * H
    with ExitStack() as ctx, own_semaphores(nc) as own:
        def sb(n, s, d=F32):
            return ctx.enter_context(nc.sbuf_tensor("sg_" + n, s, d))

        def sem(n):
            return own("sg_" + n)

        ident, ones = sb("ident", [P, P]), sb("ones", [P, P])
        state = sb("state", [P, N, DV])
        taps, w_conv = sb("taps", [BS, CONV_W, CONV_CH]), sb("w_conv", [BS, CONV_W, CONV_CH])
        th, qkv, sq = sb("th", [BS, CONV_CH]), sb("qkv", [BS, 3, H * DK]), sb("sq", [BS, 8, DK])
        ss, rn, rt = sb("ss", [BS, 8]), sb("rn", [BS, 8]), sb("rt", [BS, 8])
        z, zt, zg, w_gn = sb("z", [N, DV]), sb("zt", [N, DV]), sb("zg", [N, DV]), sb("w_gn", [N, DV])
        gate, beta, eg = sb("gate", [N, 1]), sb("beta", [N, 1]), sb("eg", [N, 1])
        rows = sb("rows", [N, 3, DK])
        kq = sb("kq", [P, N, 2])
        qk = sb("qk", [N, 1])
        diag, eb = sb("diag", [N, N]), sb("eb", [P, N])
        colT, u, spread = sb("colT", [P, 2, N]), sb("u", [N, DV]), sb("spread", [N, N, DV])
        o, osq = sb("o", [N, DV]), sb("osq", [N, DV])
        s1, r1, r2 = sb("s1", [N, 1]), sb("r1", [N, 1]), sb("r2", [N, 1])
        loaded, rows_out, rows_in = sem("loaded"), sem("rows_out"), sem("rows_in")
        steps, conv_ready, th_ready, qkv_ready = sem("steps"), sem("conv_ready"), sem("th_ready"), sem("qkv_ready")
        eg_ready, zt_ready, diag_ready = sem("eg_ready"), sem("zt_ready"), sem("diag_ready")
        turned, turned_sb, ks_ps, ks_sb, ks_row = sem("turned"), sem("turned_sb"), sem("ks_ps"), sem("ks_sb"), sem("ks_row")
        u_ready, outer, state_ready = sem("u_ready"), sem("outer"), sem("state_ready")
        cos, sin = sb("cos", [P, TILES, HALF]), sb("sin", [P, TILES, HALF])
        rot = sb("rot", [P, 4, TILES, 16, HALF])
        qk_loaded, v_loaded, rotated = sem("qk_loaded"), sem("v_loaded"), sem("rotated")
        s_loaded, o_ready, stored = sem("s_loaded"), sem("o_ready"), sem("stored")
        LOADS = 8 + BS
        row0 = CONV_W - 1 + LP

        with nc.Block() as block:
            @block.sync
            def _(sp):
                n = 0
                for dst, src in [(taps[:, 0:CONV_W - 1, :], A["state_conv"]),
                                 (taps[:, CONV_W - 1, :], A["proj"][row0:row0 + BS, 0:CONV_CH]),
                                 (w_conv[:].rearrange("p i c -> p (i c)"), A["w_conv"].rearrange("i c -> (i c)").partition_broadcast(BS)),
                                 (gate[:], A["gates_s"][0].rearrange("b (h o) -> (b h) o", o=1)),
                                 (beta[:], A["gates_s"][1].rearrange("b (h o) -> (b h) o", o=1)),
                                 (w_gn[:], A["w_gnorm"].partition_broadcast(N)),
                                 (ident[:], A["ident"]), (ones[:], A["ones"])]:
                    sp.dma_start(dst, src).then_inc(loaded, 16)
                for b in range(BS):
                    sp.dma_start(z[b * H:(b + 1) * H, :], A["proj"][row0 + b, C_Z:C_Z + H * DV].rearrange("(h j) -> h j", h=H)).then_inc(loaded, 16)
                sp.dma_start(state[:], A["state_gdn"].rearrange("i k v -> k i v")).then_inc(s_loaded, 16)
                all_rows = A["proj"][CONV_W - 1:CONV_W - 1 + RPAD, :].rearrange("(t p) c -> p t c", p=P)
                for dst, src in [(cos[:], A["cos"]), (sin[:], A["sin"]), (all_qk[:], all_rows[:, :, C_DQ:C_DQ + 2 * H * DV])]:
                    sp.dma_start(dst, src).then_inc(qk_loaded, 16)
                sp.dma_start(vals[:], all_rows[:, :, C_DV:C_DV + H * DV]).then_inc(v_loaded, 16)
                sp.dma_start(A["s_conv"][:, 0:CONV_W - 2, :], A["state_conv"][:, 1:CONV_W - 1, :]).then_inc(stored, 16)
                sp.dma_start(A["s_conv"][:, CONV_W - 2, :], A["proj"][row0:row0 + BS, 0:CONV_CH]).then_inc(stored, 16)
                sp.dma_start(A["p_conv"], A["proj"][row0 - (CONV_W - 1):row0, 0:CONV_CH]).then_inc(stored, 16)
                sp.wait_ge(qkv_ready, 2)
                sp.dma_start(A["rows_s"].rearrange("a b c -> b a c"), qkv[:]).then_inc(rows_out, 16)
                sp.wait_ge(rows_out, 16)
                sp.dma_start(rows[:], A["rows_s"].rearrange("a b (h j) -> (b h) a j", h=H)).then_inc(rows_in, 16)
                sp.wait_ge(o_ready, 1)
                for b in range(BS):
                    sp.dma_start(A["mix"][LP + b, 0:H * DV].rearrange("(h j) -> h j", h=H), o[b * H:(b + 1) * H, :]).then_inc(stored, 16)
                for i in range(2):
                    sp.wait_ge(state_ready, 2 * i + 2)
                    sp.dma_start(A["s_gdn"][i * N // 2:(i + 1) * N // 2].rearrange("i k v -> k i v"), state[:, i * N // 2:(i + 1) * N // 2, :]).then_inc(stored, 16)
                sp.wait_ge(s_loaded, 16)
                sp.wait_ge(v_loaded, 16)
                sp.wait_ge(rotated, 1)
                sp.wait_ge(stored, 16 * (5 + BS))

            @block.scalar
            def _(act):
                act.wait_ge(loaded, 16 * LOADS)
                act.activation(eg[:], gate[:], ACT.Exp).then_inc(eg_ready, 1)
                act.activation(zt[:], z[:], ACT.Tanh, scale=0.5).then_inc(zt_ready, 1)
                act.wait_ge(conv_ready, 1)
                act.activation(th[:], taps[:, 0, :], ACT.Tanh, scale=0.5).then_inc(th_ready, 1)
                act.wait_ge(turned, 1)
                act.activation(kq[:, :, 0], ps[:, 0, 0:N], ACT.Copy).then_inc(turned_sb, 1)
                act.activation(kq[:, :, 1], ps[:, 1, 0:N], ACT.Copy).then_inc(turned_sb, 1)
                act.wait_ge(diag_ready, 2)
                act.activation(eb[:], ps[:, 2, 0:N], ACT.Copy).then_inc(turned_sb, 1)
                act.wait_ge(ks_ps, 1)
                act.activation(colT[:], ps[:, 3, 0:2 * N].rearrange("p (i c) -> p c i", c=2), ACT.Copy).then_inc(ks_sb, 1)

            @block.vector
            def _(dve):
                v = nc.vector
                ch = Chain(dve, steps, 0)
                dve.wait_ge(loaded, 16 * LOADS)
                ch.link(v.tensor_tensor(taps[:], taps[:], w_conv[:], ALU.mult))
                ch.link(v.tensor_tensor(taps[:, 0:2, :], taps[:, 0:2, :], taps[:, 2:4, :], ALU.add))
                v.tensor_tensor(taps[:, 0, :], taps[:, 0, :], taps[:, 1, :], ALU.add).then_inc(conv_ready, 1)
                dve.wait_ge(th_ready, 1)
                ch.link(v.scalar_tensor_tensor(qkv[:].rearrange("p a j -> p (a j)"), th[:], 1.0, taps[:, 0, :], ALU.add, ALU.mult))
                v.tensor_scalar(qkv[:], qkv[:], 0.5, None, ALU.mult).then_inc(qkv_ready, 1)
                dve.wait_ge(qkv_ready, 1)
                qk_rows = qkv[:, 0:2, :].rearrange("p a (h j) -> p (a h) j", h=H)
                ch.link(v.tensor_tensor(sq[:], qk_rows, qk_rows, ALU.mult))
                ch.link(v.tensor_reduce(ss[:], sq[:], AX_X, ALU.add))
                rsqrt(nc, ch, rn[:], ss[:], rt[:], 1.0, EPS)
                ch.link(v.tensor_scalar(rn[:, 0:H], rn[:, 0:H], DK ** -0.5, None, ALU.mult))
                v.tensor_tensor(qk_rows, qk_rows, bc(rn[:].rearrange("p (h o) -> p h o", o=1), BS, 2 * H, DK), ALU.mult).then_inc(qkv_ready, 1)
                dve.wait_ge(eg_ready, 1)
                dve.wait_ge(zt_ready, 1)
                v.tensor_scalar(diag[:], ident[0:N, 0:N], eg[:], None, ALU.mult).then_inc(diag_ready, 1)
                ch.done(v.tensor_scalar(osq[:], zt[:], 1.0, None, ALU.add))
                ch.link(v.tensor_tensor(zg[:], z[:], w_gn[:], ALU.mult))
                ch.link(v.tensor_tensor(zg[:], zg[:], osq[:], ALU.mult))
                dve.wait_ge(qk_loaded, 48)
                x = all_qk[:].rearrange("p t (c j) -> p t c j", j=DQ)
                x1, x2 = x[:, :, :, 0:HALF], x[:, :, :, HALF:2 * HALF]
                sh = (P, TILES, 16, HALF)
                cb, sb_ = (bc(a[:].rearrange("p t (o j) -> p t o j", o=1), *sh) for a in (cos, sin))
                ch.done(v.tensor_tensor(rot[:, 0], x1, cb, ALU.mult))
                ch.done(v.tensor_tensor(rot[:, 1], x2, sb_, ALU.mult))
                ch.done(v.tensor_tensor(rot[:, 2], x2, cb, ALU.mult))
                ch.link(v.tensor_tensor(rot[:, 3], x1, sb_, ALU.mult))
                ch.done(v.tensor_tensor(x1, rot[:, 0], rot[:, 1], ALU.subtract))
                v.tensor_tensor(x2, rot[:, 2], rot[:, 3], ALU.add).then_inc(rotated, 1)
                dve.wait_ge(rows_in, 16)
                ch.link(v.tensor_tensor(osq[:], rows[:, 0, :], rows[:, 1, :], ALU.mult))
                ch.link(v.tensor_reduce(qk[:], osq[:], AX_X, ALU.add))
                dve.wait_ge(ks_row, 1)
                ch.done(v.tensor_scalar(o[:], ps[0:N, 4, P:P + DV], eg[:], None, ALU.mult))
                ch.link(v.tensor_scalar(u[:], ps[0:N, 4, 0:DV], eg[:], None, ALU.mult))
                ch.link(v.tensor_tensor(u[:], rows[:, 2, :], u[:], ALU.subtract))
                ch.link(v.tensor_scalar(u[:], u[:], beta[:], None, ALU.mult))
                v.tensor_tensor(spread[:], bc(ident[0:N, 0:N].rearrange("p (i o) -> p i o", o=1), N, N, DV),
                                bc(u[:].rearrange("p (o j) -> p o j", o=1), N, N, DV), ALU.mult).then_inc(u_ready, 1)
                dve.wait_ge(turned_sb, 3)
                ch.link(v.tensor_tensor(state[:], state[:], bc(eb[:].rearrange("p (i o) -> p i o", o=1), P, N, DV), ALU.mult))
                ch.link(v.scalar_tensor_tensor(o[:], u[:], qk[:], o[:], ALU.mult, ALU.add))
                for i in range(4):
                    dve.wait_ge(outer, 2 * i + 2)
                    part = state[:, i * N // 4:(i + 1) * N // 4, :].rearrange("p (c i) j -> p c (i j)", c=2)
                    v.tensor_tensor(part, part, ps[:, 2 * i:2 * i + 2, :], ALU.add).then_inc(state_ready, 1)
                    if i == 0:
                        ch.link(v.tensor_tensor(osq[:], o[:], o[:], ALU.mult))
                        ch.link(v.tensor_reduce(s1[:], osq[:], AX_X, ALU.add))
                        rsqrt(nc, ch, r1[:], s1[:], r2[:], 1.0 / DV, EPS, times=0.5)
                        v.scalar_tensor_tensor(o[:], o[:], r1[:], zg[:], ALU.mult, ALU.mult).then_inc(o_ready, 1)

            @block.tensor
            def _(pe):
                pe.wait_ge(loaded, 16 * LOADS)
                pe.wait_ge(rows_in, 16)
                pe.transpose(ps[:, 0, 0:N], rows[:, 1, :], ident[0:N, 0:N])
                pe.transpose(ps[:, 1, 0:N], rows[:, 0, :], ident[0:N, 0:N]).then_inc(turned, 1)
                pe.wait_ge(diag_ready, 1)
                pe.matmul(ps[:, 2, 0:N], ones[0:N, :], diag[:], start=True, stop=True).then_inc(diag_ready, 1)
                pe.wait_ge(turned_sb, 2)
                pe.wait_ge(s_loaded, 16)
                for i in range(N):
                    last = pe.matmul(ps[:, 3, 2 * i:2 * i + 2], state[:, i, :], kq[:, i, :], start=True, stop=True)
                last.then_inc(ks_ps, 1)
                pe.wait_ge(ks_sb, 1)
                for c in range(2):
                    last = pe.transpose(ps[0:N, 4, c * P:(c + 1) * P], colT[:, c, :], ident[:])
                last.then_inc(ks_row, 1)
                pe.wait_ge(u_ready, 1)
                pe.wait_ge(turned_sb, 3)
                for c in range(8):
                    pe.matmul(ps[:, c, :], rows[:, 1, :], spread[:, 4 * c:4 * c + 4, :].rearrange("p i j -> p (i j)"), start=True, stop=True).then_inc(outer, 1)


def phase_attention(nc, ps, A, keep, qk, vals, w_out):
    with ExitStack() as ctx, own_semaphores(nc) as own:
        def sb(n, s, d=F32):
            return ctx.enter_context(nc.sbuf_tensor("at_" + n, s, d))

        def sem(n):
            return own("at_" + n)

        HW = H * DV
        ident, causal = sb("ident", [P, P]), sb("causal", [P, P])
        coef = sb("coef", [P, 2])
        w_sub = sb("w_sub", [P, DV])
        KT, qT = sb("KT", [P, H, RPAD]), sb("qT", [P, H, RPAD])
        prob, w = sb("prob", [P, 2, RPAD]), sb("w", [P, 2, RPAD])
        wT = sb("wT", [P, 2, 4 * P])
        nmax, sums, rcp = sb("nmax", [P, 2]), sb("sums", [P, 2]), sb("rcp", [P, 2])
        av, osq, ao = sb("av", [P, H, DV]), sb("osq", [P, H, DV]), sb("ao", [P, 2, H, DV])
        ss, rn, rt = sb("ss", [P, H]), sb("rn", [P, H]), sb("rt", [P, H])
        loaded, steps = sem("loaded"), sem("steps")
        kq_ps, kT_ready, qT_ready, w_loaded = sem("kq_ps"), sem("kT_ready"), sem("qT_ready"), sem("w_loaded")
        s_ps, max_ready, e_ready, w_ready = sem("s_ps"), sem("max_ready"), sem("e_ready"), sem("w_ready")
        av_copied = sem("av_copied")
        wT_ps, wT_ready, av_ps, osq_ready = sem("wT_ps"), sem("wT_ready"), sem("av_ps"), sem("osq_ready")
        ao_ready, ao_stored, stored = sem("ao_ready"), [sem("ao_stored0"), sem("ao_stored1")], sem("stored")
        flat = ps[:].rearrange("p b j -> p (b j)")
        units = [(t, h) for t in range(TILES) for h in range(H)]
        groups = [[(j, min(j + 4, t + 1)) for j in range(0, t + 1, 4)] for t, h in units]
        group_no = [sum(len(g) for g in groups[:n]) for n in range(len(units))]

        def turn_banks(t):
            return 2 * (t % 4)

        def score_columns(c, k0, k1):
            return flat[:, c * 1536 + k0:c * 1536 + k1]

        last_tile = TILES - 1
        tail = LP - last_tile * P

        with nc.Block() as block:
            @block.sync
            def _(sp):
                for dst, src in [(ident[:], A["ident"]), (causal[:], A["causal"]),
                                 (w_sub[:], A["w_subln"].partition_broadcast(P)), (coef[:], A["coef"])]:
                    sp.dma_start(dst, src).then_inc(loaded, 16)
                sp.dma_start(w_out[:], A["w_out"].rearrange("(c p) n -> p c n", p=P)).then_inc(w_loaded, 16)
                for dst, src in [(A["p_k"][0:last_tile * P, :].rearrange("(t p) c -> p t c", p=P), qk[:, 0:last_tile, HW:2 * HW]),
                                 (A["p_v"][0:last_tile * P, :].rearrange("(t p) c -> p t c", p=P), vals[:, 0:last_tile, :]),
                                 (A["p_k"][last_tile * P:LP, :], qk[0:tail, last_tile, HW:2 * HW]),
                                 (A["p_v"][last_tile * P:LP, :], vals[0:tail, last_tile, :])]:
                    sp.dma_start(dst, src).then_inc(stored, 16)
                for t in range(TILES):
                    sp.wait_ge(ao_ready, t + 1)
                    for r0, r1 in ((0, P),) if t < last_tile else ((0, tail), (tail + BS, P)):
                        sp.dma_start(A["mix"][t * P + r0:t * P + r1, HW:2 * HW], ao[r0:r1, t % 2, :, :].rearrange("p h j -> p (h j)")).then_inc(ao_stored[t % 2], 16)
                sp.wait_ge(ao_stored[0], 16 * ((TILES + 1) // 2 + 1))
                sp.wait_ge(ao_stored[1], 16 * (TILES // 2))
                sp.wait_ge(w_loaded, 16)
                sp.wait_ge(stored, 16 * 4)

            @block.scalar
            def _(act):
                act.wait_ge(loaded, 16 * 4)

                def exp(n, c):
                    t, h = units[n]
                    wd = (t + 1) * P
                    act.wait_ge(max_ready, 2 * n + c + 1)
                    if n:
                        act.wait_ge(w_ready, n)
                    act.activation(prob[:, c, 0:wd], score_columns(c, 0, wd), ACT.Exp, bias=nmax[:, c:c + 1],
                                   accum_out=sums[:, c:c + 1]).then_inc(e_ready, 1)

                for t in range(TILES):
                    act.wait_ge(kq_ps, t + 1)
                    act.activation(KT[:, :, t * P:(t + 1) * P], ps[:, turn_banks(t), :].rearrange("p (h j) -> p h j", h=H), ACT.Copy).then_inc(kT_ready, 1)
                for n in range(-1, len(units)):
                    for i in range(max(2, len(groups[n])) if n >= 0 else 2):
                        if n >= 0 and i < len(groups[n]):
                            g = group_no[n] + i
                            j0, j1 = groups[n][i]
                            act.wait_ge(wT_ps, g + 1)
                            act.activation(wT[:, g % 2, 0:(j1 - j0) * P], ps[:, 6, 0:(j1 - j0) * P], ACT.Copy).then_inc(wT_ready, 1)
                        if i < 2 and n + 1 < len(units):
                            exp(n + 1, i)
                    if n >= 0 and units[n][1] == H - 1:
                        t = units[n][0]
                        act.wait_ge(av_ps, n + 1)
                        if t:
                            act.wait_ge(ao_ready, t)
                        act.activation(av[:], ps[:, 7, :].rearrange("p (h j) -> p h j", h=H), ACT.Copy).then_inc(av_copied, 1)
                        act.wait_ge(av_copied, t + 1)
                        act.activation(osq[:], av[:], ACT.Square).then_inc(osq_ready, 1)

            @block.vector
            def _(dve):
                v = nc.vector
                ch = Chain(dve, steps, 0)
                dve.wait_ge(loaded, 16 * 4)
                for t in range(TILES):
                    dve.wait_ge(kq_ps, t + 1)
                    v.tensor_scalar(qT[:, :, t * P:(t + 1) * P], ps[:, turn_banks(t) + 1, :].rearrange("p (h j) -> p h j", h=H), DQ ** -0.5, None, ALU.mult).then_inc(qT_ready, 1)

                def maximum(n, c):
                    t, h = units[n]
                    dve.wait_ge(s_ps, 2 * n + c + 1)
                    v.tensor_reduce(nmax[:, c:c + 1], score_columns(c, 0, (t + 1) * P), AX_X, ALU.max, negate=True).then_inc(max_ready, 1)

                def weights(n):
                    wd = (units[n][0] + 1) * P
                    dve.wait_ge(e_ready, 2 * n + 2)
                    ch.link(v.reciprocal(rcp[:], sums[:]))
                    ch.link(v.tensor_tensor(rcp[:], rcp[:], coef[:], ALU.mult))
                    if n >= 2:
                        dve.wait_ge(wT_ps, group_no[n - 1])
                    ch.link(v.tensor_scalar(w[:, n % 2, 0:wd], prob[:, 1, 0:wd], rcp[:, 1:2], None, ALU.mult))
                    v.scalar_tensor_tensor(w[:, n % 2, 0:wd], prob[:, 0, 0:wd], rcp[:, 0:1], w[:, n % 2, 0:wd], ALU.mult, ALU.add).then_inc(w_ready, 1)

                def norm(t):
                    dve.wait_ge(osq_ready, t + 1)
                    ch.link(v.tensor_reduce(ss[:], osq[:], AX_X, ALU.add))
                    rsqrt(nc, ch, rn[:], ss[:], rt[:], 1.0 / DV, EPS, times=1.0 - LAM_INIT)
                    if t >= 2:
                        dve.wait_ge(ao_stored[t % 2], 16 * (t // 2))
                    ch.link(v.tensor_tensor(ao[:, t % 2], av[:], bc(rn[:].rearrange("p (h o) -> p h o", o=1), P, H, DV), ALU.mult))
                    v.tensor_tensor(ao[:, t % 2], ao[:, t % 2], bc(w_sub[:].rearrange("p (o j) -> p o j", o=1), P, H, DV), ALU.mult).then_inc(ao_ready, 1)

                for c in range(2):
                    maximum(0, c)
                for n, (t, h) in enumerate(units):
                    weights(n)
                    if n + 1 < len(units):
                        for c in range(2):
                            maximum(n + 1, c)
                    if h == 0 and t:
                        norm(t - 1)
                norm(last_tile)

            @block.tensor
            def _(pe):
                pe.wait_ge(loaded, 16 * 4)

                for t in range(TILES):
                    if t >= 4:
                        pe.wait_ge(kT_ready, t - 3)
                        pe.wait_ge(qT_ready, t - 3)
                    for i, o in enumerate((HW, 0)):
                        for h in range(H):
                            last = pe.transpose(ps[:, turn_banks(t) + i, h * P:(h + 1) * P], qk[:, t, o + h * P:o + (h + 1) * P], ident[:])
                    last.then_inc(kq_ps, 1)
                pe.wait_ge(kT_ready, TILES)
                pe.wait_ge(qT_ready, TILES)

                def scores(n, c):
                    t, h = units[n]
                    wd = (t + 1) * P
                    if n:
                        pe.wait_ge(e_ready, 2 * n + c - 1)
                    q = qT[DQ * c:DQ * (c + 1), h, t * P:(t + 1) * P]
                    for k0 in range(0, wd, 512):
                        k1 = min(k0 + 512, wd)
                        pe.matmul(score_columns(c, k0, k1), q, KT[DQ * c:DQ * (c + 1), h, k0:k1], start=True, stop=k1 != wd, skip_group_check=True)
                    pe.matmul(score_columns(c, wd - P, wd), ident[:], causal[:], start=False, stop=True, skip_group_check=True).then_inc(s_ps, 1)

                def turn_weights(n, i):
                    j0, j1 = groups[n][i]
                    g = group_no[n] + i
                    if g:
                        pe.wait_ge(wT_ready, g)
                    for j in range(j0, j1):
                        last = pe.transpose(ps[:, 6, (j - j0) * P:(j - j0 + 1) * P], w[:, n % 2, j * P:(j + 1) * P], ident[:])
                    last.then_inc(wT_ps, 1)

                def weigh(n, i):
                    (t, h), (j0, j1) = units[n], groups[n][i]
                    g = group_no[n] + i
                    pe.wait_ge(wT_ready, g + 1)
                    if h == 0 and i == 0 and t:
                        pe.wait_ge(av_copied, t)
                    for j in range(j0, j1):
                        last = pe.matmul(ps[:, 7, h * P:(h + 1) * P], wT[:, g % 2, (j - j0) * P:(j - j0 + 1) * P], vals[:, j, h * DV:(h + 1) * DV],
                                         start=(j == 0), stop=(j == t))
                    if j1 == t + 1:
                        last.then_inc(av_ps, 1)

                for c in range(2):
                    scores(0, c)
                for n in range(len(units)):
                    if n + 1 < len(units):
                        scores(n + 1, 0)
                    pe.wait_ge(w_ready, n + 1)
                    turn_weights(n, 0)
                    if n + 1 < len(units):
                        scores(n + 1, 1)
                    for i in range(len(groups[n])):
                        if i + 1 < len(groups[n]):
                            turn_weights(n, i + 1)
                        weigh(n, i)




def phase_mix(nc, ps, A, keep, w_out, x2):
    with ExitStack() as ctx, own_semaphores(nc) as own:
        def sb(n, s, d=F32):
            return ctx.enter_context(nc.sbuf_tensor("mx_" + n, s, d))

        def sem(n):
            return own("mx_" + n)

        def kept(n):
            return keep.enter_context(nc.semaphore("mx_" + n))

        NL = G + NE
        ident, ones, strict = sb("ident", [P, P]), sb("ones", [P, P]), sb("strict", [P, P])
        w_r, w_norm = sb("w_r", [P, KD, NL]), sb("w_norm", [P, D])
        x, mix = sb("x", [P, 2, D]), sb("mix", [P, 2, D])
        mixT, hnT = sb("mixT", [P, D]), sb("hnT", [P, D])
        hn, squares = sb("hn", [P, 2, D]), sb("squares", [P, D])
        sq, rs = sb("sq", [P, 1]), sb("rs", [P, 2])
        valid, dump, tok = sb("valid", [P, TILES]), sb("dump", [P, TILES, 2]), sb("tok", [P, TILES], I32)
        e_no, e_group = sb("e_no", [P, NE]), sb("e_group", [P, NE])
        lg, le, geq = sb("lg", [P, 8]), sb("le", [P, NE]), sb("geq", [P, NE])
        g8, gi8, e8, ei8 = sb("g8", [P, 8]), sb("gi8", [P, 8], U32), sb("e8", [P, 8]), sb("ei8", [P, 8], U32)
        gi, ei, ngm, gx, gs, gw = sb("gi", [P, 1]), sb("ei", [P, 2]), sb("ngm", [P, 1]), sb("gx", [P, G]), sb("gs", [P, 1]), sb("gw", [P, 1])
        dd, ex, pp = sb("dd", [P, 1]), sb("ex", [P, 1]), sb("pp", [P, 2])
        oh, wt = sb("oh", [P, TILES, 2, NE]), sb("wt", [P, TILES, 2])
        both, pre, rank = sb("both", [P, TILES, NE]), sb("pre", [P, TILES + 1, NE]), sb("rank", [P, TILES, NE])
        cnt, cnt_i, ntile, inc, inc2 = sb("cnt", [P, NE]), sb("cnt_i", [P, NE], I32), sb("ntile", [P, NE]), sb("inc", [P, NE]), sb("inc2", [P, NE])
        pick, slot, slot_i = sb("pick", [P, TILES, 2, NE]), sb("slot", [P, TILES, 2]), sb("slot_i", [P, TILES, 2], I32)
        slot_c = sb("slot_c", [P, TILES, 2], I32)
        tile_no, le_cmp, ownr, own_i = sb("tile_no", [1, SLOT_TILES]), sb("le_cmp", [1, SLOT_TILES, NE]), sb("own", [1, SLOT_TILES]), sb("own_i", [1, SLOT_TILES], I32)

        loaded = sem("loaded")
        in_loaded = [sem("in_loaded0"), sem("in_loaded1")]
        steps, waited = sem("steps"), sem("waited")
        mixT_ps, mixT_ready, x2_ps, x2_ready = sem("mixT_ps"), sem("mixT_ready"), sem("x2_ps"), sem("x2_ready")
        sq_ready, hn_ready, hnT_ps, hnT_ready, lg_ps = sem("sq_ready"), sem("hn_ready"), sem("hnT_ps"), sem("hnT_ready"), sem("lg_ps")
        g_in, g_out, tile_done = sem("g_in"), sem("g_out"), sem("tile_done")
        hn_stored, out_free = kept("hn_stored"), sem("out_free")
        pre_ready, rank_ps, slots_ready, scattered = sem("pre_ready"), sem("rank_ps"), sem("slots_ready"), kept("scattered")
        own_ready, stored = sem("own_ready"), sem("stored")
        norm_steps, lg_read = sem("norm_steps"), sem("lg_read")
        NC = 13

        def row_tile(a, t):
            return a[:, bass.ds(t, 1), :].rearrange("p t n -> p (t n)")

        def ahead(eng):
            yield from tiles(eng, TILES - 2)
            yield TILES - 2, 1, (TILES - 2) // 2
            yield TILES - 1, 0, (TILES - 1) // 2

        def more(t, n):
            return not isinstance(t, int) or t + n < TILES


        with nc.Block() as block:
            @block.sync
            def _(sp):
                consts = [(ident[:], A["ident"]), (ones[:], A["ones"]), (strict[:], A["strict"]),
                          (w_r[:, :, 0:G], A["w_group"].rearrange("(c p) n -> p c n", p=P)),
                          (w_r[:, :, G:NL], A["w_expert"].rearrange("(c p) n -> p c n", p=P)),
                          (w_norm[:], A["w_norm_ffn"].partition_broadcast(P)), (valid[:], A["valid"]), (dump[:], A["dump"]),
                          (tok[:], A["tok"]), (e_no[:], A["e_no"]), (e_group[:], A["e_group"]), (tile_no[:], A["tile_no"]),
                          (A["slot_tok"], A["slot_fill"])]
                assert len(consts) == NC
                def load(t, par):
                    sp.dma_start(x[:, par, :], A["x"][bass.ds(t * P, P), :]).then_inc(in_loaded[par], 16)
                    sp.dma_start(mix[:, par, :], A["mix"][bass.ds(t * P, P), :]).then_inc(in_loaded[par], 16)

                load(0, 0)
                for dst, src in consts:
                    sp.dma_start(dst, src).then_inc(loaded, 16)
                load(1, 1)
                for t, par, k in tiles(sp, TILES - 2):
                    sp.wait_ge(x2_ready, t + 1)
                    load(t + 2, par)
                sp.wait_ge(slots_ready, 2)
                sp.dma_start(A["slots"], slot_c[:].rearrange("p t c -> p (t c)")).then_inc(stored, 16)
                sp.dma_start(A["weights"], wt[:].rearrange("p t c -> p (t c)")).then_inc(stored, 16)
                sp.wait_ge(own_ready, 1)
                sp.dma_start(A["owner"], own_i[:]).then_inc(stored, 16)
                sp.wait_ge(stored, 48)

            @block.gpsimd
            def _(pool):
                pool.sem_inc(out_free, 2)
                for t, par, k in tiles(pool):
                    if not isinstance(t, int):
                        pool.wait_ge(hn_stored, 16 * t)
                        pool.sem_inc(out_free, 1)
                    pool.wait_ge(hn_ready, t + 1)
                    pool.dma_start(A["hn"][bass.ds(t * P, P), :], hn[:, par, :]).then_inc(hn_stored, 16)
                pool.wait_ge(hn_stored, 16 * TILES)
                pool.wait_ge(slots_ready, 2)
                for t in range(TILES):
                    for c in range(2):
                        pool.indirect_dma_start(out=A["slot_tok"], out_offset=bass.IndirectOffsetOnAxis(ap=slot_i[:, t, c:c + 1], axis=0),
                                                in_=tok[:, t:t + 1], in_offset=None).then_inc(scattered, 16)
                pool.wait_ge(scattered, 32 * TILES)

            @block.scalar
            def _(act):
                def copy_mixT(t):
                    act.wait_ge(mixT_ps, t + 1)
                    act.activation(mixT[:].rearrange("p (a b) -> p a b", a=2), ps[:, 0:2, :], ACT.Copy).then_inc(mixT_ready, 1)

                def square(t, par):
                    act.wait_ge(x2_ready, t + 1)
                    act.activation(squares[:], row_tile(x2, t), ACT.Square, accum_out=sq[:]).then_inc(sq_ready, 1)

                copy_mixT(0)
                copy_mixT(1)
                square(0, 0)
                for t, par, k in ahead(act):
                    if more(t, 1):
                        square(t + 1, 1 - par)
                    act.wait_ge(hnT_ps, t + 1)
                    act.activation(hnT[:].rearrange("p (a b) -> p a b", a=2), ps[:, 4:6, :], ACT.Copy).then_inc(hnT_ready, 1)
                    if more(t, 2):
                        copy_mixT(t + 2)
                    act.wait_ge(g_in, 2 * t + 1)
                    act.activation(gx[:], lg[:, 0:G], ACT.Exp, bias=ngm[:], accum_out=gs[:]).then_inc(g_out, 1)
                    act.wait_ge(g_in, 2 * t + 2)
                    act.activation(ex[:], dd[:], ACT.Exp).then_inc(g_out, 1)

            @block.vector
            def _(dve):
                v = nc.vector
                norm_ch, ch = Chain(dve, norm_steps, RSQRT_STEPS), Chain(dve, steps, MIX_STEPS)
                pre_ch = Chain(dve, own("mx_pre_steps"), 0)
                dve.wait_ge(loaded, 16 * NC)
                pre_ch.link(v.memset(lg[:], -BIG))

                def residual_and_norm(t, par, k):
                    norm_ch.begin(t)
                    dve.wait_ge(in_loaded[par], 32 * (k + 1))
                    dve.wait_ge(x2_ps, t + 1)
                    v.tensor_tensor(row_tile(x2, t).rearrange("p (a b) -> p a b", a=2), x[:, par, :].rearrange("p (a b) -> p a b", a=2), ps[:, 2:4, :], ALU.add).then_inc(x2_ready, 1)
                    dve.wait_ge(sq_ready, t + 1)
                    rsqrt(nc, norm_ch, rs[:, 0:1], sq[:], rs[:, 1:2], 1.0 / D, EPS)
                    norm_ch.end()
                    dve.wait_ge(out_free, t + 1)
                    v.scalar_tensor_tensor(hn[:, par, :], row_tile(x2, t), rs[:, 0:1], w_norm[:], ALU.mult, ALU.mult).then_inc(hn_ready, 1)

                residual_and_norm(0, 0, 0)
                for t, par, k in ahead(dve):
                    if more(t, 1):
                        residual_and_norm(t + 1, 1 - par, k + par)
                    ch.begin(t)
                    dve.wait_ge(lg_ps, t + 1)
                    ch.link(v.tensor_copy(lg[:, 0:G], ps[:, 6, 0:G]))
                    dve.sem_inc(waited, 1)
                    ch.link(v.max(g8[:], lg[:]))
                    v.tensor_scalar(ngm[:], g8[:, 0:1], -1.0, None, ALU.mult).then_inc(g_in, 1)
                    ch.link(v.max_index(gi8[:], g8[:], lg[:]))
                    ch.link(v.tensor_copy(gi[:], gi8[:, 0:1]))
                    ch.link(v.tensor_scalar(geq[:], e_group[:], gi[:], None, ALU.is_equal))
                    ch.link(v.tensor_scalar(geq[:], geq[:], -1.0, BIG, ALU.add, ALU.mult))
                    ch.link(v.tensor_tensor(le[:], ps[:, 6, G:NL], geq[:], ALU.add))
                    dve.sem_inc(lg_read, 1)
                    dve.sem_inc(waited, 1)
                    ch.link(v.max(e8[:], le[:]))
                    v.tensor_tensor(dd[:], e8[:, 1:2], e8[:, 0:1], ALU.subtract).then_inc(g_in, 1)
                    ch.link(v.max_index(ei8[:], e8[:], le[:]))
                    ch.link(v.tensor_copy(ei[:], ei8[:, 0:2]))
                    for c in range(2):
                        ch.done(v.tensor_scalar(oh[:, bass.ds(t, 1), c, :].rearrange("p t e -> p (t e)"), e_no[:], ei[:, c:c + 1], None, ALU.is_equal))
                    dve.wait_ge(g_out, 2 * t + 2)
                    ch.done(v.reciprocal(gw[:], gs[:]))
                    ch.link(v.tensor_scalar(pp[:, 0:1], ex[:], 1.0, None, ALU.add))
                    ch.link(v.reciprocal(pp[:, 0:1], pp[:, 0:1]))
                    ch.link(v.tensor_tensor(pp[:, 0:1], pp[:, 0:1], gw[:], ALU.mult))
                    ch.link(v.tensor_tensor(pp[:, 1:2], pp[:, 0:1], ex[:], ALU.mult))
                    ch.link(v.tensor_copy(wt[:, bass.ds(t, 1), :].rearrange("p t c -> p (t c)"), pp[:]))
                    ch.end()
                vb = bc(valid[:].rearrange("p (t c e) -> p t c e", c=1, e=1), P, TILES, 2, NE)
                pc = pre_ch
                pc.link(v.tensor_tensor(oh[:], oh[:], vb, ALU.mult))
                pc.link(v.tensor_tensor(both[:], oh[:, :, 0, :], oh[:, :, 1, :], ALU.add))
                pc.link(v.memset(pre[:, 0, :], 0.0))
                for t in range(TILES):
                    ins = v.tensor_tensor(pre[:, t + 1, :], pre[:, t, :], both[:, t, :], ALU.add)
                    pc.link(ins)
                dve.sem_inc(pre_ready, 1)
                dve.wait_ge(rank_ps, 1)
                pc.link(v.tensor_copy(cnt[:], ps[:, 1, 0:NE]))
                pc.link(v.tensor_scalar(cnt_i[:], cnt[:], float(P - 1), None, ALU.add))
                pc.link(v.tensor_scalar(cnt_i[:], cnt_i[:], 7, None, ALU.logical_shift_right))
                pc.link(v.tensor_copy(ntile[:], cnt_i[:]))
                pc.link(v.tensor_copy(inc[:], ntile[:]))
                a, b = inc, inc2
                for s in (1, 2, 4, 8, 16):
                    pc.done(v.tensor_copy(b[:, 0:s], a[:, 0:s]))
                    pc.link(v.tensor_tensor(b[:, s:NE], a[:, s:NE], a[:, 0:NE - s], ALU.add))
                    a, b = b, a
                pc.link(v.tensor_tensor(b[:], a[:], ntile[:], ALU.subtract))
                pc.link(v.tensor_scalar(b[:], b[:], float(P), None, ALU.mult))
                pc.link(v.tensor_tensor(rank[:], ps[:, 0, 0:TILES * NE].rearrange("p (t e) -> p t e", t=TILES), bc(b[:].rearrange("p (o e) -> p o e", o=1), P, TILES, NE), ALU.add))
                for c in range(2):
                    pc.link(v.tensor_tensor(pick[:, :, c, :], oh[:, :, c, :], rank[:], ALU.mult))
                pc.link(v.tensor_reduce(slot[:], pick[:], AX_X, ALU.add))
                pc.link(v.tensor_tensor(slot[:], slot[:], dump[:], ALU.add))
                pc.link(v.tensor_copy(slot_i[:], slot[:]))
                v.tensor_scalar(slot_c[:], slot[:], float(SLOTS - 1), None, ALU.min).then_inc(slots_ready, 1)
                v.tensor_tensor(wt[:], wt[:], bc(valid[:].rearrange("p (t c) -> p t c", c=1), P, TILES, 2), ALU.mult).then_inc(slots_ready, 1)
                pc.link(v.tensor_tensor(le_cmp[:], bc(a[0:1, :].rearrange("p (o e) -> p o e", o=1), 1, SLOT_TILES, NE),
                                        bc(tile_no[:].rearrange("p (j o) -> p j o", o=1), 1, SLOT_TILES, NE), ALU.is_le))
                pc.link(v.tensor_reduce(ownr[:], le_cmp[:], AX_X, ALU.add))
                v.tensor_scalar(own_i[:], ownr[:], float(NE - 1), None, ALU.min).then_inc(own_ready, 1)

            @block.tensor
            def _(pe):
                pe.wait_ge(loaded, 16 * NC)
                def turn_mix(t, par, k):
                    pe.wait_ge(in_loaded[par], 32 * (k + 1))
                    for c in range(KD):
                        last = pe.transpose(ps[:, c // 4, (c % 4) * P:(c % 4 + 1) * P], mix[:, par, c * P:(c + 1) * P], ident[:])
                    last.then_inc(mixT_ps, 1)

                def project(t):
                    pe.wait_ge(mixT_ready, t + 1)
                    if not isinstance(t, int) or t > 0:
                        pe.wait_ge(x2_ready, t)
                    for n in range(2):
                        for c in range(KD):
                            last = pe.matmul(ps[:, 2 + n, :], mixT[:, c * P:(c + 1) * P], w_out[:, c, n * 512:(n + 1) * 512], start=(c == 0), stop=(c == KD - 1))
                    last.then_inc(x2_ps, 1)

                turn_mix(0, 0, 0)
                project(0)
                turn_mix(1, 1, 0)
                for t, par, k in ahead(pe):
                    if more(t, 1):
                        project(t + 1)
                    pe.wait_ge(hn_ready, t + 1)
                    for c in range(KD):
                        last = pe.transpose(ps[:, 4 + c // 4, (c % 4) * P:(c % 4 + 1) * P], hn[:, par, c * P:(c + 1) * P], ident[:])
                    last.then_inc(hnT_ps, 1)
                    if more(t, 2):
                        turn_mix(t + 2, par, k + 1)
                    pe.wait_ge(hnT_ready, t + 1)
                    if not isinstance(t, int) or t > 0:
                        pe.wait_ge(lg_read, t)
                    for c in range(KD):
                        last = pe.matmul(ps[:, 6, 0:NL], hnT[:, c * P:(c + 1) * P], w_r[:, c, :], start=(c == 0), stop=(c == KD - 1))
                    last.then_inc(lg_ps, 1)
                pe.wait_ge(pre_ready, 1)
                flat = both[:].rearrange("p t e -> p (t e)")
                pe.matmul(ps[:, 0, 0:TILES * NE], strict[:], flat, start=True, stop=False)
                pe.matmul(ps[:, 0, 0:TILES * NE], ones[:], pre[:, 0:TILES, :].rearrange("p t e -> p (t e)"), start=False, stop=True)
                pe.matmul(ps[:, 1, 0:NE], ones[:], pre[:, TILES, :], start=True, stop=True).then_inc(rank_ps, 1)


MIX_STEPS = 18


def phase_experts(nc, ps, A, keep):
    with ExitStack() as ctx, own_semaphores(nc) as own:
        def sb(n, s, d=F32):
            return ctx.enter_context(nc.sbuf_tensor("ex_" + n, s, d))

        def sem(n):
            return own("ex_" + n)

        def kept(n):
            return keep.enter_context(nc.semaphore("ex_" + n))

        NF = FE // P
        ident = sb("ident", [P, P])
        owner = sb("owner", [1, SLOT_TILES], I32)
        rows_of = sb("rows_of", [P, SLOT_TILES + 2], I32)
        idx = [sb(f"idx{i}", [P, 1], I32) for i in range(2)]
        w_gu, w_d = sb("w_gu", [P, 2, KD, 2 * FE]), sb("w_d", [P, 2, NF, D])
        xg, xT = sb("xg", [P, 2, D]), sb("xT", [P, 2, D])
        th, act_g, hh, hhT = sb("th", [P, FE]), sb("act_g", [P, FE]), sb("hh", [P, FE]), sb("hhT", [P, FE])
        y = sb("y", [P, 2, D])
        loaded, waited = sem("loaded"), sem("waited")
        gu_loaded, d_loaded = [sem("gu_loaded0"), sem("gu_loaded1")], [sem("d_loaded0"), sem("d_loaded1")]
        idx_ready, x_loaded, x_used = sem("idx_ready"), [kept("x_loaded0"), kept("x_loaded1")], sem("x_used")
        xT_ready, gu_ps, th_ready, ag_ready, hh_ready = sem("xT_ready"), sem("gu_ps"), sem("th_ready"), sem("ag_ready"), sem("hh_ready")
        hhT_ps, hhT_ready, y_ps, y0_ready, y1_ready = sem("hhT_ps"), sem("hhT_ready"), sem("y_ps"), sem("y0_ready"), sem("y1_ready")
        y_stored, y_free = kept("y_stored"), sem("y_free")
        GU_BANKS = (2, 6)

        def turns(eng):
            with eng.Fori(0, SLOT_TILES // 2 - 1) as u:
                for par in range(2):
                    yield 2 * u + par, par, u
            for j in range(SLOT_TILES - 2, SLOT_TILES):
                yield j, j % 2, j // 2

        def there_is(j, n):
            return not isinstance(j, int) or j + n < SLOT_TILES

        with nc.Block() as block:
            @block.sync
            def _(sp):
                sp.dma_start(ident[:], A["ident"]).then_inc(loaded, 16)
                sp.dma_start(owner[:], A["owner"]).then_inc(loaded, 16)
                with nc.allow_non_contiguous_dma(reason="slot lists are 4 bytes per slot"):
                    sp.dma_start(rows_of[:], A["slot_tok"].rearrange("(j p) o -> p (j o)", p=P)).then_inc(loaded, 16)
                sp.wait_ge(loaded, 48)
                with sp.Fori(0, SLOT_TILES // 2) as u:
                    for par in range(2):
                        j = 2 * u + par
                        e = sp.value_load(owner[0:1, bass.ds(j, 1)], min_val=0, max_val=NE - 1)
                        sp.wait_ge(gu_ps, j + 1)
                        sp.dma_start(w_gu[:, par, :, 0:FE], A["w_gate"][bass.ds(e, 1)].rearrange("e (p c) f -> (e p) c f", c=KD)).then_inc(gu_loaded[par], 16)
                        sp.dma_start(w_gu[:, par, :, FE:2 * FE], A["w_up"][bass.ds(e, 1)].rearrange("e (p c) f -> (e p) c f", c=KD)).then_inc(gu_loaded[par], 16)
                        sp.wait_ge(y_ps, j + 1)
                        sp.dma_start(w_d[:, par, :, :], A["w_down"][bass.ds(e, 1)].rearrange("e (p c) n -> (e p) c n", c=NF)).then_inc(d_loaded[par], 16)

            @block.gpsimd
            def _(pool):
                pool.wait_ge(loaded, 48)
                pool.sem_inc(y_free, 2)

                def gather(j, par):
                    pool.wait_ge(x_used, j + 1)
                    pool.tensor_copy(idx[par][:], rows_of[:, bass.ds(j, 1)]).then_inc(idx_ready, 1)
                    pool.wait_ge(idx_ready, j + 1)
                    pool.sem_inc(waited, 1)
                    pool.indirect_dma_start(out=xg[:, par, :], out_offset=None, in_=A["hn"],
                                            in_offset=bass.IndirectOffsetOnAxis(ap=idx[par][:], axis=0)).then_inc(x_loaded[par], 16)

                def store(j, par):
                    pool.wait_ge(y0_ready, j + 2)
                    pool.wait_ge(y1_ready, j + 2)
                    if not isinstance(j, int) or j > 0:
                        pool.wait_ge(y_stored, 16 * j)
                        pool.sem_inc(y_free, 1)
                    pool.dma_start(A["ys"][bass.ds(j * P, P), :], y[:, par, :]).then_inc(y_stored, 16)

                for j in range(4):
                    gather(j, j % 2)
                for j in range(2):
                    gather(j + 4, j)
                    store(j, j)
                with pool.Fori(1, SLOT_TILES // 2 - 2) as u:
                    for par in range(2):
                        gather(2 * u + par + 4, par)
                        store(2 * u + par, par)
                for j in range(SLOT_TILES - 4, SLOT_TILES):
                    store(j, j % 2)
                pool.wait_ge(y_stored, 16 * SLOT_TILES)
                pool.wait_ge(x_loaded[0], 16 * (SLOT_TILES // 2))
                pool.wait_ge(x_loaded[1], 16 * (SLOT_TILES // 2))

            @block.scalar
            def _(act):
                def copy_x(j, par):
                    act.wait_ge(x_used, j + 3)
                    act.activation(xT[:, par, :].rearrange("p (a b) -> p a b", a=2), ps[:, 0:2, :], ACT.Copy).then_inc(xT_ready, 1)

                def tanh(j, par, first=False):
                    if not first:
                        act.wait_ge(hh_ready, j)
                    act.wait_ge(gu_ps, j + 3)
                    act.activation(th[:], ps[:, GU_BANKS[par], 0:FE], ACT.Tanh, scale=0.5).then_inc(th_ready, 1)

                copy_x(0, 0)
                copy_x(1, 1)
                tanh(0, 0, first=True)
                for j, par, k in turns(act):
                    if there_is(j, 1):
                        tanh(j + 1, 1 - par)
                    if there_is(j, 2):
                        copy_x(j + 2, par)
                    act.wait_ge(y_ps, j + 3)
                    act.wait_ge(y_free, j + 1)
                    act.activation(y[:, par, 0:512], ps[:, 4, :], ACT.Copy).then_inc(y0_ready, 1)

            @block.vector
            def _(dve):
                v = nc.vector

                def gated(j, par):
                    dve.wait_ge(th_ready, j + 1)
                    v.scalar_tensor_tensor(act_g[:], th[:], 1.0, ps[:, GU_BANKS[par], 0:FE], ALU.add, ALU.mult).then_inc(ag_ready, 1)
                    dve.wait_ge(ag_ready, j + 1)
                    v.scalar_tensor_tensor(hh[:], act_g[:], 0.5, ps[:, GU_BANKS[par], FE:2 * FE], ALU.mult, ALU.mult).then_inc(hh_ready, 1)

                gated(0, 0)
                for j, par, k in turns(dve):
                    dve.wait_ge(hhT_ps, j + 1)
                    v.tensor_copy(hhT[:], ps[:, 3, 0:FE]).then_inc(hhT_ready, 1)
                    if there_is(j, 1):
                        gated(j + 1, 1 - par)
                    dve.wait_ge(y_ps, j + 3)
                    dve.wait_ge(y_free, j + 1)
                    v.tensor_copy(y[:, par, 512:1024], ps[:, 5, :]).then_inc(y1_ready, 1)

            @block.tensor
            def _(pe):
                pe.wait_ge(loaded, 48)
                pe.sem_inc(gu_ps, 2)
                pe.sem_inc(y_ps, 2)
                pe.sem_inc(x_used, 2)
                pe.sem_inc(y0_ready, 1)
                pe.sem_inc(y1_ready, 1)

                def turn(j, par, k):
                    pe.wait_ge(x_loaded[par], 16 * (k + 1))
                    xv = xg[:, par, :].rearrange("p (i c) -> p c i", c=KD)
                    for c in range(KD):
                        last = pe.transpose(ps[:, c // 4, (c % 4) * P:(c % 4 + 1) * P], xv[:, c, :], ident[:])
                    last.then_inc(x_used, 1)

                def gate_up(j, par, k):
                    pe.wait_ge(gu_loaded[par], 32 * (k + 1))
                    pe.wait_ge(xT_ready, j + 1)
                    for c in range(KD):
                        last = pe.matmul(ps[:, GU_BANKS[par], :], xT[:, par, c * P:(c + 1) * P], w_gu[:, par, c, :], start=(c == 0), stop=(c == KD - 1))
                    last.then_inc(gu_ps, 1)

                turn(0, 0, 0)
                pe.wait_ge(xT_ready, 1)
                turn(1, 1, 0)
                gate_up(0, 0, 0)
                for j, par, k in turns(pe):
                    if there_is(j, 1):
                        gate_up(j + 1, 1 - par, k + par)
                    pe.wait_ge(hh_ready, j + 1)
                    hv = hh[:].rearrange("p (i c) -> p c i", c=NF)
                    for c in range(NF):
                        last = pe.transpose(ps[:, 3, c * P:(c + 1) * P], hv[:, c, :], ident[:])
                    last.then_inc(hhT_ps, 1)
                    if there_is(j, 2):
                        turn(j + 2, par, k + 1)
                    pe.wait_ge(hhT_ready, j + 1)
                    pe.wait_ge(d_loaded[par], 16 * (k + 1))
                    pe.wait_ge(y0_ready, j + 1)
                    pe.wait_ge(y1_ready, j + 1)
                    for n in range(2):
                        for c in range(NF):
                            last = pe.matmul(ps[:, 4 + n, :], hhT[:, c * P:(c + 1) * P], w_d[:, par, c, n * 512:(n + 1) * 512], start=(c == 0), stop=(c == NF - 1))
                    last.then_inc(y_ps, 1)


def phase_combine(nc, ps, A, keep, x2):
    with ExitStack() as ctx, own_semaphores(nc) as own:
        def sb(n, s, d=F32):
            return ctx.enter_context(nc.sbuf_tensor("co_" + n, s, d))

        def sem(n):
            return own("co_" + n)

        def kept(n):
            return keep.enter_context(nc.semaphore("co_" + n))

        w_fin = sb("w_fin", [P, D])
        slots, wt = sb("slots", [P, TILES, 2], I32), sb("wt", [P, TILES, 2])
        NB = 4
        BATCH = 3
        ya, yb = sb("ya", [P, NB, D]), sb("yb", [P, NB, D])
        squares, sq, rs = sb("squares", [P, D]), sb("sq", [P, TILES]), sb("rs", [P, 2, BATCH])
        loaded, steps = sem("loaded"), sem("steps")
        y_loaded = [kept(f"y_loaded{i}") for i in range(NB)]
        sum_ready, sq_ready, out_ready = sem("sum_ready"), sem("sq_ready"), sem("out_ready")
        out_stored = sem("out_stored")

        with nc.Block() as block:
            @block.sync
            def _(sp):
                sp.dma_start(w_fin[:], A["w_final"].partition_broadcast(P)).then_inc(loaded, 16)
                sp.dma_start(slots[:].rearrange("p t c -> p (t c)"), A["slots"]).then_inc(loaded, 16)
                sp.dma_start(wt[:].rearrange("p t c -> p (t c)"), A["weights"]).then_inc(loaded, 16)
                for t in range(TILES):
                    sp.wait_ge(out_ready, t + 1)
                    sp.dma_start(A["y"][t * P:(t + 1) * P, :], x2[:, t, :]).then_inc(out_stored, 16)
                sp.wait_ge(out_stored, 16 * TILES)

            @block.gpsimd
            def _(pool):
                pool.wait_ge(loaded, 48)
                for t in range(TILES):
                    if t >= NB:
                        pool.wait_ge(sum_ready, t - NB + 1)
                    for c, dst in ((0, ya), (1, yb)):
                        pool.indirect_dma_start(out=dst[:, t % NB, :], out_offset=None, in_=A["ys"],
                                                in_offset=bass.IndirectOffsetOnAxis(ap=slots[:, t, c:c + 1], axis=0)).then_inc(y_loaded[t % NB], 16)

            @block.scalar
            def _(act):
                for t in range(TILES):
                    act.wait_ge(sum_ready, t + 1)
                    if t:
                        act.wait_ge(sq_ready, t)
                    act.activation(squares[:], x2[:, t, :], ACT.Square, accum_out=sq[:, t:t + 1]).then_inc(sq_ready, 1)

            @block.vector
            def _(dve):
                v = nc.vector
                ch = Chain(dve, steps, 0)
                dve.wait_ge(loaded, 48)

                def add_experts(t):
                    p = t % NB
                    dve.wait_ge(y_loaded[p], 32 * (t // NB + 1))
                    ch.link(v.scalar_tensor_tensor(x2[:, t, :], ya[:, p, :], wt[:, t, 0:1], x2[:, t, :], ALU.mult, ALU.add))
                    v.scalar_tensor_tensor(x2[:, t, :], yb[:, p, :], wt[:, t, 1:2], x2[:, t, :], ALU.mult, ALU.add).then_inc(sum_ready, 1)

                for t in range(BATCH):
                    add_experts(t)
                for t0 in range(0, TILES, BATCH):
                    for t in range(t0 + BATCH, min(t0 + 2 * BATCH, TILES)):
                        add_experts(t)
                    dve.wait_ge(sq_ready, t0 + BATCH)
                    rsqrt(nc, ch, rs[:, 0, :], sq[:, t0:t0 + BATCH], rs[:, 1, :], 1.0 / D, EPS)
                    for i in range(BATCH):
                        v.scalar_tensor_tensor(x2[:, t0 + i, :], x2[:, t0 + i, :], rs[:, 0, i:i + 1], w_fin[:], ALU.mult, ALU.mult).then_inc(out_ready, 1)
                    dve.wait_ge(out_ready, t0 + BATCH)


SCRATCH = {"proj": (RPAD + CONV_W - 1, PROJ_W), "mix": (RPAD, 2 * H * DV), "gates_s": (2, BS, H),
           "rows_s": (3, BS, H * DK), "q_s": (BS, H * DV), "coef": (P, 2), "o_s": (BS * H, DV),
           "hn": (RPAD, D), "ys": (SLOTS, D), "weights": (P, 2 * TILES)}
INT_SCRATCH = {"slot_tok": (SLOTS + 2 * P, 1), "slots": (P, 2 * TILES), "owner": (1, SLOT_TILES)}
OUTS = {"y": (RPAD, D), "p_conv": (CONV_W - 1, CONV_CH), "p_gdn": (H, DK, DV), "p_k": (LP, H * DV), "p_v": (LP, H * DV),
        "s_conv": (BS, CONV_W - 1, CONV_CH), "s_gdn": (BS * H, DK, DV), "s_k": (BS, H * DV), "s_v": (BS, H * DV)}


def program(nc, A):
    with ExitStack() as ctx:
        ps = ctx.enter_context(nc.psum_tensor("ps", [P, 8, 512], F32))
        phase_project(nc, ps, A, ctx)
        phase_recurrence_and_decode(nc, ps, A, ctx)
        w_out = ctx.enter_context(nc.sbuf_tensor("w_out", [P, KD, D], F32))
        with ExitStack() as mixer:
            qk = mixer.enter_context(nc.sbuf_tensor("qk", [P, TILES, 2 * H * DV], F32))
            vals = mixer.enter_context(nc.sbuf_tensor("vals", [P, TILES, H * DV], F32))
            phase_sample_gdn(nc, ps, A, ctx, qk, vals)
            phase_attention(nc, ps, A, ctx, qk, vals, w_out)
        x2 = ctx.enter_context(nc.sbuf_tensor("x2", [P, TILES, D], F32))
        phase_mix(nc, ps, A, ctx, w_out, x2)
        phase_experts(nc, ps, A, ctx)
        phase_combine(nc, ps, A, ctx, x2)


def constants():
    r = np.arange(P)
    f = np.float32
    c = {"ident": np.eye(P, dtype=f), "ones": np.ones((P, P), f), "upper": (r[:, None] <= r[None, :]).astype(f)}
    levels = np.zeros((P, 7, P), f)
    for l in range(7):
        s = 1 << l
        b = r // s
        levels[:, l, :] = (b[:, None] // 2 == b[None, :] // 2) & (b[:, None] % 2 == 1) & (b[None, :] % 2 == 0)
    c["levels"] = levels
    c["rowmask"] = (r[:, None] + P * np.arange(TILES)[None, :] < LP).astype(f)
    row = r[:, None] + P * np.arange(TILES)[None, :]
    c["valid"] = (row < ROWS).astype(f)
    c["dump"] = np.where(row < ROWS, 0, SLOTS + r[:, None])[:, :, None] + np.where(row < ROWS, 0, P)[:, :, None] * np.arange(2)
    c["dump"] = c["dump"].astype(f)
    c["tok"] = row.astype(np.int32)
    c["e_no"] = np.ascontiguousarray(np.broadcast_to(np.arange(NE, dtype=f), (P, NE)))
    c["e_group"] = np.ascontiguousarray(np.broadcast_to((np.arange(NE) // EPG).astype(f), (P, NE)))
    c["tile_no"] = np.arange(SLOT_TILES, dtype=f)[None, :]
    c["slot_fill"] = np.full((SLOTS + 2 * P, 1), RPAD - 1, np.int32)
    c["first"] = np.where(r == 0, f(0), f(-BIG))[:, None]
    c["lane"] = np.ascontiguousarray(np.broadcast_to((r % (P // CHUNK)).astype(np.int32)[:, None], (P, BS * CHUNKS)))
    c["strict"] = (r[:, None] < r[None, :]).astype(f)
    c["causal"] = np.where(r[:, None] >= r[None, :], f(0), f(-BIG))
    inv_freq = f(ROPE_THETA) ** (-np.arange(HALF, dtype=f) * f(2) / f(4 * HALF // 2))
    pos = np.where(np.arange(RPAD) < LP, np.arange(RPAD), PAST).astype(f)
    ang = (pos[:, None] * inv_freq[None, :]).reshape(TILES, P, HALF).transpose(1, 0, 2)
    c["cos"], c["sin"] = np.ascontiguousarray(np.cos(ang)), np.ascontiguousarray(np.sin(ang))
    c["cos_s"], c["sin_s"] = (np.ascontiguousarray(np.broadcast_to(c[n][LP % P, TILES - 1], (BS, HALF))) for n in ("cos", "sin"))
    return c


def kernel(**inputs):
    import numpy as _np
    import concourse.bacc as _bacc
    from concourse import mybir as _mybir
    from concourse.bass_utils import run_bass_kernel_spmd as _run

    nc = _bacc.Bacc("TRN2", target_bir_lowering=False, num_devices=1)
    i = {n: _np.ascontiguousarray(a) for n, a in inputs.items()}
    arrays = {
        "x": _np.concatenate([i["meta_tokens"], i["x_prompt"][0], i["x_sample"][:, 0],
                              _np.zeros((RPAD + P - ROWS, D), i["x_prompt"].dtype)], axis=0),
        "w_in": i["w_in"][0], "w_norm_mix": i["w_norm_mix"][0], "w_conv": i["w_conv"][0],
        "w_gnorm": i["w_gnorm"][0], "a_log": i["a_log"][0], "dt_bias": i["dt_bias"][0],
        "state_conv": i["state_conv"][0], "state_gdn": i["state_gdn"][0].reshape(BS * H, DK, DV), "w_subln": i["w_subln"][0],
        "cache_k": i["cache_k"][0].reshape(-1, PAGE, H * 2 * DQ), "cache_v": i["cache_v"][0].reshape(-1, PAGE, H * DV),
        "page_table": i["page_table"].reshape(BS * CHUNKS, CHUNK).T, "w_out": i["w_out"][0], "w_norm_ffn": i["w_norm_ffn"][0],
        "w_final": i["w_final"], **{n: i[n][0] for n in ("w_group", "w_expert", "w_gate", "w_up", "w_down")},
        **{n: i[n][0] for n in ("lambda_q1", "lambda_k1", "lambda_q2", "lambda_k2")},
    }
    arrays["page_table"] = _np.ascontiguousarray(arrays["page_table"])
    arrays.update(constants())
    A = {}
    for n, a in arrays.items():
        A[n] = nc.dram_tensor("in_" + n, a.shape, _mybir.dt.from_np(a.dtype), kind="ExternalInput").ap()
    for n, shape in SCRATCH.items():
        A[n] = nc.dram_tensor("scr_" + n, shape, F32, kind="Internal").ap()
    for n, shape in INT_SCRATCH.items():
        A[n] = nc.dram_tensor("scr_" + n, shape, I32, kind="Internal").ap()
    for n, shape in OUTS.items():
        A[n] = nc.dram_tensor("out_" + n, shape, F32, kind="ExternalOutput").ap()
    program(nc, A)
    r = _run(nc, [{"in_" + n: a for n, a in arrays.items()}], core_ids=[0]).results[0]
    o = {n: r["out_" + n] for n in OUTS}
    return (o["y"][N_META:LP].reshape(1, SEQ, D), o["y"][LP:ROWS].reshape(BS, 1, D),
            o["p_conv"].reshape(1, 1, CONV_W - 1, CONV_CH), o["p_gdn"].reshape(1, 1, H, DK, DV),
            o["p_k"].reshape(1, 1, LP, H, 2 * DQ), o["p_v"].reshape(1, 1, LP, H, DV),
            o["s_conv"].reshape(1, BS, CONV_W - 1, CONV_CH), o["s_gdn"].reshape(1, BS, H, DK, DV),
            o["s_k"].reshape(1, BS, 1, H, 2 * DQ), o["s_v"].reshape(1, BS, 1, H, DV))
```
